# Optimizing a Trainium2 kernel written in Bass

```python
import math
import jax, jax.numpy as jnp
from jax import lax
import numpy as np
import jax
import jax.numpy as jnp

D_MODEL = 1024
BATCH = 1
SEQ = 512
DEPTH = 1

N_META = 16
BLOCK = 128
META_PAD = BLOCK - N_META
RET_HEADS = 4
RET_DK = D_MODEL // 8
RET_DV = D_MODEL // 4
DIFF_HEADS = 8
DIFF_HD = D_MODEL // 16
DIFF_VD = 2 * DIFF_HD
CONV_WIDTH = D_MODEL
CONV_K = 3
N_BRANCH = 3
BRANCH_W = D_MODEL
D_FF = 4 * D_MODEL
EPS = 1e-6
NEG_INF = -1e30
IN_WIDTHS = (RET_HEADS * RET_DK, RET_HEADS * RET_DK, RET_HEADS * RET_DV, RET_HEADS * RET_DV,
             2 * DIFF_HEADS * DIFF_HD, 2 * DIFF_HEADS * DIFF_HD, DIFF_HEADS * DIFF_VD,
             CONV_WIDTH, CONV_WIDTH, CONV_WIDTH, N_BRANCH * D_MODEL)
D_IN = sum(IN_WIDTHS)


def rms_norm(x, w):
    xf = x.astype(jnp.float32)
    y = xf * lax.rsqrt(jnp.mean(xf * xf, axis=-1, keepdims=True) + EPS)
    return (y * w.astype(jnp.float32)).astype(x.dtype)

def head_layer_norm(y):
    yf = y.astype(jnp.float32)
    mu = jnp.mean(yf, axis=-1, keepdims=True)
    var = jnp.mean(jnp.square(yf - mu), axis=-1, keepdims=True)
    return ((yf - mu) * lax.rsqrt(var + EPS)).astype(y.dtype)

def pad_front(t, n):
    return jnp.pad(t, [(0, 0), (n, 0)] + [(0, 0)] * (t.ndim - 2))

def column_bounds():
    bounds, start = [], 0
    for w in IN_WIDTHS:
        bounds.append((start, start + w))
        start += w
    return bounds

def retention(q, k, v):
    b = q.shape[0]
    dt = q.dtype
    k = k * (RET_DK ** -0.5)
    q, k, v = (pad_front(t, META_PAD) for t in (q, k, v))
    nc = q.shape[1] // BLOCK

    def chunks(t):
        return t.reshape(b, nc, BLOCK, RET_HEADS, t.shape[-1]).transpose(1, 0, 3, 2, 4)

    log_g = jnp.log1p(-jnp.exp2(-5.0 - jnp.arange(RET_HEADS, dtype=jnp.float32)))
    i = jnp.arange(BLOCK, dtype=jnp.float32)
    dist = i[:, None] - i[None, :]
    intra = jnp.where(dist >= 0, jnp.exp(log_g[:, None, None] * jnp.maximum(dist, 0.0)), 0.0).astype(dt)
    q_decay = jnp.exp(log_g[:, None] * (i + 1.0)).astype(dt)
    k_decay = jnp.exp(log_g[:, None] * (BLOCK - 1.0 - i)).astype(dt)
    s_decay = jnp.exp(log_g * BLOCK).astype(dt)

    def step(state, qkv):
        qc, kc, vc = qkv
        scores = jnp.einsum('bhid,bhjd->bhij', qc, kc) * intra
        out = (jnp.einsum('bhij,bhjv->bhiv', scores, vc)
               + jnp.einsum('bhid,bhdv->bhiv', qc * q_decay[:, :, None], state))
        state = state * s_decay[:, None, None] + jnp.einsum('bhjd,bhjv->bhdv', kc * k_decay[:, :, None], vc)
        return state, out

    s0 = jnp.zeros((b, RET_HEADS, RET_DK, RET_DV), dt)
    _, out = lax.scan(step, s0, (chunks(q), chunks(k), chunks(v)))
    out = out.transpose(1, 0, 3, 2, 4).reshape(b, nc * BLOCK, RET_HEADS, RET_DV)
    return out[:, META_PAD:]

def diff_attention(q, k, v, lam, subln_w, lam_init):
    b = q.shape[0]
    q, k, v = (pad_front(t, META_PAD) for t in (q, k, v))
    p = q.shape[1]
    nb = p // BLOCK
    kt = k.transpose(0, 2, 3, 1, 4)
    vt = v.transpose(0, 2, 1, 3)
    qb = q.reshape(b, nb, BLOCK, DIFF_HEADS, 2, DIFF_HD).transpose(1, 0, 3, 4, 2, 5)
    slopes = jnp.exp2(-8.0 / DIFF_HEADS * (jnp.arange(DIFF_HEADS, dtype=jnp.float32) + 1.0))
    kpos = jnp.arange(p)
    scale = DIFF_HD ** -0.5

    def block(args):
        qblk, bi = args
        qpos = bi * BLOCK + jnp.arange(BLOCK)
        dist = (qpos[:, None] - kpos[None, :]).astype(jnp.float32)
        valid = (dist >= 0) & (kpos[None, :] >= META_PAD)
        logits = (jnp.einsum('bhmqd,bhmkd->bhmqk', qblk, kt, preferred_element_type=jnp.float32) * scale
                  - slopes[:, None, None, None] * dist)
        probs = jax.nn.softmax(jnp.where(valid, logits, NEG_INF), axis=-1)
        attn = probs[:, :, 0] - lam * probs[:, :, 1]
        return jnp.einsum('bhqk,bhkv->bhqv', attn.astype(vt.dtype), vt)

    out = lax.map(block, (qb, jnp.arange(nb)))
    out = out.transpose(1, 0, 3, 2, 4).reshape(b, p, DIFF_HEADS, DIFF_VD)[:, META_PAD:]
    return rms_norm(out, subln_w) * (1.0 - lam_init)

def short_conv(u, w):
    return lax.conv_general_dilated(
        u, w[:, None, :].astype(u.dtype), window_strides=(1,), padding=[(CONV_K - 1, 0)],
        dimension_numbers=('NWC', 'WIO', 'NWC'), feature_group_count=u.shape[-1])

def hybrid_layer(x, layer, norm1_w, w_in, conv_w, lam_vecs, subln_w, w_branch, w_out, norm2_w, w_up, w_down):
    b, l, _ = x.shape
    h = rms_norm(x, norm1_w)
    (rq, rk, rv, rg, dq, dk, dv, cb, cc, cx, gates) = [h @ w_in[:, s:e] for s, e in column_bounds()]

    ret = retention(rq.reshape(b, l, RET_HEADS, RET_DK), rk.reshape(b, l, RET_HEADS, RET_DK),
                    rv.reshape(b, l, RET_HEADS, RET_DV))
    ret = head_layer_norm(ret).reshape(b, l, BRANCH_W) * jax.nn.silu(rg)

    lam_init = 0.8 - 0.6 * math.exp(-0.3 * layer)
    lv = lam_vecs.astype(jnp.float32)
    lam = jnp.exp(jnp.sum(lv[0] * lv[1])) - jnp.exp(jnp.sum(lv[2] * lv[3])) + lam_init
    diff = diff_attention(dq.reshape(b, l, DIFF_HEADS, 2, DIFF_HD), dk.reshape(b, l, DIFF_HEADS, 2, DIFF_HD),
                          dv.reshape(b, l, DIFF_HEADS, DIFF_VD), lam, subln_w, lam_init).reshape(b, l, BRANCH_W)

    conv = cb * short_conv(cc * cx, conv_w)

    g = jax.nn.sigmoid(gates.astype(jnp.float32)).astype(x.dtype).reshape(b, l, N_BRANCH, D_MODEL)
    merged = (g[:, :, 0] * (ret @ w_branch[0]) + g[:, :, 1] * (diff @ w_branch[1])
              + g[:, :, 2] * (conv @ w_branch[2]))
    x = x + merged @ w_out

    u = jnp.square(jax.nn.relu(rms_norm(x, norm2_w) @ w_up))
    return x + u @ w_down

def first_inputs(seed: int = 0) -> dict:
    key = jax.random.key(seed)
    ks = jax.random.split(key, 13)
    nrm = jax.random.normal
    f32 = jnp.float32
    return {
        "x": nrm(ks[0], (BATCH, SEQ, D_MODEL), f32),
        "meta_tokens": nrm(ks[1], (N_META, D_MODEL), f32),
        "norm1_w": 1.0 + 0.02 * nrm(ks[2], (DEPTH, D_MODEL), f32),
        "w_in": nrm(ks[3], (DEPTH, D_MODEL, D_IN), f32) * D_MODEL ** -0.5,
        "conv_w": nrm(ks[4], (DEPTH, CONV_K, CONV_WIDTH), f32) * CONV_K ** -0.5,
        "diff_lambda": 0.1 * nrm(ks[5], (DEPTH, 4, DIFF_HD), f32),
        "diff_subln_w": 1.0 + 0.02 * nrm(ks[6], (DEPTH, DIFF_VD), f32),
        "w_branch": nrm(ks[7], (DEPTH, N_BRANCH, BRANCH_W, D_MODEL), f32) * BRANCH_W ** -0.5,
        "w_out": nrm(ks[8], (DEPTH, D_MODEL, D_MODEL), f32) * D_MODEL ** -0.5,
        "norm2_w": 1.0 + 0.02 * nrm(ks[9], (DEPTH, D_MODEL), f32),
        "w_up": nrm(ks[10], (DEPTH, D_MODEL, D_FF), f32) * D_MODEL ** -0.5,
        "w_down": nrm(ks[11], (DEPTH, D_FF, D_MODEL), f32) * D_FF ** -0.5,
        "final_norm_w": 1.0 + 0.02 * nrm(ks[12], (D_MODEL,), f32),
    }

def first_block(x, meta_tokens, norm1_w, w_in, conv_w, diff_lambda, diff_subln_w, w_branch, w_out,
              norm2_w, w_up, w_down, final_norm_w):
    b = x.shape[0]
    meta = jnp.broadcast_to(meta_tokens.astype(x.dtype)[None], (b, N_META, D_MODEL))
    h = jnp.concatenate([meta, x], axis=1)
    for layer in range(DEPTH):
        h = hybrid_layer(h, layer, norm1_w[layer], w_in[layer], conv_w[layer], diff_lambda[layer],
                         diff_subln_w[layer], w_branch[layer], w_out[layer], norm2_w[layer],
                         w_up[layer], w_down[layer])
    return rms_norm(h[:, N_META:], final_norm_w)


GRID_W = 64
CTX_LEN = 256
N_HEADS_NA = 8
HEAD_DIM_NA = 64
WIN_H = 8
WIN_W = 16
NA_QCOLS = 16
NA_KCOLS = 32
N_HEADS_MLA = 8
MLA_Q_RANK = 768
MLA_KV_RANK = 256
MLA_NOPE_DIM = 64
MLA_ROPE_DIM = 32
MLA_V_DIM = 64
D_FF_2 = 2816
ROPE_BASE = 10000.0
RMS_EPS = 1e-6
ATTN_QBLOCK = 128
N_MOD = 9
HALF_STEP = 0.5
NA_WIDTH = N_HEADS_NA * HEAD_DIM_NA
MLA_QK_DIM = MLA_NOPE_DIM + MLA_ROPE_DIM
IN_SPLITS = (NA_WIDTH, 2 * NA_WIDTH, 3 * NA_WIDTH, 3 * NA_WIDTH + MLA_Q_RANK,
             3 * NA_WIDTH + MLA_Q_RANK + MLA_KV_RANK,
             3 * NA_WIDTH + MLA_Q_RANK + MLA_KV_RANK + MLA_ROPE_DIM)
IN_COLS = IN_SPLITS[-1] + 2 * D_MODEL


def _rmsnorm(x, g):
    x32 = x.astype(jnp.float32)
    y = x32 * lax.rsqrt(jnp.mean(x32 * x32, axis=-1, keepdims=True) + RMS_EPS)
    return y.astype(x.dtype) * g

def _modnorm(x, g_pre, shift, scale):
    return _rmsnorm(x, g_pre) * (1 + scale) + shift

def _residual(x, y, g_post, gate, weight):
    return x + weight * gate * _rmsnorm(y, g_post)

def _swiglu(h, w1, w3, w2):
    return (jax.nn.silu(h @ w1) * (h @ w3)) @ w2

def _axial_angles(n_tokens):
    half = MLA_ROPE_DIM // 4
    freqs = ROPE_BASE ** (-jnp.arange(half, dtype=jnp.float32) / half)
    t = jnp.arange(n_tokens)
    rows = (t // GRID_W).astype(jnp.float32)
    cols = (t % GRID_W).astype(jnp.float32)
    return rows[:, None] * freqs, cols[:, None] * freqs

def _rope_axis(x, ang):
    half = x.shape[-1] // 2
    cos = jnp.cos(ang)[None, :, None, :].astype(x.dtype)
    sin = jnp.sin(ang)[None, :, None, :].astype(x.dtype)
    x1, x2 = x[..., :half], x[..., half:]
    return jnp.concatenate([x1 * cos - x2 * sin, x2 * cos + x1 * sin], axis=-1)

def _axial_rope(x, ang_r, ang_c):
    a = MLA_ROPE_DIM // 2
    return jnp.concatenate([_rope_axis(x[..., :a], ang_r), _rope_axis(x[..., a:], ang_c)], axis=-1)

def _project(h, w_in, b_gate, g_q, g_kv, w_uq, w_ukv):
    B, T, _ = h.shape
    qa, ka, va, cq, ckv, kr, gates = jnp.split(h @ w_in, IN_SPLITS, axis=-1)
    heads = lambda t, n: t.reshape(B, T, n, -1)
    q = heads(_rmsnorm(cq, g_q) @ w_uq, N_HEADS_MLA)
    kv = heads(_rmsnorm(ckv, g_kv) @ w_ukv, N_HEADS_MLA)
    g = jax.nn.sigmoid(gates + b_gate)
    return (heads(qa, N_HEADS_NA), heads(ka, N_HEADS_NA), heads(va, N_HEADS_NA),
            q[..., :MLA_NOPE_DIM], q[..., MLA_NOPE_DIM:],
            kv[..., :MLA_NOPE_DIM], kr[:, :, None, :], kv[..., MLA_NOPE_DIM:],
            g[..., :D_MODEL], g[..., D_MODEL:])

def _mla_q(q_nope, q_rope):
    return jnp.concatenate([q_nope, q_rope], axis=-1)

def _mla_k(k_nope, k_rope):
    k_rope = jnp.broadcast_to(k_rope, k_nope.shape[:-1] + (k_rope.shape[-1],))
    return jnp.concatenate([k_nope, k_rope], axis=-1)

def _attend(q, k, v):
    s = jnp.einsum('bqhd,bkhd->bhqk', q * q.shape[-1] ** -0.5, k).astype(jnp.float32)
    p = jax.nn.softmax(s, axis=-1).astype(v.dtype)
    return jnp.einsum('bhqk,bkhd->bqhd', p, v)

def _blocked_attention(q, k, v):
    B, S, H, dq = q.shape
    qb = q.reshape(B, S // ATTN_QBLOCK, ATTN_QBLOCK, H, dq).swapaxes(0, 1)
    out = lax.map(lambda qq: _attend(qq, k, v), qb)
    return out.swapaxes(0, 1).reshape(B, S, H, v.shape[-1])

def _na_column_tables():
    n_blk = GRID_W // NA_QCOLS
    j = np.arange(n_blk)
    k_start = np.clip(j * NA_QCOLS - WIN_W // 2, 0, GRID_W - NA_KCOLS)
    key_col = k_start[:, None] + np.arange(NA_KCOLS)
    q_col = j[:, None] * NA_QCOLS + np.arange(NA_QCOLS)
    w_start = np.clip(q_col - WIN_W // 2, 0, GRID_W - WIN_W)
    kc = key_col[:, None, :]
    valid = (kc >= w_start[..., None]) & (kc < w_start[..., None] + WIN_W)
    off = np.clip(kc - q_col[..., None], -(WIN_W - 1), WIN_W - 1) + (WIN_W - 1)
    return jnp.asarray(key_col, jnp.int32), jnp.asarray(valid), jnp.asarray(off, jnp.int32)

def _neighbourhood_attention(q, k, v, k_ctx, v_ctx, rpb, n_rows):
    B, S, H, d = q.shape
    kh = min(WIN_H, n_rows)
    n_blk = GRID_W // NA_QCOLS
    n_loc = kh * NA_KCOLS
    key_col, valid, col_off = _na_column_tables()
    grid = lambda t: t.reshape(B, n_rows, GRID_W, H, t.shape[-1])
    qg, kg, vg = grid(q * d ** -0.5), grid(k), grid(v)
    neg = jnp.finfo(jnp.float32).min

    def row(r):
        rs = jnp.clip(r - kh // 2, 0, n_rows - kh)
        q_r = lax.dynamic_index_in_dim(qg, r, axis=1, keepdims=False).reshape(B, n_blk, NA_QCOLS, H, d)
        k_b = jnp.moveaxis(lax.dynamic_slice_in_dim(kg, rs, kh, axis=1)[:, :, key_col], 2, 1)
        v_b = jnp.moveaxis(lax.dynamic_slice_in_dim(vg, rs, kh, axis=1)[:, :, key_col], 2, 1)
        row_off = rs + jnp.arange(kh) - r + (WIN_H - 1)
        bias = rpb[:, row_off[None, None, :, None], col_off[:, :, None, :]]
        s_loc = jnp.einsum('bjqhd,bjakhd->bhjqak', q_r, k_b).astype(jnp.float32) + bias.astype(jnp.float32)
        s_loc = jnp.where(valid[:, :, None, :], s_loc, neg).reshape(B, H, n_blk, NA_QCOLS, n_loc)
        s_ctx = jnp.einsum('bjqhd,bkhd->bhjqk', q_r, k_ctx).astype(jnp.float32)
        p = jax.nn.softmax(jnp.concatenate([s_loc, s_ctx], axis=-1), axis=-1).astype(v.dtype)
        p_loc = p[..., :n_loc].reshape(B, H, n_blk, NA_QCOLS, kh, NA_KCOLS)
        o = (jnp.einsum('bhjqak,bjakhd->bjqhd', p_loc, v_b)
             + jnp.einsum('bhjqk,bkhd->bjqhd', p[..., n_loc:], v_ctx))
        return o.reshape(B, GRID_W, H, v.shape[-1])

    out = lax.map(row, jnp.arange(n_rows))
    return jnp.moveaxis(out, 0, 1).reshape(B, S, H, v.shape[-1])

def _merge(o_na, o_mla, g_na, g_mla, w_o_na, w_o_mla, w_out):
    B, T = o_na.shape[:2]
    y = g_na * (o_na.reshape(B, T, -1) @ w_o_na) + g_mla * (o_mla.reshape(B, T, -1) @ w_o_mla)
    return y @ w_out

def second_inputs(seed: int = 0) -> dict:
    key = jax.random.key(seed)
    ks = jax.random.split(key, 24)
    nrm = lambda k, shape, s: jax.random.normal(k, shape, jnp.float32) * s
    D = D_MODEL
    return {
        'x': nrm(ks[0], (BATCH, SEQ, D), 1.0),
        'c': nrm(ks[1], (BATCH, D), 1.0),
        'ctx': nrm(ks[2], (BATCH, CTX_LEN, D), 1.0),
        'c_ctx': nrm(ks[3], (D,), 1.0),
        'w_ada': nrm(ks[4], (DEPTH, D, N_MOD * D), 0.5 * D ** -0.5),
        'b_ada': nrm(ks[5], (DEPTH, N_MOD * D), 0.02),
        'norm_g': 1.0 + nrm(ks[6], (DEPTH, 6, D), 0.02),
        'ffn1_w1': nrm(ks[7], (DEPTH, D, D_FF_2), D ** -0.5),
        'ffn1_w3': nrm(ks[8], (DEPTH, D, D_FF_2), D ** -0.5),
        'ffn1_w2': nrm(ks[9], (DEPTH, D_FF_2, D), D_FF_2 ** -0.5),
        'w_in': nrm(ks[10], (DEPTH, D, IN_COLS), D ** -0.5),
        'b_gate': nrm(ks[11], (DEPTH, 2 * D), 0.1),
        'g_q_lora': 1.0 + nrm(ks[12], (DEPTH, MLA_Q_RANK), 0.02),
        'g_kv_lora': 1.0 + nrm(ks[13], (DEPTH, MLA_KV_RANK), 0.02),
        'w_uq': nrm(ks[14], (DEPTH, MLA_Q_RANK, N_HEADS_MLA * MLA_QK_DIM), MLA_Q_RANK ** -0.5),
        'w_ukv': nrm(ks[15], (DEPTH, MLA_KV_RANK, N_HEADS_MLA * (MLA_NOPE_DIM + MLA_V_DIM)), MLA_KV_RANK ** -0.5),
        'rpb': nrm(ks[16], (DEPTH, N_HEADS_NA, 2 * WIN_H - 1, 2 * WIN_W - 1), 0.1),
        'w_o_na': nrm(ks[17], (DEPTH, NA_WIDTH, D), NA_WIDTH ** -0.5),
        'w_o_mla': nrm(ks[18], (DEPTH, N_HEADS_MLA * MLA_V_DIM, D), (N_HEADS_MLA * MLA_V_DIM) ** -0.5),
        'w_out': nrm(ks[19], (DEPTH, D, D), D ** -0.5),
        'ffn2_w1': nrm(ks[20], (DEPTH, D, D_FF_2), D ** -0.5),
        'ffn2_w3': nrm(ks[21], (DEPTH, D, D_FF_2), D ** -0.5),
        'ffn2_w2': nrm(ks[22], (DEPTH, D_FF_2, D), D_FF_2 ** -0.5),
    }

def second_block(x, c, ctx, c_ctx, w_ada, b_ada, norm_g, ffn1_w1, ffn1_w3, ffn1_w2, w_in, b_gate,
              g_q_lora, g_kv_lora, w_uq, w_ukv, rpb, w_o_na, w_o_mla, w_out, ffn2_w1, ffn2_w3, ffn2_w2):
    n_lat = x.shape[1]
    n_rows = n_lat // GRID_W
    ang_r, ang_c = _axial_angles(n_lat)
    h_ctx = ctx
    for l in range(DEPTH):
        last = l == DEPTH - 1
        m = jnp.split((jax.nn.silu(c) @ w_ada[l] + b_ada[l])[:, None, :], N_MOD, axis=-1)
        mc = jnp.split(jax.nn.silu(c_ctx) @ w_ada[l] + b_ada[l], N_MOD, axis=-1)
        g = norm_g[l]
        x = _residual(x, _swiglu(_modnorm(x, g[0], m[0], m[1]), ffn1_w1[l], ffn1_w3[l], ffn1_w2[l]),
                      g[1], m[2], HALF_STEP)
        h_ctx = _residual(h_ctx, _swiglu(_modnorm(h_ctx, g[0], mc[0], mc[1]), ffn1_w1[l], ffn1_w3[l], ffn1_w2[l]),
                          g[1], mc[2], HALF_STEP)
        pw = (w_in[l], b_gate[l], g_q_lora[l], g_kv_lora[l], w_uq[l], w_ukv[l])
        qa, ka, va, qn, qr, kn, kr, vb, ga, gb = _project(_modnorm(x, g[2], m[3], m[4]), *pw)
        cqa, cka, cva, cqn, cqr, ckn, ckr, cvb, cga, cgb = _project(_modnorm(h_ctx, g[2], mc[3], mc[4]), *pw)
        o_na = _neighbourhood_attention(qa, ka, va, cka, cva, rpb[l], n_rows)
        k_ctx_mla = _mla_k(ckn, ckr)
        q_mla = _mla_q(qn, _axial_rope(qr, ang_r, ang_c))
        k_mla = jnp.concatenate([k_ctx_mla, _mla_k(kn, _axial_rope(kr, ang_r, ang_c))], axis=1)
        v_mla = jnp.concatenate([cvb, vb], axis=1)
        o_mla = _blocked_attention(q_mla, k_mla, v_mla)
        y = _merge(o_na, o_mla, ga, gb, w_o_na[l], w_o_mla[l], w_out[l])
        x = _residual(x, y, g[3], m[5], 1.0)
        if not last:
            yc = _merge(_attend(cqa, cka, cva), _attend(_mla_q(cqn, cqr), k_ctx_mla, cvb),
                        cga, cgb, w_o_na[l], w_o_mla[l], w_out[l])
            h_ctx = _residual(h_ctx, yc, g[3], mc[5], 1.0)
            h_ctx = _residual(h_ctx, _swiglu(_modnorm(h_ctx, g[4], mc[6], mc[7]), ffn2_w1[l], ffn2_w3[l], ffn2_w2[l]),
                              g[5], mc[8], HALF_STEP)
        x = _residual(x, _swiglu(_modnorm(x, g[4], m[6], m[7]), ffn2_w1[l], ffn2_w3[l], ffn2_w2[l]),
                      g[5], m[8], HALF_STEP)
    return x


def setup_inputs(seed=0):
    out = dict(first_inputs(seed))
    for name, value in second_inputs(seed + 1).items():
        if name != "x":
            out[name + "_2"] = value
    return out


def reference(
    x, meta_tokens, norm1_w, w_in, conv_w, diff_lambda, diff_subln_w, w_branch, w_out, norm2_w,
    w_up, w_down, final_norm_w, c_2, ctx_2, c_ctx_2, w_ada_2, b_ada_2, norm_g_2, ffn1_w1_2,
    ffn1_w3_2, ffn1_w2_2, w_in_2, b_gate_2, g_q_lora_2, g_kv_lora_2, w_uq_2, w_ukv_2, rpb_2,
    w_o_na_2, w_o_mla_2, w_out_2, ffn2_w1_2, ffn2_w3_2, ffn2_w2_2,
):
    x = first_block(
        x, meta_tokens, norm1_w, w_in, conv_w, diff_lambda, diff_subln_w, w_branch, w_out,
        norm2_w, w_up, w_down, final_norm_w,
    )
    return second_block(
        x, c_2, ctx_2, c_ctx_2, w_ada_2, b_ada_2, norm_g_2, ffn1_w1_2, ffn1_w3_2, ffn1_w2_2,
        w_in_2, b_gate_2, g_q_lora_2, g_kv_lora_2, w_uq_2, w_ukv_2, rpb_2, w_o_na_2, w_o_mla_2,
        w_out_2, ffn2_w1_2, ffn2_w3_2, ffn2_w2_2,
    )


_drawn_inputs = setup_inputs


def setup_inputs(seed=0):
    import zlib

    import numpy as np

    out = dict(_drawn_inputs(seed))
    spreads = {}
    factors = {'diff_subln_w': 7.076,
     'norm2_w': 3.551,
     'final_norm_w': 2.859,
     'norm_g_2': 5.271,
     'b_gate_2': 5.153,
     'g_q_lora_2': 8.0,
     'g_kv_lora_2': 8.0,
     'rpb_2': 8.0}
    for name, (base, spread) in spreads.items():
        noise = np.random.default_rng([zlib.crc32(name.encode()), seed]).standard_normal(out[name].shape)
        drawn = base * np.exp(spread * noise) if base else spread * noise
        out[name] = jnp.asarray(drawn.astype(out[name].dtype))
    for name, factor in factors.items():
        out[name] = (out[name] * factor).astype(out[name].dtype)
    return out
```

```python
import math
from contextlib import ExitStack

import numpy as np
import concourse.bass as bass
from concourse import mybir

F32 = mybir.dt.float32
F32R = mybir.dt.float32r
ALU = mybir.AluOpType
ACT = mybir.ActivationFunctionType
AX = mybir.AxisListType.X

P = 128
D = 1024
KC = D // P
SEQ = 512
META = 16
T1 = META + SEQ
CTX = 256
T2 = CTX + SEQ
NT = SEQ // P
EPS = 1e-6
NEG = -1e30

TILES = [(0, META)] + [(META + P * t, P) for t in range(NT)]

RET_H, RET_DK, RET_DV = 4, P, 2 * P
DIFF_H = 8
W_RQ, W_RK, W_RV, W_RG = 0, 512, 1024, 2048
W_DQ, W_DK, W_DV = 3072, 4096, 5120
W_CB, W_CC, W_CX, W_GATE = 6144, 7168, 8192, 9216
FF1 = 4 * D
LAM_INIT = 0.8 - 0.6 * math.exp(0.0)

GRID_W, GRID_H = 64, 8
NA_H, NA_HD = 8, 64
W_QA, W_KA, W_VA, W_CQ, W_CKV, W_KR, W_G2 = 0, 512, 1024, 1536, 2304, 2560, 2592
QR, KVR = 768, 256
NOPE, ROPE, VD = 64, 32, 64
QK = NOPE + ROPE
FF2 = 2816
FF2_CHUNKS = FF2 // P
NA_START = [8 * min(max(16 * t - 8, 0), 32) for t in range(NT)]
V_STARTS = [0, 64, 128, 192, 256, 320, 384]
NV = len(V_STARTS)

_C = {}


def _layout():
    at = 0
    for name, n in (("ident", P), ("ones", P), ("slope8", DIFF_H), ("onehot8", 16), ("window", 3 * 32),
                    ("rot", QK), ("eps", 1), ("minus_half", 8)):
        _C[name] = (at, n)
        at += n
    return at


CONST_N = _layout()


def shape_constants():
    c = np.zeros((P, CONST_N), np.float32)

    def put(name, v):
        a, n = _C[name]
        c[:, a:a + n] = v

    p = np.arange(P)
    put("ident", np.eye(P))
    put("ones", 1.0)
    x = np.arange(T1)[None, :] - (T1 - P) - p[:, None]
    rel = np.where(x > 0, NEG, x).astype(np.float32)
    put("slope8", 8.0 * 2.0 ** -(np.arange(DIFF_H) + 1.0)[None, :])
    put("onehot8", np.where(p[:, None] // GRID_H == np.arange(16)[None, :], 8.0, 0.0))
    b, a = (p // GRID_H)[:, None], np.arange(32)[None, :]
    kinds = []
    for t in (0, 1, 3):
        ws = np.clip(16 * t + b - 8, 0, GRID_W - 16)
        kc = NA_START[t] // GRID_H + a
        kinds.append(np.where((kc >= ws) & (kc < ws + 16), 0.0, NEG))
    put("window", np.concatenate(kinds, 1))
    rot = np.zeros((P, QK), np.float32)
    for i in range(8):
        for o in (NOPE, NOPE + 16):
            rot[o + 8 + i, o + i] = -1.0
            rot[o + i, o + 8 + i] = 1.0
    put("rot", rot)
    half = 8
    freqs = (np.float32(10000.0) ** (-np.arange(half, dtype=np.float32) / np.float32(half))).astype(np.float32)
    n = np.arange(SEQ)
    rows, cols = (n % GRID_H).astype(np.float32), (n // GRID_H).astype(np.float32)
    ang = np.concatenate([rows[None] * freqs[:, None]] * 2 + [cols[None] * freqs[:, None]] * 2, 0)
    rope = np.stack([np.cos(ang.astype(np.float32)), np.sin(ang.astype(np.float32))], 1)
    put("eps", EPS)
    put("minus_half", -0.5)
    log_g = np.log1p(-np.exp2(-5.0 - np.arange(RET_H)))
    m = np.arange(T1)[None, None, :] - p[:, None, None]
    decay = np.where(m >= 0, np.exp(log_g[None, :, None] * np.maximum(m, 0)) * RET_DK ** -0.5, 0.0)
    return {"const": c, "rel": rel, "rope": rope.astype(np.float32), "decay": decay.astype(np.float32)}


class Count:

    def __init__(self, base, *terms):
        self.base, self.terms = base, terms

    def __add__(self, n):
        return Count(self.base + n, *self.terms)

    @property
    def slot(self):
        return self.base % 2

    def value(self, add=0):
        v = self.base + add
        for reg, step in self.terms:
            v = reg * step + v
        return v

    def turns(self):
        return Count(self.base // 2, *((reg, step // 2) for reg, step in self.terms))


def turn(i, base, step):
    return Count(base + i * step) if isinstance(i, int) else Count(base, (i, step))


def flat(ap, n):
    names = " ".join(f"d{i}" for i in range(len(ap.shape)))
    return ap.rearrange(f"{names} -> ({names})").rearrange("(r n) -> r n", n=n)


def val(count):
    return count.value() if isinstance(count, Count) else count


def alone(eng, passed):
    eng.sem_inc(passed, 1)


U_RET = 0
U_BR = [RET_H * 6, RET_H * 6 + 16 + DIFF_H * 3, RET_H * 6 + 32 + DIFF_H * 3 + KC * 3]
U_DIFF = U_BR[0] + 16
U_CONV = U_BR[1] + 16
U_OUT = U_BR[2] + 16
U_FF = U_OUT + KC
U_FA = U_FF + (FF1 // D) * 16
U_NA = U_FA + 48 + 20
U_LORA = U_NA + 12
U_MLA = U_LORA + 9
U_GATE = U_MLA + 16
U_OUT2 = U_GATE + 32
U_FB = U_OUT2 + KC
U_END = U_FB + 48 + 20

G1 = [(0, T1 // 2), (T1 // 2, T1 // 2)]
G2 = [(0, T2 // 2), (T2 // 2, T2 // 2)]
GL = [(CTX, SEQ)]
GS = [(0, SEQ)]


def build(nc, I, out):
    with ExitStack() as ctx:
        def sem(name):
            return ctx.enter_context(nc.semaphore(name))

        def ps(name, cols):
            return ctx.enter_context(nc.psum_tensor(name, [P, cols], F32))

        base0 = (nc.sbuf_base + 63) // 64 * 64

        def at(name, off, shape, dt=F32):
            return nc.alloc_sbuf_tensor_at(name, [P] + list(shape), dt, offset=base0 + off)

        top = [0]

        def seq(name, shape, dt=F32):
            n = 4 * int(np.prod(shape))
            t = at(name, top[0], shape, dt)
            top[0] += (n + 31) // 32 * 32
            return t

        raw = [seq(f"raw{s}", [KC, P]) for s in range(2)]
        wh = [seq(f"w_hi{s}", [KC, P], F32R) for s in range(2)]
        wl = [seq(f"w_lo{s}", [KC, P], F32R) for s in range(2)]
        const = seq("const", [CONST_N])
        col_a = seq("col_a", [65])
        col_b = seq("col_b", [72])
        col_c = seq("col_c", [72])
        silu_c = seq("silu_c", [KC, 2])
        ada = seq("ada", [72, 2])
        gain = [seq(f"gain{i}", [KC, 2]) for i in range(3)]
        resg = [seq(f"res_gain{i}", [KC, 2]) for i in range(3)]
        small = seq("small", [8])
        rope = seq("rope", [2, SEQ])
        PH = top[0]

        def cst(name, lo=0, hi=P):
            a, n = _C[name]
            return const[lo:hi, a:a + n]

        ident = cst("ident")
        ones = cst("ones")
        eps_col = cst("eps")
        minus_half = cst("minus_half")

        ACT_B = KC * T1 * 4
        X = at("x1", PH, [KC, T1])
        HH = at("h_hi", PH + ACT_B, [KC, T1], F32R)
        HL = at("h_lo", PH + 2 * ACT_B, [KC, T1], F32R)
        BH = at("branch_hi", PH + 3 * ACT_B, [KC, T1], F32R)
        BL = at("branch_lo", PH + 4 * ACT_B, [KC, T1], F32R)
        MG = at("merged", PH + 5 * ACT_B, [KC, T1])
        SCR = PH + 6 * ACT_B
        tmp = [at(f"tmp{s}", SCR + s * 4 * T1, [T1]) for s in range(2)]
        sqb = [at(f"square{s}", SCR + (2 + s) * 4 * T1, [T1]) for s in range(2)]
        ssq = at("ssq", SCR + 4 * 4 * T1, [T1])
        rstd = at("rstd", SCR + 5 * 4 * T1, [T1])
        S1 = SCR + 6 * 4 * T1
        DT = at("decay", S1, [RET_H, T1])
        o = S1 + RET_H * T1 * 4
        rq = at("ret_q", o, [T1]); o += 4 * T1
        rk = at("ret_k", o, [T1]); o += 4 * T1
        rvT = [at(f"ret_vT{s}", o + s * 4 * T1, [T1]) for s in range(2)]; o += 8 * T1
        rg = [at(f"ret_g{s}", o + s * 4 * T1, [T1]) for s in range(2)]; o += 8 * T1
        ST_W = [T1 - q0 for q0, _ in TILES]
        ST_AT = [sum(ST_W[:c]) for c in range(5)]
        rST = at("ret_scoresT", o, [sum(ST_W)]); o += 4 * sum(ST_W)
        rV = at("ret_v", o, [5, RET_DV]); o += 4 * 5 * RET_DV
        rY = at("ret_y", o, [5, RET_DV]); o += 4 * 5 * RET_DV
        bst = at("bn_stats", o, [5, 6]); o += 128
        bag = at("bn_aggr", o, [5, 2]); o += 64
        rvar = at("ret_var", o, [5]); o += 32
        rpow = at("ret_rstd", o, [5]); o += 32
        SCR_USED = o
        o = S1
        dqs = [at("diff_q0", o, [T1]), at("diff_q1", SCR + 2 * 4 * T1, [T1])]; o += 4 * T1
        dks = [at("diff_k0", o, [T1]), at("diff_k1", SCR + 3 * 4 * T1, [T1])]; o += 4 * T1
        dvT = at("diff_vT", o, [T1]); o += 4 * T1
        dR = at("diff_bias", o, [T1]); o += 4 * T1
        dL = [[at(f"diff_p{s}{m}", o + (2 * s + m) * 4 * T1, [T1]) for m in range(2)] for s in range(2)]; o += 16 * T1
        dT = [at(f"diff_pT{s}", o + s * 4 * 5 * P, [5, P]) for s in range(2)]; o += 8 * 5 * P
        dV = at("diff_v", o, [5, P]); o += 20 * P
        dO = at("diff_o", o, [5, P]); o += 20 * P
        dOn = at("diff_on", o, [5, P]); o += 20 * P
        dsq = at("diff_sq", o, [P]); o += 4 * P
        dmax = at("diff_max", o, [2, 2]); o += 32
        dnb = at("diff_nb", o, [2, 2]); o += 32
        dsum = at("diff_sum", o, [2, 2]); o += 32
        drc = at("diff_rc", o, [2, 2]); o += 32
        dlr = at("diff_lr", o, [2, 1]); o += 32
        dss = at("diff_ss", o, [5]); o += 32
        dss2 = at("diff_ss2", o, [5]); o += 32
        dpow = at("diff_rstd", o, [5]); o += 32
        SCR_USED = max(SCR_USED, o)
        rel = at("rel", SCR_USED, [T1])
        cb = at("conv_b", S1, [T1])
        cc = at("conv_c", S1 + 4 * T1, [T1])
        cu = at("conv_u", S1 + 8 * T1, [T1])
        cy = at("conv_y", S1 + 12 * T1, [T1])
        sg = [at(f"gate{s}", S1 + (4 + s) * 4 * T1, [T1]) for s in range(2)]
        MH = at("merged_hi", S1 + 6 * 4 * T1, [KC, T1], F32R)
        ML = at("merged_lo", S1 + 6 * 4 * T1 + ACT_B, [KC, T1], F32R)
        xt = [at(f"x_rows{t}", PH + 3 * ACT_B + 4096 * t, [D]) for t in range(5)]
        rows_a = at("rows_a", PH + 3 * ACT_B + 4096 * 5, [P])
        rows_b = at("rows_b", PH + 3 * ACT_B + 4096 * 5 + 512, [P])
        rows_c = at("rows_c", PH + 3 * ACT_B + 4096 * 5 + 1024, [P])
        lam_v = at("lam_v", PH + 3 * ACT_B + 4096 * 5 + 1536, [4, 64])
        lam_p = at("lam_p", PH + 3 * ACT_B + 4096 * 5 + 2560, [2, 64])
        araw = [at(f"ada_raw{s}", S1 + s * 4096, [KC, P]) for s in range(2)]
        ACT2 = KC * T2 * 4
        X2 = at("x2", PH + 5 * ACT2 + 32512, [KC, T2])
        H2H = at("h2_hi", PH, [KC, T2], F32R)
        H2L = at("h2_lo", PH + ACT2, [KC, T2], F32R)
        U2 = PH + 2 * ACT2
        UH2 = at("u2_hi", U2, [KC, T2], F32R)
        UL2 = at("u2_lo", U2 + ACT2, [KC, T2], F32R)
        Y2 = at("y2", U2 + 2 * ACT2, [KC, T2])
        E = U2 + 3 * ACT2
        tm2 = [at(f"tmp2_{s}", E + s * 4 * T2, [T2]) for s in range(2)]
        ss2 = at("ssq2", E + 2 * 4 * T2, [T2])
        rs2 = at("rstd2", E + 3 * 4 * T2, [T2])
        EE = E + 16 * T2
        rpbG = at("rpb_rows", EE, [NA_H * GRID_H, 31])
        rpbT = at("rpb_shifted", EE + 7936, [NA_H * GRID_H, 48])
        assert EE + 7936 + 12288 <= PH + 5 * ACT2 + 32512
        ctxr = [at(f"ctx_rows{t}", PH + 5 * ACT_B + 4096 * t, [D]) for t in range(2)]
        NA_OH = at("na_oT_hi", U2, [4, SEQ], F32R)
        NA_OL = at("na_oT_lo", U2 + 8192, [4, SEQ], F32R)
        L2 = U2 + 16384
        o = L2
        nB = at("na_bias", o, [3, NA_H, 256]); o += 3 * NA_H * 1024
        nq = at("na_q", o, [SEQ]); o += 2048
        nk = at("na_k", o, [T2]); o += 4 * T2
        nvT = at("na_vT", o, [T2]); o += 4 * T2
        nV = at("na_v", o, [NV + 2, P]); o += 512 * (NV + 2)
        nP = [at(f"na_p{s}", o + s * 2048, [SEQ]) for s in range(2)]; o += 4096
        nT = [at(f"na_pT{s}", o + s * 2048, [4, P]) for s in range(2)]; o += 4096
        nO = at("na_o", o, [NT, NA_H * NA_HD]); o += NT * 2048
        nst = at("na_stat", o, [2, 8]); o += 64
        nBs = [at(f"na_bias_head{s}", EE + 7936 + s * 3072, [3, 256]) for s in range(2)]
        assert o <= E
        o = L2
        ckvT = at("ckv", o, [2, T2]); o += 8 * T2
        CKH = at("ckv_hi", o, [2, T2], F32R); o += 8 * T2
        CKL = at("ckv_lo", o, [2, T2], F32R); o += 8 * T2
        cqT = at("cq", o, [6, SEQ]); o += 6 * 2048
        CQ = o
        CQH = at("cq_hi", o, [6, SEQ], F32R); o += 6 * 2048
        CQL = at("cq_lo", o, [6, SEQ], F32R); o += 6 * 2048
        mV = at("mla_v", o, [6, VD]); o += 24 * VD
        mst = at("mla_stat", o, [2, 8]); o += 64
        assert o <= E
        mP = [at(f"mla_p{s}", L2 + s * 4 * T2, [T2]) for s in range(2)]
        mO = at("mla_o", L2 + 3 * 8 * T2, [NT, 512])
        o = EE
        mkr = at("mla_kr", o, [T2]); o += 4 * T2
        mks = [at("mla_k0", o, [T2]), at("mla_k1", E, [T2])]; o += 4 * T2
        mqs = [at("mla_q0", o, [SEQ]), at("mla_q1", E + 4 * T2, [SEQ])]; o += 2048
        mqr = at("mla_qr", o, [SEQ]); o += 2048
        mvT = at("mla_vT", o, [T2]); o += 4 * T2
        mT = [at(f"mla_pT{s}", o + s * 4 * T2, [6, P]) for s in range(2)]; o += 8 * T2
        assert o <= PH + 5 * ACT2 + 32512
        MH2 = at("merged2_hi", L2, [KC, SEQ], F32R)
        ML2 = at("merged2_lo", L2 + 16384, [KC, SEQ], F32R)
        ML_OH = at("mla_oT_hi", CQ + 2048, [4, SEQ], F32R)
        ML_OL = at("mla_oT_lo", CQ + 2048 + 8192, [4, SEQ], F32R)
        sgl = [at(f"gate2_{s}", CQ + 2048 + 16384 + s * 2048, [SEQ]) for s in range(2)]
        orow = [at(f"out_rows{s}", U2 + s * 4096, [D]) for s in range(2)]

        G = [ps(f"unit_acc{s}", 1024) for s in range(2)]
        A = [ps(f"aux{s}", 1024) for s in range(2)]

        raw_landed = [sem(f"raw_landed{s}") for s in range(2)]
        hi_split = sem("hi_split")
        lo_split = sem("lo_split")
        unit_done = sem("unit_done")
        evicted = [sem(f"evicted{s}") for s in range(2)]
        const_in = sem("const_in")
        pe_passed, sp_passed, dve_passed = sem("pe_passed"), sem("sp_passed"), sem("dve_passed")
        x_in = sem("x_in")
        rows_in = sem("rows_in")
        decay_in = sem("decay_in")
        rel_in = sem("rel_in")
        rope_in = sem("rope_in")
        lam_in = sem("lam_in")
        xT_done = sem("xT_done")
        xT_out = sem("xT_out")
        cols_done = sem("cols_done")
        cols_out = sem("cols_out")
        cols_act = sem("cols_act")
        lam_dve = sem("lam_dve")
        lam_act = sem("lam_act")
        nrm_sq = sem("nrm_sq")
        nrm_add = sem("nrm_add")
        nrm_sum = sem("nrm_sum")
        nrm_root = sem("nrm_root")
        ap_tmp = sem("ap_tmp")
        ap_hi = sem("ap_hi")
        ap_lo = sem("ap_lo")
        r_sc = sem("ret_sc"); r_st = sem("ret_st"); r_vt = sem("ret_vt"); r_v = sem("ret_v_ready")
        r_pv = sem("ret_pv"); r_var = sem("ret_var_ready"); r_pow = sem("ret_pow"); r_y = sem("ret_y_ready")
        r_yt = sem("ret_yt"); r_tmp = sem("ret_tmp"); r_hi = sem("ret_hi")
        br_lo = sem("branch_ready")
        mg_add = sem("merged_added"); mg_hi = sem("merged_hi_done")
        d_bias = sem("diff_bias_ready"); d_qk = sem("diff_qk"); d_log = sem("diff_logits"); d_exp = sem("diff_exp")
        d_att = sem("diff_att"); d_tr = sem("diff_tr"); d_at = sem("diff_at"); d_pv = sem("diff_pv")
        d_o = sem("diff_o_out"); d_vt = sem("diff_vt"); d_v = sem("diff_v_ready"); d_ss = sem("diff_ss_ready")
        d_pow = sem("diff_pow"); d_on = sem("diff_on_ready"); d_ot = sem("diff_ot"); d_hi = sem("diff_hi")
        c_y = sem("conv_y_ready"); c_hi = sem("conv_hi")
        m_lo = sem("merged_ready")
        ff_r = sem("ff_relu"); ff_hi = sem("ff_hi"); ff_lo = sem("ff_lo")
        ada_landed = [sem(f"ada_landed{s}") for s in range(2)]
        ada_used = sem("ada_used")
        ada_out = sem("ada_out")
        ctx_in = sem("ctx_in"); ctx_done = sem("ctx_done"); ctx_out = sem("ctx_out")
        x2_out = sem("x2_out"); x2_tmp = sem("x2_tmp")
        rpb_in = sem("rpb_in"); rpb_zero = sem("rpb_zero"); y_zero = sem("y_zero")
        n_qk = sem("na_qk"); n_log = sem("na_log"); n_exp = sem("na_exp"); n_tr = sem("na_tr"); n_at = sem("na_at")
        n_pv = sem("na_pv"); n_o = sem("na_o_out"); n_vt = sem("na_vt"); n_v = sem("na_v_ready")
        n_tab = sem("na_bias_ready"); n_bias = sem("na_bias_head_ready")
        n_ot = sem("na_ot"); n_hi = sem("na_hi"); n_lo = sem("na_lo")
        k_qk = sem("mla_qk"); k_log = sem("mla_log"); k_exp = sem("mla_exp"); k_tr = sem("mla_tr"); k_tr1 = sem("mla_tr_second")
        k_at = sem("mla_at"); k_ad = sem("mla_ad"); k_pv = sem("mla_pv"); k_o = sem("mla_o_out")
        k_vt = sem("mla_vt"); k_v = sem("mla_v_ready"); k_ot = sem("mla_ot"); k_hi = sem("mla_hi"); k_lo = sem("mla_lo")
        k_rot = sem("mla_rot"); k_q = sem("mla_q_ready"); k_kr = sem("mla_kr_ready"); k_kra = sem("mla_kr_act")
        o_tr = sem("out_tr"); o_cp = sem("out_cp"); o_st = [sem(f"out_st{s}") for s in range(2)]

        def two(ap, n):
            return ap.rearrange("p (s n) -> p s n", s=2)

        def acc(t, geo, rows=P, lo=0):
            n = geo[0][1]
            if len(geo) == 1:
                return t[lo:rows, 0:n]
            return t[:, :].rearrange("p (s n) -> p s n", s=2)[lo:rows, :, 0:n]

        def like(ap, geo):
            return ap if len(geo) == 1 else two(ap, geo[0][1])

        def meta_pT(t, n):
            a = P if t == 4 else 512 + P * t
            return A[1][0:META, a:a + n]

        def landed(eng, v):
            eng.wait_ge(raw_landed[v.slot], val(Count(16 * (v.base // 2) + 16, *((r, 8 * st) for r, st in v.terms))))

        NSQ = {}
        for k, chunks in enumerate((8, 8, 8, 8, 8, 8, 2, 6, 8, 8, 8)):
            NSQ[k + 1] = NSQ.get(k, 0) + chunks

        block = ctx.enter_context(nc.Block())

        @block.sync
        def _(sp):
            sp.dma_start(const[:, :], I["const"]).then_inc(const_in, 16)
            for t, (q0, n) in enumerate(TILES):
                src = I["meta_tokens"] if t == 0 else I["x"][0, P * (t - 1):P * t, :]
                sp.dma_start(xt[t][0:n, :], src).then_inc(x_in, 16)
            row = 0
            for src, n in ((I["norm1_w"], 8), (I["norm2_w"], 8), (I["final_norm_w"], 8), (I["conv_w"], 24),
                           (I["diff_subln_w"], 1), (I["c_2"], 8), (I["c_ctx_2"], 8)):
                sp.dma_start(rows_a[row:row + n, :], flat(src, P)).then_inc(rows_in, 16)
                row += n
            row = 0
            for src, n in ((I["norm_g_2"], 48), (I["b_gate_2"], 16), (I["g_q_lora_2"], 6), (I["g_kv_lora_2"], 2)):
                sp.dma_start(rows_b[row:row + n, :], flat(src, P)).then_inc(rows_in, 16)
                row += n
            sp.dma_start(rows_c[0:72, :], flat(I["b_ada_2"], P)).then_inc(rows_in, 16)
            sp.dma_start(lam_v[:, :, :], I["diff_lambda"].partition_broadcast(P)).then_inc(lam_in, 16)

            def load(u, src, kc, n):
                if u.terms or u.base >= 2:
                    sp.wait_ge(lo_split, val(u + (-1)))
                if u.terms:
                    alone(sp, sp_passed)
                sp.dma_start(raw[u.slot][:, 0:kc, 0:n], src.rearrange("(k p) n -> p k n", p=P)).then_inc(
                    raw_landed[u.slot], 16)

            def load_ada(a):
                if a.terms or a.base >= 2:
                    sp.wait_ge(ada_used, val(a + (-1)))
                if a.terms:
                    alone(sp, sp_passed)
                sp.dma_start(araw[a.slot][:, :, :],
                             I["w_ada_2"][0, :, bass.ds(a.value() * P, P)].rearrange("(k p) n -> p k n", p=P)
                             ).then_inc(ada_landed[a.slot], 16)

            def cols(name, at_, n=P, j=None, r0=0, rn=D):
                w = I[name][0] if j is None else I[name][0, j]
                return w[r0:r0 + rn, bass.ds(at_, n)]

            def ret_cols(h, k):
                c, step = ((W_RQ, P), (W_RK, P), (W_RV, 256), (W_RV + P, 256), (W_RG, 256), (W_RG + P, 256))[k]
                return cols("w_in", h * step + c)

            for k in range(2):
                load(Count(k), ret_cols(0, k), KC, P)
            sp.dma_start(DT[:, :, :], I["decay"]).then_inc(decay_in, 16)
            sp.dma_start(rel[:, :], I["rel"]).then_inc(rel_in, 16)
            sp.dma_start(rope[NOPE:QK, :, :], I["rope"]).then_inc(rope_in, 16)
            with sp.Fori(0, RET_H - 1) as h:
                for k in range(2, 6):
                    load(Count(U_RET + k, (h, 6)), ret_cols(h, k), KC, P)
                for k in range(2):
                    load(Count(U_RET + 6 + k, (h, 6)), ret_cols(h + 1, k), KC, P)
            for k in range(2, 6):
                load(Count(U_RET + 6 * (RET_H - 1) + k), ret_cols(RET_H - 1, k), KC, P)

            def load_branch(r):
                with sp.Fori(0, KC) as n:
                    u = Count(U_BR[r], (n, 2))
                    load(u, cols("w_in", n * P + (W_GATE + r * D)), KC, P)
                    load(u + 1, cols("w_branch", n * P, j=r), KC, P)

            load_branch(0)
            with sp.Fori(0, DIFF_H // 2) as i:
                for e in range(2):
                    for k, c in enumerate((W_DQ, W_DK, W_DV)):
                        load(Count(U_DIFF + 3 * e + k, (i, 6)), cols("w_in", i * 256 + (c + e * P)), KC, P)
            load_branch(1)
            with sp.Fori(0, KC // 2) as i:
                for e in range(2):
                    for k, c in enumerate((W_CB, W_CC, W_CX)):
                        load(Count(U_CONV + 3 * e + k, (i, 6)), cols("w_in", i * 256 + (c + e * P)), KC, P)
            load_branch(2)
            for n in range(KC):
                load(Count(U_OUT + n), cols("w_out", n * P), KC, P)
                load_ada(Count(n))
            with sp.Fori(0, FF1 // D) as part:
                with sp.Fori(0, 4) as i:
                    for e in range(2):
                        load(Count(U_FF + e, (part, 16), (i, 2)), cols("w_up", part * D + (i * 256 + e * P)), KC, P)
                        load_ada(Count(8 + e, (part, 16), (i, 2)))
                with sp.Fori(0, 4) as i:
                    for e in range(2):
                        load(Count(U_FF + 8 + e, (part, 16), (i, 2)),
                             I["w_down"][0, bass.ds(part * D, D), bass.ds(i * 256 + e * P, P)], KC, P)
                        load_ada(Count(16 + e, (part, 16), (i, 2)))
            for t in range(2):
                sp.dma_start(ctxr[t][:, :], I["ctx_2"][0, P * t:P * (t + 1), :]).then_inc(ctx_in, 16)

            def load_swiglu(base, w1, w3, w2):
                with sp.Fori(0, 2) as part:
                    with sp.Fori(0, 8) as n:
                        for e, w in enumerate((w1, w3)):
                            load(Count(base + e, (part, 24), (n, 2)), cols(w, part * D + n * P), KC, P)
                    with sp.Fori(0, 4) as i:
                        for e in range(2):
                            load(Count(base + 16 + e, (part, 24), (i, 2)),
                                 I[w2][0, bass.ds(part * D, D), bass.ds(i * 256 + e * P, P)], KC, P)
                with sp.Fori(0, 6) as n:
                    for e, w in enumerate((w1, w3)):
                        load(Count(base + 48 + e, (n, 2)), cols(w, n * P + 2 * D), KC, P)
                with sp.Fori(0, 4) as i:
                    for e in range(2):
                        load(Count(base + 60 + e, (i, 2)),
                             I[w2][0, 2 * D:FF2, bass.ds(i * 256 + e * P, P)], 6, P)

            src = I["rpb_2"][0]
            for r in range(GRID_H):
                sp.dma_start(
                    rpbG[r:P:GRID_H, :, :].rearrange("p (h a) n -> p h (a n)", h=NA_H),
                    src[:, GRID_H - 1 - r:2 * GRID_H - 1 - r, :].rearrange("h r n -> h (r n)").partition_broadcast(16)
                ).then_inc(rpb_in, 16)
            load_swiglu(U_FA, "ffn1_w1_2", "ffn1_w3_2", "ffn1_w2_2")
            with sp.Fori(0, 2) as i:
                for e in range(2):
                    for k, c in enumerate((W_QA, W_KA, W_VA)):
                        load(Count(U_NA + 3 * e + k, (i, 6)), cols("w_in_2", i * 256 + (c + e * P)), KC, P)
            for k in range(2):
                load(Count(U_LORA + k), cols("w_in_2", W_CKV + k * P), KC, P)
            load(Count(U_LORA + 2), cols("w_in_2", W_KR - NOPE, QK), KC, QK)
            for k in range(6):
                load(Count(U_LORA + 3 + k), cols("w_in_2", W_CQ + k * P), KC, P)
            with sp.Fori(0, 8) as h:
                load(Count(U_MLA, (h, 2)), I["w_uq_2"][0, :, bass.ds(h * QK, QK)], 6, QK)
                load(Count(U_MLA + 1, (h, 2)), I["w_ukv_2"][0, :, bass.ds(h * P, P)], 2, P)
            with sp.Fori(0, KC) as n:
                load(Count(U_GATE, (n, 4)), cols("w_in_2", n * P + W_G2), KC, P)
                load(Count(U_GATE + 1, (n, 4)), I["w_o_na_2"][0, :, bass.ds(n * P, P)], 4, P)
                load(Count(U_GATE + 2, (n, 4)), cols("w_in_2", n * P + (W_G2 + D)), KC, P)
                load(Count(U_GATE + 3, (n, 4)), I["w_o_mla_2"][0, :, bass.ds(n * P, P)], 4, P)
            with sp.Fori(0, 4) as i:
                for e in range(2):
                    load(Count(U_OUT2 + e, (i, 2)), cols("w_out_2", i * 256 + e * P), KC, P)
            load_swiglu(U_FB, "ffn2_w1_2", "ffn2_w3_2", "ffn2_w2_2")
            grid = out[0].rearrange("(r c) d -> c r d", r=GRID_H)
            for t in range(NT):
                sp.wait_ge(o_cp, t + 1)
                sp.dma_start(grid[16 * t:16 * t + 16, :, :], orow[t % 2][:, :]).then_inc(o_st[t % 2], 16)
            for s in range(2):
                sp.wait_ge(o_st[s], 32)

        @block.tensor
        def _(pe):
            def tr(dst, src, k=P, k0=0):
                return pe.transpose(dst, src, ident[k0:k0 + k, k0:k0 + k])

            def unit(u, hi, lo, geo, kc=KC, n=P, ready=None, part=None):
                k0, k1 = part or (0, kc)
                if k0 == 0:
                    pe.wait_ge(lo_split, val(u + 1))
                    pe.wait_ge(evicted[u.slot], val(u.turns() + 1))
                s = u.slot
                for k in range(k0, k1):
                    if ready is not None:
                        pe.wait_ge(ready[0], ready[1] + k + 1)
                    for i, (w, x) in enumerate(((wh, hi), (wh, lo), (wl, hi))):
                        for j, (a, m) in enumerate(geo):
                            last = pe.matmul(G[s][0:n, 512 * j:512 * j + m], w[s][:, k, 0:n], x[:, k, a:a + m],
                                             start=(k == 0 and i == 0), stop=(k == kc - 1 and i == 2))
                if k1 == kc:
                    last.then_inc(unit_done, 1)

            norms = [0]

            def sum_squares(src, geo):
                norms[0] += 1
                pe.wait_ge(nrm_add, NSQ[norms[0]])
                for j, (a, m) in enumerate(geo):
                    last = pe.matmul(A[0][:, 512 * j:512 * j + m], ones, src[:, a:a + m], start=True, stop=True)
                last.then_inc(nrm_sum, 1)

            pe.wait_ge(const_in, 16)
            pe.wait_ge(rows_in, 16 * 12)
            tr(A[0][:, 0:65], rows_a[0:65, :], 65)
            tr(A[0][:, 128:200], rows_b[0:72, :], 72)
            tr(A[0][:, 256:328], rows_c[0:72, :], 72).then_inc(cols_done, 1)
            pe.wait_ge(x_in, 16 * 5)
            pe.wait_ge(cols_out, 1)
            for c in range(KC):
                if c >= 2:
                    pe.wait_ge(xT_out, val(c - 1))
                for t, (q0, n) in enumerate(TILES):
                    dst = A[c % 2][:, 512:512 + n] if t == 0 else A[c % 2][:, P * (t - 1):P * t]
                    last = tr(dst, xt[t][0:n, P * c:P * (c + 1)], n)
                last.then_inc(xT_done, 1)
            sum_squares(ssq, G1)

            def retention(h):
                u = Count(U_RET, (h, 6))
                for k in range(3):
                    unit(u + k, HH, HL, G1, ready=(ap_lo, 0) if k == 0 else None)
                for s in range(2):
                    pe.wait_ge(evicted[s], val(u.turns() + 2))
                for c, (q0, n) in enumerate(TILES):
                    if c >= 2:
                        pe.wait_ge(r_st, val(Count(c - 1, (h, 5))))
                    w = ST_W[c]
                    for a in range(0, w, 512):
                        m = min(512, w - a)
                        last = pe.matmul(A[c % 2][0:n, a:a + m], rk[:, q0:q0 + n], rq[:, q0 + a:q0 + a + m],
                                         start=True, stop=True)
                    last.then_inc(r_sc, 1)
                unit(u + 3, HH, HL, G1)
                for s in range(2):
                    pe.wait_ge(evicted[s], val(u.turns() + 3))
                pe.wait_ge(r_st, val(Count(5, (h, 5))))
                for half in range(2):
                    for t, (q0, n) in reversed(list(enumerate(TILES))):
                        a = (t - 1) * RET_DV + half * P
                        dst = A[1][0:n, half * P:half * P + P] if t == 0 else A[0][:, a:a + P]
                        last = tr(dst, rvT[half][:, q0:q0 + n])
                last.then_inc(r_vt, 1)
                unit(u + 4, HH, HL, G1)
                pe.wait_ge(r_v, val(Count(1, (h, 1))))
                for t, (q0, n) in reversed(list(enumerate(TILES))):
                    dst = A[1][0:n, 0:RET_DV] if t == 0 else A[0][:, (t - 1) * RET_DV:t * RET_DV]
                    for c in range(t, -1, -1):
                        k0, kn = TILES[c]
                        a = ST_AT[c] + q0 - k0
                        last = pe.matmul(dst, rST[0:kn, a:a + n], rV[0:kn, c, :], start=(c == t), stop=(c == 0))
                last.then_inc(r_pv, 1)
                unit(u + 5, HH, HL, G1)
                pe.wait_ge(r_y, val(Count(1, (h, 1))))
                for half in range(2):
                    for t, (q0, n) in reversed(list(enumerate(TILES))):
                        a = 512 if t == 0 else P * (t - 1)
                        last = tr(A[half][:, a:a + n], rY[0:n, t, half * P:half * P + P], n)
                last.then_inc(r_yt, 1)

            with pe.Fori(0, RET_H) as h:
                retention(h)

            def merge(r):
                with pe.Fori(0, KC) as n:
                    u = Count(U_BR[r], (n, 2))
                    unit(u, HH, HL, G1)
                    unit(u + 1, BH, BL, G1, ready=(br_lo, KC * r))

            merge(0)

            def diff_head(i, e, more):
                u = turn(i, U_DIFF + 3 * e, 6)
                dq, dk = dqs[e], dks[e]

                def fill(k, k0, k1):
                    if more:
                        unit(u + 3 + k, HH, HL, G1, part=(k0, k1))

                def cnt(k):
                    return turn(i, k + 5 * e, 10)

                def qk(t):
                    q0, n = TILES[t]
                    if t < 4:
                        pe.wait_ge(d_log, val(cnt(4 - t)))
                    w = q0 + n
                    if t == 0:
                        alone(pe, pe_passed)
                    for m in range(2):
                        r = slice(64 * m, 64 * m + 64)
                        last = pe.matmul(A[0][0:n, 512 * m:512 * m + min(w, 512)], dq[r, q0:q0 + n],
                                         dk[r, 0:min(w, 512)], start=True, stop=True)
                    if w > 512:
                        for m in range(2):
                            r = slice(64 * m, 64 * m + 64)
                            last = pe.matmul(A[1][0:n, 512 * m:512 * m + w - 512], dq[r, q0:q0 + n],
                                             dk[r, 512:w], start=True, stop=True)
                    last.then_inc(d_qk, 1)

                def transpose_p(t):
                    q0, n = TILES[t]
                    pe.wait_ge(d_att, val(cnt(5 - t)))
                    if t < 4:
                        pe.wait_ge(d_at, val(cnt(4 - t)))
                    p = dL[t % 2][0]
                    if t == 0:
                        alone(pe, pe_passed)
                    for c in range(t, 0, -1):
                        tr(A[1][:, 512 + P * (c - 1):512 + P * (c - 1) + n],
                           p[0:n, TILES[c][0]:TILES[c][0] + P], n)
                    tr(meta_pT(t, n), p[0:n, 0:META], n).then_inc(d_tr, 1)

                def pv(t):
                    q0, n = TILES[t]
                    pe.wait_ge(d_at, val(cnt(5 - t)))
                    if t < 4:
                        pe.wait_ge(d_o, val(cnt(4 - t)))
                    if t == 0:
                        alone(pe, pe_passed)
                    for c in range(t, -1, -1):
                        kn = TILES[c][1]
                        last = pe.matmul(A[1][0:n, 256:384], dT[t % 2][0:kn, c, 0:n], dV[0:kn, c, :],
                                         start=(c == t), stop=(c == 0))
                    last.then_inc(d_pv, 1)

                for k in range(2):
                    pe.wait_ge(evicted[(u + k).slot], val((u + k).turns() + 2))
                pe.wait_ge(br_lo, val(turn(i, KC + e, 2)))
                qk(4)
                fill(0, 0, 3)
                qk(3)
                pe.wait_ge(evicted[u.slot], val((u + 2).turns() + 2))
                for t, (q0, n) in reversed(list(enumerate(TILES))):
                    dst = A[1][0:n, P:2 * P] if t == 0 else A[1][:, 512 + P * (t - 1):512 + P * t]
                    last = tr(dst, dvT[:, q0:q0 + n])
                last.then_inc(d_vt, 1)
                fill(0, 3, 8)
                pe.wait_ge(d_v, val(turn(i, 1 + e, 2)))
                transpose_p(4)
                qk(2)
                fill(1, 0, 3)
                pv(4)
                transpose_p(3)
                qk(1)
                fill(1, 3, 6)
                pv(3)
                transpose_p(2)
                qk(0)
                fill(1, 6, 8)
                pv(2)
                transpose_p(1)
                fill(2, 0, 1)
                pv(1)
                transpose_p(0)
                fill(2, 1, 2)
                pv(0)
                fill(2, 2, 6)
                pe.wait_ge(d_on, val(turn(i, 1 + e, 2)))
                for t, (q0, n) in reversed(list(enumerate(TILES))):
                    dst = A[1][:, 0:n] if t == 0 else A[0][:, P * (t - 1):P * t]
                    last = tr(dst, dOn[0:n, t, :], n)
                last.then_inc(d_ot, 1)
                fill(2, 6, 8)

            for k in range(3):
                unit(Count(U_DIFF + k), HH, HL, G1)
            with pe.Fori(0, DIFF_H // 2 - 1) as i:
                for e in range(2):
                    diff_head(i, e, True)
            for e in range(2):
                diff_head(DIFF_H // 2 - 1, e, e == 0)
            merge(1)

            with pe.Fori(0, KC // 2) as i:
                for k in range(6):
                    unit(Count(U_CONV + k, (i, 6)), HH, HL, G1)
            merge(2)

            def ada_unit(a):
                pe.wait_ge(ada_landed[a.slot], val(Count(16 * (a.base // 2) + 16, *((r, 8 * st) for r, st in a.terms))))
                dst = A[1][:, bass.ds(a.value() * 2 + 512, 2)]
                for k in range(KC):
                    last = pe.matmul(dst, araw[a.slot][:, k, :], silu_c[:, k, :], start=(k == 0), stop=(k == KC - 1))
                last.then_inc(ada_used, 1)

            pe.wait_ge(cols_act, 1)
            for n in range(KC):
                unit(Count(U_OUT + n), MH, ML, G1, ready=(m_lo, 0))
                ada_unit(Count(n))
            sum_squares(ssq, G1)

            with pe.Fori(0, FF1 // D) as part:
                with pe.Fori(0, 4) as i:
                    for e in range(2):
                        unit(Count(U_FF + e, (part, 16), (i, 2)), HH, HL, G1, ready=(ap_lo, KC))
                        ada_unit(Count(8 + e, (part, 16), (i, 2)))
                with pe.Fori(0, 4) as i:
                    for e in range(2):
                        u = Count(U_FF + 8 + e, (part, 16), (i, 2))
                        pe.wait_ge(ff_lo, val(Count(8, (part, 8))))
                        unit(u, BH, BL, G1)
                        ada_unit(Count(16 + e, (part, 16), (i, 2)))
            sum_squares(ssq, G1)

            pe.wait_ge(ctx_in, 32)
            pe.wait_ge(nrm_root, 3)
            for c in range(KC):
                if c >= 2:
                    pe.wait_ge(ctx_out, val(c - 1))
                for t in range(2):
                    last = tr(A[c % 2][:, P * t:P * t + P], ctxr[t][:, P * c:P * (c + 1)])
                last.then_inc(ctx_done, 1)
            pe.wait_ge(ctx_out, KC)
            sum_squares(ss2, G2)

            def swiglu(base, geo, ap0, f0):
                with pe.Fori(0, 2) as part:
                    with pe.Fori(0, 8) as n:
                        for e in range(2):
                            unit(Count(base + e, (part, 24), (n, 2)), H2H, H2L, geo,
                                 ready=(ap_lo, ap0) if e == 0 else None)
                    with pe.Fori(0, 4) as i:
                        for e in range(2):
                            pe.wait_ge(ff_lo, val(Count(f0 + 8, (part, 8))))
                            unit(Count(base + 16 + e, (part, 24), (i, 2)), UH2, UL2, geo)
                with pe.Fori(0, 6) as n:
                    for e in range(2):
                        unit(Count(base + 48 + e, (n, 2)), H2H, H2L, geo)
                with pe.Fori(0, 4) as i:
                    for e in range(2):
                        pe.wait_ge(ff_lo, f0 + 22)
                        unit(Count(base + 60 + e, (i, 2)), UH2, UL2, geo, kc=6)

            swiglu(U_FA, G2, 2 * KC, 32)
            sum_squares(ss2, G2)
            sum_squares(ss2, G2)

            def na_pair(p, u):
                for k in range(3):
                    unit(u + k, H2H, H2L, GL if k == 0 else G2, ready=(ap_lo, 3 * KC) if k == 0 else None)
                for k in range(3):
                    pe.wait_ge(evicted[(u + k).slot], val((u + k).turns() + 2))
                for half in range(2):
                    if half:
                        pe.wait_ge(n_v, val(Count(half + 2 * p[2], (p[0], 2 * p[1]))))
                    for j in (range(5) if half == 0 else range(5, NV + 2)):
                        a = CTX + V_STARTS[j] if j < NV else P * (j - NV)
                        b = j if half == 0 else j - 5
                        last = tr(A[1][:, P * b:P * b + P] if b < 4 else A[0][:, 0:P], nvT[:, a:a + P])
                    last.then_inc(n_vt, 1)
                pe.wait_ge(n_v, val(Count(2 + 2 * p[2], (p[0], 2 * p[1]))))

                def at_(s):
                    return Count(s + 8 * p[2], (p[0], 8 * p[1]))

                def qk(s):
                    e, t = divmod(s, NT)
                    if s >= 2:
                        pe.wait_ge(n_exp, val(at_(s - 1)))
                    r = slice(64 * e, 64 * e + 64)
                    a = CTX + NA_START[t]
                    q = nq[r, P * t:P * t + P]
                    b = 512 * (s % 2)
                    pe.matmul(A[0][:, b:b + 256], q, nk[r, a:a + 256], start=True, stop=True)
                    pe.matmul(A[0][:, b + 256:b + 512], q, nk[r, 0:CTX], start=True, stop=True).then_inc(n_qk, 1)

                def transpose_p(s):
                    pe.wait_ge(n_exp, val(at_(s + 1)))
                    if s:
                        pe.wait_ge(n_at, val(at_(s)))
                    for j in range(4):
                        last = tr(A[1][:, P * j:P * j + P], nP[s % 2][:, P * j:P * j + P])
                    last.then_inc(n_tr, 1)

                def pv(s):
                    e, t = divmod(s, NT)
                    pe.wait_ge(n_at, val(at_(s + 1)))
                    if s:
                        pe.wait_ge(n_o, val(at_(s)))
                    v0 = NA_START[t] // 64
                    for j, v in enumerate((v0, v0 + 2, NV, NV + 1)):
                        last = pe.matmul(A[1][:, 512:512 + NA_HD], nT[s % 2][:, j, :], nV[:, v, 64 * e:64 * e + 64],
                                         start=(j == 0), stop=(j == 3))
                    last.then_inc(n_pv, 1)

                qk(0)
                qk(1)
                for s in range(8):
                    transpose_p(s)
                    if s:
                        pv(s - 1)
                    if s < 6:
                        qk(s + 2)
                pv(7)

            with pe.Fori(0, 2) as i:
                for e in range(2):
                    na_pair((i, 2, e), Count(U_NA + 3 * e, (i, 6)))
            pe.wait_ge(n_o, 32)
            for c in range(4):
                if c >= 2:
                    pe.wait_ge(n_lo, val(c - 1))
                for t in range(NT):
                    last = tr(A[c % 2][:, P * t:P * t + P], nO[:, t, P * c:P * c + P])
                last.then_inc(n_ot, 1)

            for k in range(2):
                unit(Count(U_LORA + k), H2H, H2L, G2)
            unit(Count(U_LORA + 2), H2H, H2L, G2, n=QK)
            pe.wait_ge(n_lo, 4)
            sum_squares(ss2, G2)
            for k in range(6):
                unit(Count(U_LORA + 3 + k), H2H, H2L, GL)
            pe.wait_ge(k_kr, 1)
            pe.matmul(A[1][0:QK, 0:SEQ], cst("rot", 0, QK), mkr[0:QK, CTX:T2], start=True, stop=True).then_inc(k_rot, 1)
            sum_squares(ss2, GS)
            pe.wait_ge(ap_lo, 4 * KC + 8)

            def mla_ready(u, e, head):
                pe.wait_ge(evicted[u.slot], val(u.turns() + 2))
                pe.matmul(A[1][0:QK, 0:SEQ], cst("rot", 0, QK), mqs[e][0:QK, :], start=True, stop=True).then_inc(k_rot, 1)
                pe.wait_ge(evicted[(u + 1).slot], val((u + 1).turns() + 2))
                if head:
                    pe.wait_ge(k_o, val(head))
                alone(pe, pe_passed)
                for j in range(6):
                    last = tr(A[1][:, 512 + VD * j:512 + VD * j + VD], mvT[64:P, P * j:P * j + P], 64, 64)
                last.then_inc(k_vt, 1)

            def mla_head(i, e, more):
                u = turn(i, U_MLA + 2 * e, 4)
                mq, mk = mqs[e], mks[e]

                def cnt(k):
                    return turn(i, k + NT * e, 2 * NT)

                def fill_q(k0, k1):
                    if more:
                        unit(u + 2, CQH, CQL, GS, kc=6, n=QK, part=(k0, k1))

                def fill_kv(k0, k1):
                    if more:
                        unit(u + 3, CKH, CKL, G2, kc=2, part=(k0, k1))

                def qk(t):
                    if t:
                        pe.wait_ge(k_exp, val(cnt(t)))
                    for a, m in ((0, 512), (512, T2 - 512)):
                        last = pe.matmul(A[0][:, a:a + m], mq[0:QK, P * t:P * t + P], mk[0:QK, a:a + m],
                                         start=True, stop=True)
                    last.then_inc(k_qk, 1)

                def transpose_p(t):
                    pe.wait_ge(k_exp, val(cnt(t + 1)))
                    if t:
                        pe.wait_ge(k_ad, val(cnt(t)))
                        pe.wait_ge(k_at, val(cnt(t)))
                    if t > 1:
                        pe.wait_ge(k_o, val(cnt(t - 1)))
                    for j in (4, 5):
                        last = tr(A[1][:, P * j:P * j + P], mP[t % 2][:, P * j:P * j + P])
                    last.then_inc(k_tr1, 1)
                    for j in range(4):
                        last = tr(A[1][:, P * j:P * j + P], mP[t % 2][:, P * j:P * j + P])
                    last.then_inc(k_tr, 1)

                def pv(t):
                    pe.wait_ge(k_at, val(cnt(t + 1)))
                    pe.wait_ge(k_ad, val(cnt(min(t + 2, NT))))
                    for j in range(6):
                        last = pe.matmul(A[1][:, 768:768 + VD], mT[t % 2][:, j, :], mV[:, j, :],
                                         start=(j == 0), stop=(j == 5))
                    last.then_inc(k_pv, 1)

                pe.wait_ge(k_q, val(turn(i, 1 + e, 2)))
                qk(0)
                fill_q(0, 2)
                pe.wait_ge(k_v, val(turn(i, 1 + e, 2)))
                qk(1)
                fill_q(2, 3)
                transpose_p(0)
                qk(2)
                fill_q(3, 5)
                transpose_p(1)
                pv(0)
                qk(3)
                fill_q(5, 6)
                transpose_p(2)
                pv(1)
                fill_kv(0, 1)
                transpose_p(3)
                fill_kv(1, 2)
                pv(2)
                pe.wait_ge(k_o, val(cnt(NT - 1)))
                pv(3)
                if more:
                    mla_ready(u + 2, 1 - e, cnt(NT))

            unit(Count(U_MLA), CQH, CQL, GS, kc=6, n=QK)
            unit(Count(U_MLA + 1), CKH, CKL, G2, kc=2)
            mla_ready(Count(U_MLA), 0, None)
            with pe.Fori(0, 3) as i:
                for e in range(2):
                    mla_head(i, e, True)
            for e in range(2):
                mla_head(3, e, e == 0)
            pe.wait_ge(k_o, 32)
            for c in range(4):
                if c >= 2:
                    pe.wait_ge(k_lo, val(c - 1))
                for t in range(NT):
                    last = tr(A[c % 2][:, P * t:P * t + P], mO[:, t, P * c:P * c + P])
                last.then_inc(k_ot, 1)

            with pe.Fori(0, KC) as n:
                u = Count(U_GATE, (n, 4))
                unit(u, H2H, H2L, GL)
                unit(u + 1, NA_OH, NA_OL, GS, kc=4)
                unit(u + 2, H2H, H2L, GL)
                pe.wait_ge(k_lo, 4)
                unit(u + 3, ML_OH, ML_OL, GS, kc=4)
            with pe.Fori(0, 4) as i:
                for e in range(2):
                    unit(Count(U_OUT2 + e, (i, 2)), MH2, ML2, GS, ready=(m_lo, KC))
            sum_squares(ss2, GL)
            sum_squares(ss2, GL)
            swiglu(U_FB, GL, 4 * KC + 8, 32 + 22)
            sum_squares(ss2, GL)

            for t in range(NT):
                if t == 0:
                    pe.wait_ge(x2_out, 4 * KC)
                if t >= 2:
                    pe.wait_ge(o_cp, val(t - 1))
                for c in range(KC):
                    last = tr(A[t % 2][:, P * c:P * c + P], X2[:, c, CTX + P * t:CTX + P * t + P])
                last.then_inc(o_tr, 1)

        @block.scalar
        def _(act):
            for s in range(2):
                act.sem_inc(evicted[s], 1)

            def split(v):
                act.drain()
                landed(act, v)
                if v.terms or v.base >= 2:
                    act.wait_ge(unit_done, val(v + (-1)))
                act.activation(wh[v.slot][:, :, :], raw[v.slot][:, :, :], ACT.Copy).then_inc(hi_split, 1)

            def done(u):
                act.drain()
                act.wait_ge(unit_done, val(u + 1))

            nsq, nroot, nap = [0], [0], [0]

            def square(chunk, buf, n):
                if nsq[0] >= 2:
                    act.wait_ge(nrm_add, val(nsq[0] - 1))
                act.activation(buf[nsq[0] % 2][:, 0:n], chunk, ACT.Square).then_inc(nrm_sq, 1)
                nsq[0] += 1

            def root(dst, geo, features):
                nroot[0] += 1
                act.drain()
                act.wait_ge(nrm_sum, nroot[0])
                n0 = geo[0][0]
                n1 = geo[-1][0] + geo[-1][1]
                act.activation(like(dst[:, n0:n1], geo), acc(A[0], geo), ACT.Sqrt, bias=eps_col,
                               scale=1.0 / features).then_inc(nrm_root, 1)

            def hi_part(dst, src):
                nap[0] += 1
                act.wait_ge(ap_tmp, nap[0])
                act.activation(dst, src, ACT.Copy).then_inc(ap_hi, 1)

            act.wait_ge(cols_out, 1)
            c2 = col_a[:, 49:65].rearrange("p (e k) -> p k e", e=2)
            act.activation(silu_c[:, :, :], c2, ACT.Silu).then_inc(cols_act, 1)
            act.wait_ge(lam_dve, 1)
            act.activation(small[:, 4:6], small[:, 2:4], ACT.Exp).then_inc(lam_act, 1)
            for v in range(2):
                split(Count(v))
            for c in range(KC):
                act.wait_ge(xT_out, c + 1)
                square(X[:, c, :], sqb, T1)
            root(rstd, G1, D)
            for c in range(KC):
                hi_part(HH[:, c, :], tmp[c % 2][:, :])

            with act.Fori(0, RET_H) as h:
                u = Count(U_RET, (h, 6))
                for k, dst in enumerate((rq, rk, rvT[0], rvT[1])):
                    done(u + k)
                    act.activation(two(dst[:, :], T1 // 2), acc(G[k % 2], G1), ACT.Copy).then_inc(evicted[k % 2], 1)
                    split(u + k + 2)
                act.wait_ge(r_vt, val(Count(1, (h, 1))))
                act.activation(rV[:, 1:5, :], A[0][:, :].rearrange("p (t n) -> p t n", t=4), ACT.Copy)
                act.activation(rV[0:META, 0, :], A[1][0:META, 0:RET_DV], ACT.Copy).then_inc(r_v, 1)
                for k in (4, 5):
                    done(u + k)
                    act.activation(two(rg[k - 4][:, :], T1 // 2), acc(G[k % 2], G1), ACT.Silu).then_inc(
                        evicted[k % 2], 1)
                    split(u + k + 2)
                for half in range(2):
                    act.wait_ge(r_tmp, val(Count(half + 1, (h, 2))))
                    act.activation(BH[:, bass.ds(h * 2 + half, 1), :], tmp[half][:, :].unsqueeze(1),
                                   ACT.Copy).then_inc(r_hi, 1)

            def merge(r):
                with act.Fori(0, KC) as n:
                    u = Count(U_BR[r], (n, 2))
                    done(u)
                    act.wait_ge(evicted[(u + -1).slot], val((u + -1).turns() + 2))
                    act.activation(two(sg[0][:, :], T1 // 2), acc(G[u.slot], G1), ACT.Sigmoid).then_inc(
                        evicted[u.slot], 1)
                    split(u + 2)
                    split(u + 3)
                    if r == 2:
                        act.wait_ge(mg_add, val(Count(1, (n, 1))))
                        act.activation(MH[:, bass.ds(n, 1), :], MG[:, bass.ds(n, 1), :], ACT.Copy).then_inc(mg_hi, 1)

            merge(0)

            def diff_project(u, k, e):
                v = u + k
                done(v)
                act.activation(two((dqs[e], dks[e], dvT)[k][:, :], T1 // 2), acc(G[v.slot], G1),
                               ACT.Copy).then_inc(evicted[v.slot], 1)
                split(v + 2)

            def diff_head(i, e, more):
                u = turn(i, U_DIFF + 3 * e, 6)

                def cnt(k):
                    return turn(i, k + 5 * e, 10)

                def next_head(k):
                    if more:
                        diff_project(u + 3, k, 1 - e)

                def exps(t):
                    q0, n = TILES[t]
                    act.drain()
                    act.wait_ge(d_log, val(cnt(5 - t)))
                    for m in range(2):
                        p = dL[t % 2][m][0:n, 0:q0 + n]
                        last = act.activation(p, p, ACT.Exp, bias=dnb[0:n, t % 2, m:m + 1], scale=0.125,
                                              accum_out=dsum[0:n, t % 2, m:m + 1])
                    last.then_inc(d_exp, 1)

                def copy_pT(t):
                    q0, n = TILES[t]
                    act.drain()
                    act.wait_ge(d_tr, val(cnt(5 - t)))
                    last = act.activation(dT[t % 2][0:META, 0, 0:n], meta_pT(t, n), ACT.Copy)
                    if t:
                        last = act.activation(dT[t % 2][:, 1:t + 1, :],
                                              A[1][:, 512:512 + P * t].rearrange("p (c n) -> p c n", n=P), ACT.Copy)
                    last.then_inc(d_at, 1)

                def out_o(t):
                    q0, n = TILES[t]
                    act.drain()
                    act.wait_ge(d_pv, val(cnt(5 - t)))
                    act.activation(dO[0:n, t, :], A[1][0:n, 256:384], ACT.Copy)
                    act.activation(dsq[0:n, :], A[1][0:n, 256:384], ACT.Square,
                                   accum_out=dss[0:n, t:t + 1]).then_inc(d_o, 1)

                head = i * 2 + e
                act.drain()
                act.activation(dR[:, :], rel[:, :], ACT.Copy,
                               scale=cst("slope8")[:, bass.ds(head, 1)]).then_inc(d_bias, 1)
                exps(4)
                act.drain()
                act.wait_ge(d_vt, val(turn(i, 1 + e, 2)))
                act.activation(dV[0:META, 0, :], A[1][0:META, P:2 * P], ACT.Copy)
                act.activation(dV[:, 1:5, :], A[1][:, 512:1024].rearrange("p (c n) -> p c n", n=P),
                               ACT.Copy).then_inc(d_v, 1)
                exps(3)
                next_head(0)
                copy_pT(4)
                exps(2)
                out_o(4)
                copy_pT(3)
                exps(1)
                out_o(3)
                copy_pT(2)
                exps(0)
                out_o(2)
                copy_pT(1)
                out_o(1)
                copy_pT(0)
                out_o(0)
                next_head(1)
                act.wait_ge(d_ot, val(turn(i, 1 + e, 2)))
                act.activation(BH[:, bass.ds(head, 1), META:T1], A[0][:, 0:SEQ].unsqueeze(1), ACT.Copy,
                               scale=small[:, 0:1])
                act.activation(BH[:, bass.ds(head, 1), 0:META], A[1][:, 0:META].unsqueeze(1), ACT.Copy,
                               scale=small[:, 0:1]).then_inc(d_hi, 1)
                next_head(2)

            act.wait_ge(rel_in, 16)
            for k in range(3):
                diff_project(Count(U_DIFF), k, 0)
            with act.Fori(0, DIFF_H // 2 - 1) as i:
                for e in range(2):
                    diff_head(i, e, True)
            for e in range(2):
                diff_head(DIFF_H // 2 - 1, e, e == 0)
            merge(1)

            with act.Fori(0, KC // 2) as i:
                for e in range(2):
                    u = Count(U_CONV + 3 * e, (i, 6))
                    for k, dst in enumerate((cb, cc)):
                        s = (u + k).slot
                        done(u + k)
                        act.activation(two(dst[:, :], T1 // 2), acc(G[s], G1), ACT.Copy).then_inc(evicted[s], 1)
                        split(u + k + 2)
                    split(u + 4)
                    act.wait_ge(c_y, val(Count(1 + e, (i, 2))))
                    act.activation(BH[:, bass.ds(i * 2 + e, 1), :], cy[:, :].unsqueeze(1), ACT.Copy).then_inc(c_hi, 1)
            merge(2)

            for n in range(KC):
                u = Count(U_OUT + n)
                split(u + 2)
                act.wait_ge(evicted[u.slot], val(u.turns() + 2))
                square(X[:, n, :], sqb, T1)
            root(rstd, G1, D)
            for c in range(KC):
                hi_part(HH[:, c, :], tmp[c % 2][:, :])

            with act.Fori(0, FF1 // D) as part:
                with act.Fori(0, 4) as i:
                    for e in range(2):
                        u = Count(U_FF + e, (part, 16), (i, 2))
                        done(u)
                        act.activation(two(sqb[0][:, :], T1 // 2), acc(G[u.slot], G1), ACT.Relu).then_inc(ff_r, 1)
                        split(u + 2)
                        act.wait_ge(evicted[u.slot], val(u.turns() + 2))
                        act.activation(BH[:, bass.ds(i * 2 + e, 1), :], sqb[1][:, :].unsqueeze(1),
                                       ACT.Copy).then_inc(ff_hi, 1)
                with act.Fori(0, 4) as i:
                    for e in range(2):
                        split(Count(U_FF + 10 + e, (part, 16), (i, 2)))
            for s in range(2):
                u = Count(U_FA - 2 + s)
                act.wait_ge(evicted[u.slot], val(u.turns() + 2))
            act.drain()
            for c in range(KC):
                square(X[:, c, :], sqb, T1)
            root(rstd, G1, D)

            def squares2(src, n0, ready):
                act.drain()
                act.wait_ge(ap_lo, nap[0])
                for c in range(KC):
                    ready(c)
                    square(src[:, c, n0:T2], tm2, T2 - n0)

            def modulate(i, shift, n0):
                for c in range(KC):
                    t = tm2[c % 2]
                    act.wait_ge(ap_tmp, nap[0] + 1)
                    for e, (a, b) in enumerate(((CTX, T2), (0, CTX))):
                        if a >= n0:
                            v = t[:, a:b]
                            act.activation(v, v, ACT.Identity, bias=ada[:, shift * KC + c, e:e + 1],
                                           scale=gain[i][:, c, e:e + 1])
                    act.drain()
                    hi_part(H2H[:, c, n0:T2], t[:, n0:T2])

            def both_chunks(c):
                act.wait_ge(x2_out, c + 1)
                act.wait_ge(ctx_out, c + 1)

            squares2(X2, 0, both_chunks)
            root(rs2, G2, D)
            modulate(0, 0, 0)

            def swiglu(base, geo, n0, f0, final):
                g0 = geo[0][0]

                def up(u, n):
                    done(u)
                    act.activation(like(tm2[0][:, n0:T2], geo), acc(G[u.slot], geo), ACT.Silu).then_inc(
                        evicted[u.slot], 1)
                    split(u + 2)
                    split(u + 3)
                    act.wait_ge(evicted[(u + 1).slot], val((u + 1).turns() + 2))
                    act.activation(UH2[:, bass.ds(n, 1), n0:T2], tm2[1][:, n0:T2].unsqueeze(1),
                                   ACT.Copy).then_inc(ff_hi, 1)

                act.wait_ge(ap_lo, nap[0])
                with act.Fori(0, 2) as part:
                    with act.Fori(0, 8) as n:
                        up(Count(base, (part, 24), (n, 2)), n)
                    with act.Fori(0, 4) as i:
                        for e in range(2):
                            split(Count(base + 18 + e, (part, 24), (i, 2)))
                with act.Fori(0, 6) as n:
                    up(Count(base + 48, (n, 2)), n)
                with act.Fori(0, 3 if final else 4) as i:
                    for e in range(2):
                        split(Count(base + 62 + e, (i, 2)))
                last_two = [Count(base + 66 + e) for e in range(2)]
                for u in last_two:
                    act.wait_ge(evicted[u.slot], val(u.turns() + 2))

            swiglu(U_FA, G2, 0, 32, False)
            squares2(Y2, 0, lambda c: None)
            root(rs2, G2, D)
            squares2(X2, 0, lambda c: act.wait_ge(x2_out, KC + c + 1))
            root(rs2, G2, D)
            modulate(1, 3, 0)

            with act.Fori(0, 2) as i:
                for p in range(2):
                    u = Count(U_NA + 3 * p, (i, 6))
                    for k, (dst, geo) in enumerate(((nq, GL), (nk, G2), (nvT, G2))):
                        s = (u + k).slot
                        done(u + k)
                        act.activation(like(dst[:, :], geo), acc(G[s], geo), ACT.Copy).then_inc(evicted[s], 1)
                        split(u + k + 2)
                    for s in range(8):
                        act.drain()
                        act.wait_ge(n_log, val(Count(s + 1 + 8 * p, (i, 16))))
                        b = s % 2
                        act.activation(nP[b][:, 0:256], nP[b][:, 0:256], ACT.Exp, bias=nst[:, b, 3:4], scale=0.125,
                                       accum_out=nst[:, b, 4:5])
                        act.activation(nP[b][:, 256:512], A[0][:, 512 * b + 256:512 * b + 512], ACT.Exp,
                                       bias=nst[:, b, 3:4], scale=0.125, accum_out=nst[:, b, 5:6]).then_inc(n_exp, 1)
            for c in range(4):
                act.wait_ge(n_ot, c + 1)
                act.activation(NA_OH[:, c, :], A[c % 2][:, 0:SEQ], ACT.Copy).then_inc(n_hi, 1)

            def lora_square(src, n):
                act.drain()
                square(src, tm2, n)

            for k in range(2):
                u = Count(U_LORA + k)
                done(u)
                act.activation(two(ckvT[:, k, :], T2 // 2), acc(G[u.slot], G2), ACT.Copy).then_inc(evicted[u.slot], 1)
                split(u + 2)
            for k in range(2):
                lora_square(ckvT[:, k, :], T2)
            u = Count(U_LORA + 2)
            done(u)
            act.activation(two(mkr[:, :], T2 // 2)[0:QK], acc(G[u.slot], G2, QK), ACT.Copy).then_inc(evicted[u.slot], 1)
            act.drain().then_inc(k_kr, 1)
            split(u + 2)
            root(rs2, G2, KVR)
            for k in range(2):
                hi_part(CKH[:, k, :], tm2[k % 2][:, :])
            for k in range(6):
                u = Count(U_LORA + 3 + k)
                done(u)
                act.activation(cqT[:, k, :], acc(G[u.slot], GS), ACT.Copy).then_inc(evicted[u.slot], 1)
                split(u + 2)
            act.wait_ge(ap_lo, nap[0])
            for k in range(6):
                lora_square(cqT[:, k, :], SEQ)
            root(rs2, GS, QR)
            for k in range(6):
                hi_part(CQH[:, k, :], tm2[k % 2][:, 0:SEQ])

            def mla_q(u, e):
                done(u)
                act.activation(mqs[e][0:QK, :], acc(G[u.slot], GS, QK), ACT.Copy).then_inc(evicted[u.slot], 1)
                split(u + 2)

            def mla_kv(u, e):
                done(u)
                s = u.slot
                act.activation(two(mks[e][:, :], T2 // 2)[0:NOPE], acc(G[s], G2, NOPE), ACT.Copy)
                act.activation(two(mvT[:, :], T2 // 2)[NOPE:P], acc(G[s], G2, P, NOPE), ACT.Copy).then_inc(evicted[s], 1)
                split(u + 2)

            def mla_head(i, e, more):
                u = turn(i, U_MLA + 2 * e, 4)

                def exps(t):
                    b = t % 2
                    act.drain()
                    act.wait_ge(k_log, val(turn(i, t + 1 + NT * e, 2 * NT)))
                    act.activation(mP[b][:, :], A[0][:, 0:T2], ACT.Exp, bias=mst[:, b, 1:2], scale=QK ** -0.5,
                                   accum_out=mst[:, b, 2:3]).then_inc(k_exp, 1)

                exps(0)
                for t in range(NT):
                    if t < NT - 1:
                        exps(t + 1)
                    act.wait_ge(k_tr, val(turn(i, t + 1 + NT * e, 2 * NT)))
                    act.activation(mT[t % 2][:, 0:4, :], A[1][:, 0:512].rearrange("p (c n) -> p c n", n=P),
                                   ACT.Copy).then_inc(k_at, 1)
                    if more and t == 2:
                        mla_q(u + 2, 1 - e)
                if more:
                    mla_kv(u + 3, 1 - e)

            mla_q(Count(U_MLA), 0)
            mla_kv(Count(U_MLA + 1), 0)
            with act.Fori(0, 3) as i:
                for e in range(2):
                    mla_head(i, e, True)
            for e in range(2):
                mla_head(3, e, e == 0)
            for c in range(4):
                act.wait_ge(k_ot, c + 1)
                act.activation(ML_OH[:, c, :], A[c % 2][:, 0:SEQ], ACT.Copy).then_inc(k_hi, 1)

            with act.Fori(0, KC) as n:
                u = Count(U_GATE, (n, 4))
                for k in range(2):
                    v = u + 2 * k
                    done(v)
                    act.activation(sgl[k][:, :], acc(G[v.slot], GS), ACT.Sigmoid,
                                   bias=col_b[:, bass.ds(n + (48 + KC * k), 1)]).then_inc(evicted[v.slot], 1)
                    split(v + 2)
                    split(v + 3)
                act.wait_ge(mg_add, val(Count(KC + 1, (n, 1))))
                act.activation(MH2[:, bass.ds(n, 1), :], tm2[0][:, 0:SEQ].unsqueeze(1), ACT.Copy).then_inc(mg_hi, 1)
            with act.Fori(0, 4) as i:
                for e in range(2):
                    u = Count(U_OUT2 + e, (i, 2))
                    done(u)
                    act.activation(Y2[:, bass.ds(i * 2 + e, 1), CTX:T2], acc(G[u.slot], GS).unsqueeze(1),
                                   ACT.Copy).then_inc(evicted[u.slot], 1)
                    split(u + 2)
            act.drain()
            squares2(Y2, CTX, lambda c: None)
            root(rs2, GL, D)
            squares2(X2, CTX, lambda c: act.wait_ge(x2_out, 2 * KC + c + 1))
            root(rs2, GL, D)
            modulate(2, 6, CTX)
            swiglu(U_FB, GL, CTX, 54, True)
            squares2(Y2, CTX, lambda c: None)
            root(rs2, GL, D)

        @block.gpsimd
        def _(pool):
            pool.wait_ge(const_in, 16)
            with pool.Fori(0, RET_H) as h:
                pool.wait_ge(r_var, val(Count(1, (h, 1))))
                pool.tensor_tensor(rpow[:, :], rvar[:, :], minus_half[:, 0:5], ALU.pow).then_inc(r_pow, 1)
            with pool.Fori(0, DIFF_H) as h:
                pool.wait_ge(d_ss, val(Count(1, (h, 1))))
                pool.tensor_tensor(dpow[:, :], dss2[:, :], minus_half[:, 0:5], ALU.pow).then_inc(d_pow, 1)
            pool.wait_ge(x2_out, KC)
            pool.memset(rpbT[:, :, :], 0.0).then_inc(rpb_zero, 1)
            pool.memset(Y2[:, :, :], 0.0).then_inc(y_zero, 1)
            pool.wait_ge(n_tab, 1)
            for e in range(2):
                pool.tensor_copy(nBs[e][:, :, :], nB[:, :, e, :]).then_inc(n_bias, 1)
            with pool.Fori(0, NA_H // 2 - 1) as p:
                for e in range(2):
                    pool.wait_ge(n_log, val(Count(4 * e + 4, (p, 8))))
                    pool.tensor_copy(nBs[e][:, :, :], nB[:, :, bass.ds(p * 2 + (2 + e), 1), :].rearrange(
                        "p k a n -> p k (a n)")).then_inc(n_bias, 1)
            pool.wait_ge(x2_out, 3 * KC)
            pool.memset(Y2[:, :, CTX:T2], 0.0).then_inc(y_zero, 1)

        @block.vector
        def _(dve):
            def split(v):
                dve.wait_ge(hi_split, val(v + 1))
                s = v.slot
                dve.tensor_tensor(wl[s][:, :, :], raw[s][:, :, :], wh[s][:, :, :].bitcast(F32),
                                  ALU.subtract).then_inc(lo_split, 1)

            def done(u):
                dve.drain()
                dve.wait_ge(unit_done, val(u + 1))

            nsq, nroot, nap = [0], [0], [0]

            def add_square(dst, buf, n, first):
                b = buf[nsq[0] % 2][:, 0:n]
                nsq[0] += 1
                dve.drain()
                dve.wait_ge(nrm_sq, nsq[0])
                if first:
                    dve.tensor_copy(dst, b).then_inc(nrm_add, 1)
                else:
                    dve.tensor_tensor(dst, dst, b, ALU.add).then_inc(nrm_add, 1)

            def recip(dst):
                nroot[0] += 1
                dve.drain()
                dve.wait_ge(nrm_root, nroot[0])
                dve.reciprocal(dst, dst)
                dve.drain()

            def scaled(chunks, bufs, hi, lo, scale):
                n0 = nap[0]

                def low(c):
                    dve.wait_ge(ap_hi, n0 + c + 1)
                    dve.tensor_tensor(lo(c), bufs(c), hi(c).bitcast(F32), ALU.subtract).then_inc(ap_lo, 1)

                for c in range(chunks):
                    if c >= 2:
                        dve.drain()
                    scale(c, bufs(c)).then_inc(ap_tmp, 1)
                    if c >= 1:
                        low(c - 1)
                low(chunks - 1)
                nap[0] += chunks
                dve.drain()

            dve.memset(bag[:, :, :], 1.0)
            dve.wait_ge(cols_done, 1)
            dve.tensor_copy(col_a[:, :], A[0][:, 0:65])
            dve.tensor_copy(col_b[:, :], A[0][:, 128:200])
            dve.tensor_copy(col_c[:, :], A[0][:, 256:328]).then_inc(cols_out, 1)
            dve.wait_ge(lam_in, 16)
            dve.tensor_tensor(lam_p[:, :, :], lam_v[:, 0:4:2, :], lam_v[:, 1:4:2, :], ALU.mult)
            dve.drain()
            dve.tensor_reduce(small[:, 2:4], lam_p[:, :, :], AX, ALU.add).then_inc(lam_dve, 1)
            dve.tensor_scalar(small[:, 0:1], col_a[:, 48:49], 1.0 - LAM_INIT, None, ALU.mult)
            dve.wait_ge(lam_act, 1)
            dve.scalar_tensor_tensor(out=small[:, 1:2], in0=small[:, 4:5], scalar=LAM_INIT, in1=small[:, 5:6],
                                     op0=ALU.add, op1=ALU.subtract)
            for v in range(2):
                split(Count(v))
            for c in range(KC):
                dve.wait_ge(xT_done, c + 1)
                dve.tensor_copy(X[:, c, META:T1], A[c % 2][:, 0:SEQ])
                dve.tensor_copy(X[:, c, 0:META], A[c % 2][:, SEQ:T1]).then_inc(xT_out, 1)
                if c >= 1:
                    add_square(ssq[:, :], sqb, T1, c == 1)
            add_square(ssq[:, :], sqb, T1, False)
            recip(rstd[:, :])

            def weighted(col):
                return lambda c, b: dve.scalar_tensor_tensor(out=b, in0=X[:, c, :], scalar=col_a[:, col + c:col + c + 1],
                                                             in1=rstd[:, :], op0=ALU.mult, op1=ALU.mult)

            scaled(KC, lambda c: tmp[c % 2][:, :], lambda c: HH[:, c, :], lambda c: HL[:, c, :], weighted(0))

            dve.wait_ge(decay_in, 16)
            with dve.Fori(0, RET_H) as h:
                u = Count(U_RET, (h, 6))
                split(u + 2)
                split(u + 3)
                for c, (q0, n) in enumerate(TILES):
                    dve.wait_ge(r_sc, val(Count(c + 1, (h, 5))))
                    w = ST_W[c]
                    dve.tensor_tensor(rST[0:n, ST_AT[c]:ST_AT[c] + w], A[c % 2][0:n, 0:w],
                                      DT[0:n, bass.ds(h, 1), 0:w].rearrange("p a n -> p (a n)"),
                                      ALU.mult).then_inc(r_st, 1)
                split(u + 4)
                split(u + 5)
                dve.drain()
                dve.wait_ge(r_pv, val(Count(1, (h, 1))))

                def head_psum(t, n):
                    return A[1][0:n, 0:RET_DV] if t == 0 else A[0][:, (t - 1) * RET_DV:t * RET_DV]

                for t, (q0, n) in enumerate(TILES):
                    dve.bn_stats(bst[0:n, t, :], head_psum(t, n))
                dve.drain()
                for t, (q0, n) in enumerate(TILES):
                    dve.bn_aggr(bag[0:n, t, :], bst[0:n, t, :])
                dve.drain()
                dve.tensor_scalar(rvar[:, :], bag[:, :, 1], EPS, None, ALU.add).then_inc(r_var, 1)
                split(u + 6)
                dve.wait_ge(r_pow, val(Count(1, (h, 1))))
                for t, (q0, n) in enumerate(TILES):
                    last = dve.tensor_scalar(rY[0:n, t, :], head_psum(t, n), bag[0:n, t, 0:1], rpow[0:n, t:t + 1],
                                             ALU.subtract, ALU.mult)
                last.then_inc(r_y, 1)
                split(u + 7)
                dve.drain()
                dve.wait_ge(r_yt, val(Count(1, (h, 1))))
                for half in range(2):
                    dve.tensor_tensor(tmp[half][:, META:T1], A[half][:, 0:SEQ], rg[half][:, META:T1], ALU.mult)
                    dve.tensor_tensor(tmp[half][:, 0:META], A[half][:, SEQ:T1], rg[half][:, 0:META],
                                      ALU.mult).then_inc(r_tmp, 1)
                dve.drain()
                for half in range(2):
                    dve.wait_ge(r_hi, val(Count(half + 1, (h, 2))))
                    dve.tensor_tensor(BL[:, bass.ds(h * 2 + half, 1), :], tmp[half][:, :].unsqueeze(1),
                                      BH[:, bass.ds(h * 2 + half, 1), :].bitcast(F32), ALU.subtract).then_inc(br_lo, 1)
                dve.drain()

            def merge(r):
                with dve.Fori(0, KC) as n:
                    u = Count(U_BR[r], (n, 2))
                    split(u + 2)
                    done(u + 1)
                    s = (u + 1).slot
                    g = two(sg[0][:, :], T1 // 2)
                    mg = MG[:, bass.ds(n, 1), :]
                    if r == 0:
                        dve.tensor_tensor(mg.rearrange("p a (s n) -> p (a s) n", s=2), acc(G[s], G1), g,
                                          ALU.mult).then_inc(evicted[s], 1)
                    else:
                        dve.tensor_tensor(two(tmp[0][:, :], T1 // 2), acc(G[s], G1), g, ALU.mult).then_inc(evicted[s], 1)
                        dve.drain()
                        last = dve.tensor_tensor(mg, mg, tmp[0][:, :].unsqueeze(1), ALU.add)
                        if r == 2:
                            last.then_inc(mg_add, 1)
                    split(u + 3)
                    if r == 2:
                        dve.drain()
                        dve.wait_ge(mg_hi, val(Count(1, (n, 1))))
                        dve.tensor_tensor(ML[:, bass.ds(n, 1), :], mg, MH[:, bass.ds(n, 1), :].bitcast(F32),
                                          ALU.subtract).then_inc(m_lo, 1)

            merge(0)

            def diff_head(i, e, more):
                u = turn(i, U_DIFF + 3 * e, 6)

                def cnt(k):
                    return turn(i, k + 5 * e, 10)

                def logits(t):
                    q0, n = TILES[t]
                    w, b = q0 + n, t % 2
                    r0 = T1 - P - q0
                    w1 = min(w, 512)
                    dve.drain()
                    if t == 4:
                        dve.wait_ge(d_bias, val(turn(i, 1 + e, 2)))
                    dve.wait_ge(d_qk, val(cnt(5 - t)))
                    alone(dve, dve_passed)
                    for m in range(2):
                        dve.tensor_tensor_reduce(dL[b][m][0:n, 0:w1], A[0][0:n, 512 * m:512 * m + w1],
                                                 dR[0:n, r0:r0 + w1], 1.0, 3 * NEG * 1e7, ALU.add, ALU.max,
                                                 dmax[0:n, 0, m:m + 1])
                    if w > 512:
                        dve.drain()
                        for m in range(2):
                            dve.tensor_tensor_reduce(dL[b][m][0:n, 512:w], A[1][0:n, 512 * m:512 * m + w - 512],
                                                     dR[0:n, r0 + 512:r0 + w], 1.0, dmax[0:n, 0, m:m + 1],
                                                     ALU.add, ALU.max, dmax[0:n, 1, m:m + 1])
                    dve.drain()
                    dve.tensor_scalar(dnb[0:n, b, :], dmax[0:n, 1 if w > 512 else 0, :], -0.125, None,
                                      ALU.mult).then_inc(d_log, 1)

                def combine(t):
                    q0, n = TILES[t]
                    w, b = q0 + n, t % 2
                    dve.drain()
                    dve.wait_ge(d_exp, val(cnt(5 - t)))
                    dve.reciprocal(drc[0:n, b, :], dsum[0:n, b, :])
                    dve.drain()
                    dve.tensor_scalar(dlr[0:n, b, :], drc[0:n, b, 1:2], small[0:n, 1:2], None, ALU.mult)
                    dve.drain()
                    p0, p1 = dL[b][0][0:n, 0:w], dL[b][1][0:n, 0:w]
                    dve.tensor_scalar(p1, p1, dlr[0:n, b, 0:1], None, ALU.mult)
                    dve.drain()
                    dve.scalar_tensor_tensor(out=p0, in0=p0, scalar=drc[0:n, b, 0:1], in1=p1, op0=ALU.mult,
                                             op1=ALU.subtract).then_inc(d_att, 1)

                head = i * 2 + e
                for t in (4, 3, 2, 1, 0):
                    logits(t)
                    combine(t)
                    if more and t == 3:
                        split(u + 5)
                dve.drain()
                dve.wait_ge(d_o, val(cnt(5)))
                dve.tensor_scalar(dss2[:, :], dss[:, :], 1.0 / P, EPS, ALU.mult, ALU.add).then_inc(d_ss, 1)
                dve.wait_ge(d_pow, val(turn(i, 1 + e, 2)))
                dve.tensor_tensor(dOn[:, :, :], dO[:, :, :], dpow[:, :].unsqueeze(2).to_broadcast([P, 5, P]),
                                  ALU.mult).then_inc(d_on, 1)
                if more:
                    split(u + 6)
                dve.wait_ge(d_hi, val(turn(i, 1 + e, 2)))
                c = bass.ds(head, 1)
                dve.scalar_tensor_tensor(out=BL[:, c, META:T1], in0=A[0][:, 0:SEQ].unsqueeze(1), scalar=small[:, 0:1],
                                         in1=BH[:, c, META:T1].bitcast(F32), op0=ALU.mult, op1=ALU.subtract)
                dve.scalar_tensor_tensor(out=BL[:, c, 0:META], in0=A[1][:, 0:META].unsqueeze(1), scalar=small[:, 0:1],
                                         in1=BH[:, c, 0:META].bitcast(F32), op0=ALU.mult,
                                         op1=ALU.subtract).then_inc(br_lo, 1)
                if more:
                    split(u + 7)

            dve.drain()
            dve.memset(dO[:, :, :], 0.0)
            dve.memset(dss[:, :], 1.0)
            for k in range(3):
                split(Count(U_DIFF + 2 + k))
            with dve.Fori(0, DIFF_H // 2 - 1) as i:
                for e in range(2):
                    diff_head(i, e, True)
            for e in range(2):
                diff_head(DIFF_H // 2 - 1, e, e == 0)
            merge(1)

            with dve.Fori(0, KC // 2) as i:
                for e in range(2):
                    u = Count(U_CONV + 3 * e, (i, 6))
                    split(u + 2)
                    split(u + 3)
                    done(u + 2)
                    s = (u + 2).slot
                    dve.tensor_tensor(two(cu[:, :], T1 // 2), acc(G[s], G1), two(cc[:, :], T1 // 2),
                                      ALU.mult).then_inc(evicted[s], 1)
                    dve.drain()

                    def tap(k):
                        return col_a[:, bass.ds(i * 2 + (24 + KC * k + e), 1)]

                    dve.tensor_scalar(cy[:, :], cu[:, :], tap(2), None, ALU.mult)
                    for k in (1, 0):
                        dve.drain()
                        d = 2 - k
                        dve.scalar_tensor_tensor(out=cy[:, d:T1], in0=cu[:, 0:T1 - d], scalar=tap(k), in1=cy[:, d:T1],
                                                 op0=ALU.mult, op1=ALU.add)
                    dve.drain()
                    dve.tensor_tensor(cy[:, :], cy[:, :], cb[:, :], ALU.mult).then_inc(c_y, 1)
                    split(u + 4)
                    dve.drain()
                    dve.wait_ge(c_hi, val(Count(1 + e, (i, 2))))
                    c = bass.ds(i * 2 + e, 1)
                    dve.tensor_tensor(BL[:, c, :], cy[:, :].unsqueeze(1), BH[:, c, :].bitcast(F32),
                                      ALU.subtract).then_inc(br_lo, 1)
            merge(2)

            for n in range(KC):
                u = Count(U_OUT + n)
                done(u)
                x = two(X[:, n, :], T1 // 2)
                dve.tensor_tensor(x, acc(G[u.slot], G1), x, ALU.add).then_inc(evicted[u.slot], 1)
                split(u + 2)
                if n >= 1:
                    add_square(ssq[:, :], sqb, T1, n == 1)
            add_square(ssq[:, :], sqb, T1, False)
            recip(rstd[:, :])
            scaled(KC, lambda c: tmp[c % 2][:, :], lambda c: HH[:, c, :], lambda c: HL[:, c, :], weighted(8))

            with dve.Fori(0, FF1 // D) as part:
                with dve.Fori(0, 4) as i:
                    for e in range(2):
                        u = Count(U_FF + e, (part, 16), (i, 2))
                        dve.drain()
                        dve.wait_ge(ff_r, val(Count(1 + e, (part, 8), (i, 2))))
                        dve.scalar_tensor_tensor(out=two(sqb[1][:, :], T1 // 2), in0=acc(G[u.slot], G1), scalar=0.0,
                                                 in1=two(sqb[0][:, :], T1 // 2), op0=ALU.max,
                                                 op1=ALU.mult).then_inc(evicted[u.slot], 1)
                        split(u + 2)
                        dve.drain()
                        dve.wait_ge(ff_hi, val(Count(1 + e, (part, 8), (i, 2))))
                        c = bass.ds(i * 2 + e, 1)
                        dve.tensor_tensor(BL[:, c, :], sqb[1][:, :].unsqueeze(1), BH[:, c, :].bitcast(F32),
                                          ALU.subtract).then_inc(ff_lo, 1)
                with dve.Fori(0, 4) as i:
                    for e in range(2):
                        u = Count(U_FF + 8 + e, (part, 16), (i, 2))
                        done(u)
                        x = X[:, bass.ds(i * 2 + e, 1), :].rearrange("p a (s n) -> p (a s) n", s=2)
                        dve.tensor_tensor(x, acc(G[u.slot], G1), x, ALU.add).then_inc(evicted[u.slot], 1)
                        split(u + 2)
            dve.wait_ge(ada_used, 72)
            for e in range(2):
                dve.tensor_tensor(ada[:, :, e], A[1][:, 512:656].rearrange("p (n e) -> p n e", e=2)[:, :, e],
                                  col_c[:, :], ALU.add)
            dve.drain()

            def mod(j, e):
                return ada[:, KC * j:KC * j + KC, e]

            for i, (g, sc) in enumerate(((0, 1), (2, 4), (4, 7))):
                for e in range(2):
                    dve.scalar_tensor_tensor(out=gain[i][:, :, e], in0=mod(sc, e), scalar=1.0,
                                             in1=col_b[:, KC * g:KC * g + KC], op0=ALU.add, op1=ALU.mult)
            for i, (g, gt, weight) in enumerate(((1, 2, 0.5), (3, 5, 1.0), (5, 8, 0.5))):
                for e in range(2):
                    dve.scalar_tensor_tensor(out=resg[i][:, :, e], in0=mod(gt, e), scalar=weight,
                                             in1=col_b[:, KC * g:KC * g + KC], op0=ALU.mult, op1=ALU.mult)
            for c in range(KC):
                add_square(ssq[:, :], sqb, T1, c == 0)
            recip(rstd[:, :])

            def by_column(ap):
                return ap.rearrange("p (r c) -> p c r", r=GRID_H)

            for c in range(KC):
                dve.scalar_tensor_tensor(out=X2[:, c, CTX:T2].rearrange("p (c r) -> p c r", r=GRID_H),
                                         in0=by_column(X[:, c, META:T1]), scalar=col_a[:, 16 + c:17 + c],
                                         in1=by_column(rstd[:, META:T1]), op0=ALU.mult,
                                         op1=ALU.mult).then_inc(x2_out, 1)
            for c in range(KC):
                dve.wait_ge(ctx_done, c + 1)
                dve.tensor_copy(X2[:, c, 0:CTX], A[c % 2][:, 0:CTX]).then_inc(ctx_out, 1)

            def sums2(n0):
                for c in range(KC):
                    add_square(ss2[:, n0:T2], tm2, T2 - n0, c == 0)
                recip(rs2[:, n0:T2])

            def normed(n0):
                scaled(KC, lambda c: tm2[c % 2][:, n0:T2], lambda c: H2H[:, c, n0:T2], lambda c: H2L[:, c, n0:T2],
                       lambda c, b: dve.tensor_tensor(b, X2[:, c, n0:T2], rs2[:, n0:T2], ALU.mult))

            def residual(i, n0):
                for c in range(KC):
                    for e, (a, b) in enumerate(((CTX, T2), (0, CTX))):
                        if a >= n0:
                            dve.scalar_tensor_tensor(out=Y2[:, c, a:b], in0=Y2[:, c, a:b], scalar=resg[i][:, c, e:e + 1],
                                                     in1=rs2[:, a:b], op0=ALU.mult, op1=ALU.mult)
                    dve.drain()
                    x = X2[:, c, n0:T2]
                    dve.tensor_tensor(x, x, Y2[:, c, n0:T2], ALU.add).then_inc(x2_out, 1)

            sums2(0)
            normed(0)

            def swiglu(base, geo, n0, f0, final, shift):
                def up(u, n, fcount):
                    split(u + 2)
                    done(u + 1)
                    s = (u + 1).slot
                    dve.wait_ge(evicted[u.slot], val(u.turns() + 2))
                    dve.tensor_tensor(like(tm2[1][:, n0:T2], geo), acc(G[s], geo), like(tm2[0][:, n0:T2], geo),
                                      ALU.mult).then_inc(evicted[s], 1)
                    split(u + 3)
                    dve.drain()
                    dve.wait_ge(ff_hi, val(fcount + 1))
                    c = bass.ds(n, 1)
                    dve.tensor_tensor(UL2[:, c, n0:T2], tm2[1][:, n0:T2].unsqueeze(1), UH2[:, c, n0:T2].bitcast(F32),
                                      ALU.subtract).then_inc(ff_lo, 1)

                def down(u, n, last):
                    done(u)
                    m = len(geo)
                    y = Y2[:, bass.ds(n, 1), n0:T2]
                    y = y.rearrange("p a (s n) -> p (a s) n", s=m)
                    p = acc(G[u.slot], geo) if m == 2 else acc(G[u.slot], geo).unsqueeze(1)
                    dve.tensor_tensor(y, p, y, ALU.add).then_inc(evicted[u.slot], 1)
                    if not last:
                        split(u + 2)

                with dve.Fori(0, 2) as part:
                    with dve.Fori(0, 8) as n:
                        up(Count(base, (part, 24), (n, 2)), n, Count(f0, (part, 8), (n, 1)))
                        if shift:
                            b = part * 8 + n
                            t = rpbT[:, :, bass.ds(b + 1, 31)]
                            dve.scalar_tensor_tensor(out=t, in0=rpbG[:, :, :], scalar=cst("onehot8")[:, bass.ds(b, 1)],
                                                     in1=t, op0=ALU.mult, op1=ALU.add)
                    with dve.Fori(0, 4) as i:
                        for e in range(2):
                            down(Count(base + 16 + e, (part, 24), (i, 2)), i * 2 + e, False)
                with dve.Fori(0, 6) as n:
                    up(Count(base + 48, (n, 2)), n, Count(f0 + 16, (n, 1)))
                with dve.Fori(0, 3 if final else 4) as i:
                    for e in range(2):
                        down(Count(base + 60 + e, (i, 2)), i * 2 + e, False)
                if final:
                    for e in range(2):
                        down(Count(base + 66 + e), 6 + e, True)
                dve.drain()

            dve.wait_ge(rpb_zero, 1)
            dve.wait_ge(rpb_in, 16 * GRID_H)
            dve.wait_ge(y_zero, 1)
            swiglu(U_FA, G2, 0, 32, False, True)
            sums2(0)
            residual(0, 0)
            sums2(0)
            normed(0)

            for kind, off in enumerate((16, 8, 0)):
                dve.tensor_tensor(
                    nB[:, kind, :, :].rearrange("p h (a r) -> p h a r", r=GRID_H),
                    rpbT[:, :, off:off + 32].rearrange("p (h r) a -> p h a r", r=GRID_H),
                    cst("window")[:, 32 * kind:32 * kind + 32].unsqueeze(1).unsqueeze(3).to_broadcast(
                        [P, NA_H, 32, GRID_H]), ALU.add)
            dve.drain()
            dve.memset(nst[:, :, :], 0.0).then_inc(n_tab, 1)
            dve.drain()
            with dve.Fori(0, 2) as i:
                for p in range(2):
                    u = Count(U_NA + 3 * p, (i, 6))
                    for k in range(3):
                        split(u + k + 2)
                    for half in range(2):
                        dve.drain()
                        dve.wait_ge(n_vt, val(Count(half + 1 + 2 * p, (i, 4))))
                        if half == 0:
                            dve.tensor_copy(nV[:, 0:4, :], A[1][:, 0:512].rearrange("p (c n) -> p c n", n=P))
                            dve.tensor_copy(nV[:, 4, :], A[0][:, 0:P]).then_inc(n_v, 1)
                        else:
                            dve.tensor_copy(nV[:, 5:9, :], A[1][:, 0:512].rearrange("p (c n) -> p c n", n=P)).then_inc(
                                n_v, 1)

                    def cnt(k):
                        return Count(k + 8 * p, (i, 16))

                    def logits(s):
                        e, t = divmod(s, NT)
                        b = s % 2
                        kind = (0, 1, 1, 2)[t]
                        dve.drain()
                        if t == 0:
                            dve.wait_ge(n_bias, val(Count(2 * p + e + 1, (i, 4))))
                        dve.wait_ge(n_qk, val(cnt(s + 1)))
                        alone(dve, dve_passed)
                        dve.tensor_tensor_reduce(nP[b][:, 0:256], A[0][:, 512 * b:512 * b + 256],
                                                 nBs[e][:, kind, :],
                                                 1.0, 3 * NEG * 1e7, ALU.add, ALU.max, nst[:, b, 0:1])
                        dve.tensor_reduce(nst[:, b, 1:2], A[0][:, 512 * b + 256:512 * b + 512], AX, ALU.max)
                        dve.drain()
                        dve.tensor_tensor(nst[:, b, 2:3], nst[:, b, 0:1], nst[:, b, 1:2], ALU.max)
                        dve.drain()
                        dve.tensor_scalar(nst[:, b, 3:4], nst[:, b, 2:3], -0.125, None, ALU.mult).then_inc(n_log, 1)

                    def copy_pT(s):
                        b = s % 2
                        dve.wait_ge(n_tr, val(cnt(s + 1)))
                        dve.tensor_copy(nT[b][:, :, :], A[1][:, 0:512].rearrange("p (c n) -> p c n", n=P)).then_inc(
                            n_at, 1)
                        dve.tensor_tensor(nst[:, b, 6:7], nst[:, b, 4:5], nst[:, b, 5:6], ALU.add)
                        dve.drain()
                        dve.reciprocal(nst[:, b, 7:8], nst[:, b, 6:7])
                        dve.drain()

                    def out_o(s):
                        e, t = divmod(s, NT)
                        dve.wait_ge(n_pv, val(cnt(s + 1)))
                        dve.tensor_scalar(nO[:, t, bass.ds(i * 256 + (2 * p + e) * NA_HD, NA_HD)],
                                          A[1][:, 512:512 + NA_HD], nst[:, s % 2, 7:8], None, ALU.mult).then_inc(n_o, 1)

                    logits(0)
                    logits(1)
                    for s in range(8):
                        copy_pT(s)
                        if s:
                            out_o(s - 1)
                        if s < 6:
                            logits(s + 2)
                    out_o(7)
                    dve.drain()
            for c in range(4):
                dve.wait_ge(n_hi, c + 1)
                dve.tensor_tensor(NA_OL[:, c, :], A[c % 2][:, 0:SEQ], NA_OH[:, c, :].bitcast(F32),
                                  ALU.subtract).then_inc(n_lo, 1)

            for k in range(2):
                split(Count(U_LORA + k + 2))
            for k in range(2):
                add_square(ss2[:, :], tm2, T2, k == 0)
            split(Count(U_LORA + 4))
            recip(rs2[:, :])
            scaled(2, lambda c: tm2[c % 2][:, :], lambda c: CKH[:, c, :], lambda c: CKL[:, c, :],
                   lambda c, b: dve.scalar_tensor_tensor(out=b, in0=ckvT[:, c, :], scalar=col_b[:, 70 + c:71 + c],
                                                         in1=rs2[:, :], op0=ALU.mult, op1=ALU.mult))
            for k in range(6):
                split(Count(U_LORA + 5 + k))
            dve.wait_ge(rope_in, 16)
            R = slice(NOPE, QK)

            def rotate(x, n):
                dve.drain()
                dve.wait_ge(k_rot, val(n))
                dve.tensor_tensor(mqr[R, :], A[1][R, 0:SEQ], rope[R, 1, :], ALU.mult)
                dve.tensor_tensor(x, x, rope[R, 0, :], ALU.mult)
                dve.drain()
                return dve.tensor_tensor(x, x, mqr[R, :], ALU.add)

            rotate(mkr[R, CTX:T2], 1)
            dve.drain()
            dve.tensor_copy(mks[0][R, :], mkr[R, :])
            for k in range(6):
                add_square(ss2[:, 0:SEQ], tm2, SEQ, k == 0)
            recip(rs2[:, 0:SEQ])
            scaled(6, lambda c: tm2[c % 2][:, 0:SEQ], lambda c: CQH[:, c, :], lambda c: CQL[:, c, :],
                   lambda c, b: dve.scalar_tensor_tensor(out=b, in0=cqT[:, c, :], scalar=col_b[:, 64 + c:65 + c],
                                                         in1=rs2[:, 0:SEQ], op0=ALU.mult, op1=ALU.mult))

            dve.tensor_copy(mks[1][R, :], mkr[R, :])

            def mla_ready(i, e, parity):
                rotate(mqs[parity][R, :], turn(i, 2 + e, 2)).then_inc(k_q, 1)
                dve.wait_ge(k_vt, val(turn(i, 1 + e, 2)))
                dve.tensor_copy(mV[:, :, :], A[1][:, 512:896].rearrange("p (c n) -> p c n", n=VD)).then_inc(k_v, 1)

            def mla_head(i, e, more):
                u = turn(i, U_MLA + 2 * e, 4)

                def cnt(t):
                    return turn(i, t + 1 + NT * e, 2 * NT)

                def row_max(t):
                    b = t % 2
                    dve.drain()
                    dve.wait_ge(k_qk, val(cnt(t)))
                    dve.tensor_reduce(mst[:, b, 0:1], A[0][:, 0:T2], AX, ALU.max)
                    dve.drain()
                    dve.tensor_scalar(mst[:, b, 1:2], mst[:, b, 0:1], -(QK ** -0.5), None, ALU.mult).then_inc(k_log, 1)

                def copy_pT(t):
                    dve.wait_ge(k_tr1, val(cnt(t)))
                    dve.tensor_copy(mT[t % 2][:, 4:6, :], A[1][:, 512:768].rearrange("p (c n) -> p c n", n=P)).then_inc(
                        k_ad, 1)
                    dve.reciprocal(mst[:, t % 2, 3:4], mst[:, t % 2, 2:3])
                    dve.drain()

                def out_o(t):
                    dve.wait_ge(k_pv, val(cnt(t)))
                    at_ = i * 128 + VD * e
                    dve.tensor_scalar(mO[:, t, bass.ds(at_, VD)], A[1][:, 768:768 + VD], mst[:, t % 2, 3:4], None,
                                      ALU.mult).then_inc(k_o, 1)

                row_max(0)
                for t in range(NT):
                    if t < NT - 1:
                        row_max(t + 1)
                    copy_pT(t)
                    if t:
                        out_o(t - 1)
                    if more and t == 2:
                        split(u + 4)
                out_o(NT - 1)
                dve.drain()
                if more:
                    mla_ready(i, 1 + e, 1 - e)
                    split(u + 5)

            for k in range(2):
                split(Count(U_MLA + 2 + k))
            mla_ready(0, 0, 0)
            with dve.Fori(0, 3) as i:
                for e in range(2):
                    mla_head(i, e, True)
            for e in range(2):
                mla_head(3, e, e == 0)
            for c in range(4):
                dve.wait_ge(k_hi, c + 1)
                dve.tensor_tensor(ML_OL[:, c, :], A[c % 2][:, 0:SEQ], ML_OH[:, c, :].bitcast(F32),
                                  ALU.subtract).then_inc(k_lo, 1)

            with dve.Fori(0, KC) as n:
                u = Count(U_GATE, (n, 4))
                for k in range(2):
                    v = u + (2 * k)
                    split(v + 2)
                    done(v + 1)
                    s = (v + 1).slot
                    dve.wait_ge(evicted[v.slot], val(v.turns() + 2))
                    dve.tensor_tensor(tm2[k][:, 0:SEQ], acc(G[s], GS), sgl[k][:, :], ALU.mult).then_inc(evicted[s], 1)
                    if k == 0:
                        split(v + 3)
                dve.drain()
                dve.tensor_tensor(tm2[0][:, 0:SEQ], tm2[0][:, 0:SEQ], tm2[1][:, 0:SEQ], ALU.add).then_inc(mg_add, 1)
                split(u + 5)
                dve.drain()
                dve.wait_ge(mg_hi, val(Count(KC + 1, (n, 1))))
                c = bass.ds(n, 1)
                dve.tensor_tensor(ML2[:, c, :], tm2[0][:, 0:SEQ].unsqueeze(1), MH2[:, c, :].bitcast(F32),
                                  ALU.subtract).then_inc(m_lo, 1)
            with dve.Fori(0, 4) as i:
                for e in range(2):
                    split(Count(U_OUT2 + 2 + e, (i, 2)))
            sums2(CTX)
            residual(1, CTX)
            sums2(CTX)
            normed(CTX)
            dve.wait_ge(y_zero, 2)
            swiglu(U_FB, GL, CTX, 54, True, False)
            sums2(CTX)
            residual(2, CTX)

            for t in range(NT):
                dve.wait_ge(o_tr, t + 1)
                if t >= 2:
                    dve.wait_ge(o_st[t % 2], val(16 * (t // 2)))
                dve.tensor_copy(orow[t % 2][:, :], A[t % 2][:, :]).then_inc(o_cp, 1)


_INS = ["x", "meta_tokens", "norm1_w", "w_in", "conv_w", "diff_lambda", "diff_subln_w", "w_branch", "w_out",
        "norm2_w", "w_up", "w_down", "final_norm_w", "c_2", "ctx_2", "c_ctx_2", "w_ada_2", "b_ada_2", "norm_g_2",
        "ffn1_w1_2", "ffn1_w3_2", "ffn1_w2_2", "w_in_2", "b_gate_2", "g_q_lora_2", "g_kv_lora_2", "w_uq_2",
        "w_ukv_2", "rpb_2", "w_o_na_2", "w_o_mla_2", "w_out_2", "ffn2_w1_2", "ffn2_w3_2", "ffn2_w2_2"]


def kernel(**inputs):
    import concourse.bacc as _bacc
    from concourse.bass_utils import run_bass_kernel_spmd as _run

    nc = _bacc.Bacc("TRN2", target_bir_lowering=False, num_devices=1)
    arrays, aps = {}, {}
    for name in _INS:
        a = np.ascontiguousarray(inputs[name])
        arrays[f"in_{name}_dram"] = a
        aps[name] = nc.dram_tensor(f"in_{name}_dram", a.shape, mybir.dt.from_np(a.dtype), kind="ExternalInput").ap()
    for name, a in shape_constants().items():
        a = np.ascontiguousarray(a)
        arrays[f"const_{name}_dram"] = a
        aps[name] = nc.dram_tensor(f"const_{name}_dram", a.shape, F32, kind="ExternalInput").ap()
    out = nc.dram_tensor("out_0_dram", (1, SEQ, D), F32, kind="ExternalOutput").ap()
    build(nc, aps, out)
    r = _run(nc, [arrays], core_ids=[0])
    return r.results[0]["out_0_dram"]
```

```python
import math
from contextlib import ExitStack

import numpy as np
import concourse.bass as bass
from concourse import mybir

F32 = mybir.dt.float32
F32R = mybir.dt.float32r
ALU = mybir.AluOpType
ACT = mybir.ActivationFunctionType
AX = mybir.AxisListType.X

P = 128
D = 1024
KC = D // P
SEQ = 512
META = 16
T1 = META + SEQ
CTX = 256
T2 = CTX + SEQ
NT = SEQ // P
EPS = 1e-6
NEG = -1e30

TILES = [(0, META)] + [(META + P * t, P) for t in range(NT)]

RET_H, RET_DK, RET_DV = 4, P, 2 * P
DIFF_H = 8
W_RQ, W_RK, W_RV, W_RG = 0, 512, 1024, 2048
W_DQ, W_DK, W_DV = 3072, 4096, 5120
W_CB, W_CC, W_CX, W_GATE = 6144, 7168, 8192, 9216
FF1 = 4 * D
LAM_INIT = 0.8 - 0.6 * math.exp(0.0)

GRID_W, GRID_H = 64, 8
NA_H, NA_HD = 8, 64
W_QA, W_KA, W_VA, W_CQ, W_CKV, W_KR, W_G2 = 0, 512, 1024, 1536, 2304, 2560, 2592
QR, KVR = 768, 256
NOPE, ROPE, VD = 64, 32, 64
QK = NOPE + ROPE
FF2 = 2816
FF2_CHUNKS = FF2 // P
NA_START = [8 * min(max(16 * t - 8, 0), 32) for t in range(NT)]
V_STARTS = [0, 64, 128, 192, 256, 320, 384]
NV = len(V_STARTS)

_C = {}


def _layout():
    at = 0
    for name, n in (("ident", P), ("ones", P), ("slope8", DIFF_H), ("onehot8", 16), ("window", 3 * 32),
                    ("rot", QK), ("eps", 1), ("minus_half", 8)):
        _C[name] = (at, n)
        at += n
    return at


CONST_N = _layout()


def shape_constants():
    c = np.zeros((P, CONST_N), np.float32)

    def put(name, v):
        a, n = _C[name]
        c[:, a:a + n] = v

    p = np.arange(P)
    put("ident", np.eye(P))
    put("ones", 1.0)
    x = np.arange(T1)[None, :] - (T1 - P) - p[:, None]
    rel = np.where(x > 0, NEG, x).astype(np.float32)
    put("slope8", 8.0 * 2.0 ** -(np.arange(DIFF_H) + 1.0)[None, :])
    put("onehot8", np.where(p[:, None] // GRID_H == np.arange(16)[None, :], 8.0, 0.0))
    b, a = (p // GRID_H)[:, None], np.arange(32)[None, :]
    kinds = []
    for t in (0, 1, 3):
        ws = np.clip(16 * t + b - 8, 0, GRID_W - 16)
        kc = NA_START[t] // GRID_H + a
        kinds.append(np.where((kc >= ws) & (kc < ws + 16), 0.0, NEG))
    put("window", np.concatenate(kinds, 1))
    rot = np.zeros((P, QK), np.float32)
    for i in range(8):
        for o in (NOPE, NOPE + 16):
            rot[o + 8 + i, o + i] = -1.0
            rot[o + i, o + 8 + i] = 1.0
    put("rot", rot)
    half = 8
    freqs = (np.float32(10000.0) ** (-np.arange(half, dtype=np.float32) / np.float32(half))).astype(np.float32)
    n = np.arange(SEQ)
    rows, cols = (n % GRID_H).astype(np.float32), (n // GRID_H).astype(np.float32)
    ang = np.concatenate([rows[None] * freqs[:, None]] * 2 + [cols[None] * freqs[:, None]] * 2, 0)
    rope = np.stack([np.cos(ang.astype(np.float32)), np.sin(ang.astype(np.float32))], 1)
    put("eps", EPS)
    put("minus_half", -0.5)
    log_g = np.log1p(-np.exp2(-5.0 - np.arange(RET_H)))
    m = np.arange(T1)[None, None, :] - p[:, None, None]
    decay = np.where(m >= 0, np.exp(log_g[None, :, None] * np.maximum(m, 0)) * RET_DK ** -0.5, 0.0)
    return {"const": c, "rel": rel, "rope": rope.astype(np.float32), "decay": decay.astype(np.float32)}


class Count:

    def __init__(self, base, *terms):
        self.base, self.terms = base, terms

    def __add__(self, n):
        return Count(self.base + n, *self.terms)

    @property
    def slot(self):
        return self.base % 2

    def value(self, add=0):
        v = self.base + add
        for reg, step in self.terms:
            v = reg * step + v
        return v

    def turns(self):
        return Count(self.base // 2, *((reg, step // 2) for reg, step in self.terms))


def count(base, *terms):
    return Count(base + sum(r * st for r, st in terms if isinstance(r, int)),
                 *(t for t in terms if not isinstance(t[0], int)))


def turn(i, base, step):
    return count(base, (i, step))


def flat(ap, n):
    names = " ".join(f"d{i}" for i in range(len(ap.shape)))
    return ap.rearrange(f"{names} -> ({names})").rearrange("(r n) -> r n", n=n)


def val(count):
    return count.value() if isinstance(count, Count) else count


def alone(eng, passed):
    eng.sem_inc(passed, 1)


ADA_BOTH = 5 * KC
ADA_STEPS = 4 * KC
ADA_STEP = (0, KC, 3 * KC)
ADA_STEP_CONV = 2 * KC

U_RET = 0
U_BR = [RET_H * 6, RET_H * 6 + 16 + DIFF_H * 3, RET_H * 6 + 32 + DIFF_H * 3 + KC * 3]
U_DIFF = U_BR[0] + 16
U_CONV = U_BR[1] + 16
U_OUT = U_BR[2] + 16
U_FF = U_OUT + KC
U_FA = U_FF + (FF1 // D) * 16
U_NA = U_FA + 48 + 20
U_LORA = U_NA + 12
U_MLA = U_LORA + 9
U_GATE = U_MLA + 16
U_OUT2 = U_GATE + 32
U_FB = U_OUT2 + KC
U_END = U_FB + 48 + 20

G1 = [(0, T1 // 2), (T1 // 2, T1 // 2)]
G2 = [(0, T2 // 2), (T2 // 2, T2 // 2)]
GL = [(CTX, SEQ)]
GS = [(0, SEQ)]


def build(nc, I, out):
    with ExitStack() as ctx:
        def sem(name):
            return ctx.enter_context(nc.semaphore(name))

        def ps(name, cols):
            return ctx.enter_context(nc.psum_tensor(name, [P, cols], F32))

        base0 = (nc.sbuf_base + 63) // 64 * 64

        def at(name, off, shape, dt=F32):
            return nc.alloc_sbuf_tensor_at(name, [P] + list(shape), dt, offset=base0 + off)

        top = [0]

        def seq(name, shape, dt=F32):
            n = 4 * int(np.prod(shape))
            t = at(name, top[0], shape, dt)
            top[0] += (n + 31) // 32 * 32
            return t

        raw = [seq(f"raw{s}", [KC, P]) for s in range(2)]
        wh = [seq(f"w_hi{s}", [KC, P], F32R) for s in range(2)]
        wl = [seq(f"w_lo{s}", [KC, P], F32R) for s in range(2)]
        const = seq("const", [CONST_N])
        col_a = seq("col_a", [65])
        col_b = seq("col_b", [72])
        col_c = seq("col_c", [72])
        silu_c = seq("silu_c", [KC, 2])
        ada = seq("ada", [72, 2])
        gain = [seq(f"gain{i}", [KC, 2]) for i in range(3)]
        resg = [seq(f"res_gain{i}", [KC, 2]) for i in range(3)]
        small = seq("small", [8])
        rope = seq("rope", [2, SEQ])
        PH = top[0]

        def cst(name, lo=0, hi=P):
            a, n = _C[name]
            return const[lo:hi, a:a + n]

        ident = cst("ident")
        ones = cst("ones")
        eps_col = cst("eps")
        minus_half = cst("minus_half")

        ACT_B = KC * T1 * 4
        X = at("x1", PH, [KC, T1])
        HH = at("h_hi", PH + ACT_B, [KC, T1], F32R)
        HL = at("h_lo", PH + 2 * ACT_B, [KC, T1], F32R)
        BH = at("branch_hi", PH + 3 * ACT_B, [KC, T1], F32R)
        BL = at("branch_lo", PH + 4 * ACT_B, [KC, T1], F32R)
        MG = at("merged", PH + 5 * ACT_B, [KC, T1])
        SCR = PH + 6 * ACT_B
        tmp = [at(f"tmp{s}", SCR + s * 4 * T1, [T1]) for s in range(2)]
        sqb = [at(f"square{s}", SCR + (2 + s) * 4 * T1, [T1]) for s in range(2)]
        ssq = at("ssq", SCR + 4 * 4 * T1, [T1])
        rstd = at("rstd", SCR + 5 * 4 * T1, [T1])
        S1 = SCR + 6 * 4 * T1
        DT = at("decay", S1, [RET_H, T1])
        o = S1 + RET_H * T1 * 4
        rq = at("ret_q", o, [T1]); o += 4 * T1
        rk = at("ret_k", o, [T1]); o += 4 * T1
        rvT = [at(f"ret_vT{s}", o + s * 4 * T1, [T1]) for s in range(2)]; o += 8 * T1
        rg = [at(f"ret_g{s}", o + s * 4 * T1, [T1]) for s in range(2)]; o += 8 * T1
        ST_W = [T1 - q0 for q0, _ in TILES]
        ST_AT = [sum(ST_W[:c]) for c in range(5)]
        rST = at("ret_scoresT", o, [sum(ST_W)]); o += 4 * sum(ST_W)
        rV = at("ret_v", o, [5, RET_DV]); o += 4 * 5 * RET_DV
        rY = at("ret_y", o, [5, RET_DV]); o += 4 * 5 * RET_DV
        bst = at("bn_stats", o, [5, 6]); o += 128
        bag = at("bn_aggr", o, [5, 2]); o += 64
        rvar = at("ret_var", o, [5]); o += 32
        rpow = at("ret_rstd", o, [5]); o += 32
        SCR_USED = o
        o = S1
        dqs = [at("diff_q0", o, [T1]), at("diff_q1", SCR + 2 * 4 * T1, [T1])]; o += 4 * T1
        dks = [at("diff_k0", o, [T1]), at("diff_k1", SCR + 3 * 4 * T1, [T1])]; o += 4 * T1
        dvT = at("diff_vT", o, [T1]); o += 4 * T1
        dR = at("diff_bias", o, [T1]); o += 4 * T1
        dL = [[at(f"diff_p{s}{m}", o + (2 * s + m) * 4 * T1, [T1]) for m in range(2)] for s in range(2)]; o += 16 * T1
        dT = [at(f"diff_pT{s}", o + s * 4 * 5 * P, [5, P]) for s in range(2)]; o += 8 * 5 * P
        dV = at("diff_v", o, [5, P]); o += 20 * P
        dO = at("diff_o", o, [5, P]); o += 20 * P
        dOn = at("diff_on", o, [5, P]); o += 20 * P
        dsq = at("diff_sq", o, [P]); o += 4 * P
        dmax = at("diff_max", o, [2, 2]); o += 32
        dnb = at("diff_nb", o, [2, 2]); o += 32
        dsum = at("diff_sum", o, [2, 2]); o += 32
        drc = at("diff_rc", o, [2, 2]); o += 32
        dlr = at("diff_lr", o, [2, 1]); o += 32
        dss = at("diff_ss", o, [5]); o += 32
        dss2 = at("diff_ss2", o, [5]); o += 32
        dpow = at("diff_rstd", o, [5]); o += 32
        SCR_USED = max(SCR_USED, o)
        rel = at("rel", SCR_USED, [T1])
        cb = at("conv_b", S1, [T1])
        cc = at("conv_c", S1 + 4 * T1, [T1])
        cu = at("conv_u", S1 + 8 * T1, [T1])
        cy = at("conv_y", S1 + 12 * T1, [T1])
        sg = [at(f"gate{s}", S1 + (4 + s) * 4 * T1, [T1]) for s in range(2)]
        MH = at("merged_hi", S1 + 6 * 4 * T1, [KC, T1], F32R)
        ML = at("merged_lo", S1 + 6 * 4 * T1 + ACT_B, [KC, T1], F32R)
        xt = [at(f"x_rows{t}", PH + 3 * ACT_B + 4096 * t, [D]) for t in range(5)]
        rows_a = at("rows_a", PH + 3 * ACT_B + 4096 * 5, [P])
        rows_b = at("rows_b", PH + 3 * ACT_B + 4096 * 5 + 512, [P])
        rows_c = at("rows_c", PH + 3 * ACT_B + 4096 * 5 + 1024, [P])
        lam_v = at("lam_v", PH + 3 * ACT_B + 4096 * 5 + 1536, [4, 64])
        lam_p = at("lam_p", PH + 3 * ACT_B + 4096 * 5 + 2560, [2, 64])
        AD = max(SCR_USED + 4 * T1, S1 + 6 * 4 * T1 + 2 * ACT_B)
        araw = [at(f"ada_raw{s}", AD + s * 4096, [KC, P]) for s in range(2)]
        asum = at("ada_sum", AD + 2 * 4096, [P])
        ACT2 = KC * T2 * 4
        X2 = at("x2", PH + 5 * ACT2 + 32512, [KC, T2])
        H2H = at("h2_hi", PH, [KC, T2], F32R)
        H2L = at("h2_lo", PH + ACT2, [KC, T2], F32R)
        U2 = PH + 2 * ACT2
        UH2 = at("u2_hi", U2, [KC, T2], F32R)
        UL2 = at("u2_lo", U2 + ACT2, [KC, T2], F32R)
        Y2 = at("y2", U2 + 2 * ACT2, [KC, T2])
        E = U2 + 3 * ACT2
        tm2 = [at(f"tmp2_{s}", E + s * 4 * T2, [T2]) for s in range(2)]
        ss2 = at("ssq2", E + 2 * 4 * T2, [T2])
        rs2 = at("rstd2", E + 3 * 4 * T2, [T2])
        EE = E + 16 * T2
        rpbG = at("rpb_rows", EE, [NA_H * GRID_H, 31])
        rpbT = at("rpb_shifted", EE + 7936, [NA_H * GRID_H, 48])
        assert EE + 7936 + 12288 <= PH + 5 * ACT2 + 32512
        ctxr = [at(f"ctx_rows{t}", PH + 5 * ACT_B + 4096 * t, [D]) for t in range(2)]
        NA_OH = at("na_oT_hi", U2, [4, SEQ], F32R)
        NA_OL = at("na_oT_lo", U2 + 8192, [4, SEQ], F32R)
        L2 = U2 + 16384
        o = L2
        nB = at("na_bias", o, [3, NA_H, 256]); o += 3 * NA_H * 1024
        nqs = [at("na_q0", o, [SEQ]), at("na_q1", E + 4 * T2, [SEQ])]; o += 2048
        nks = [at("na_k0", o, [T2]), at("na_k1", E, [T2])]; o += 4 * T2
        nvT = at("na_vT", o, [T2]); o += 4 * T2
        nV = at("na_v", o, [NV + 2, P]); o += 512 * (NV + 2)
        nP = [at(f"na_p{s}", o + s * 2048, [SEQ]) for s in range(2)]; o += 4096
        nT = [at(f"na_pT{s}", o + s * 2048, [4, P]) for s in range(2)]; o += 4096
        nO = at("na_o", o, [NT, NA_H * NA_HD]); o += NT * 2048
        nst = at("na_stat", o, [2, 8]); o += 64
        nBs = [at(f"na_bias_head{s}", EE + 7936 + s * 3072, [3, 256]) for s in range(2)]
        assert o <= E
        o = L2
        ckvT = at("ckv", o, [2, T2]); o += 8 * T2
        CKH = at("ckv_hi", o, [2, T2], F32R); o += 8 * T2
        CKL = at("ckv_lo", o, [2, T2], F32R); o += 8 * T2
        cqT = at("cq", o, [6, SEQ]); o += 6 * 2048
        CQ = o
        CQH = at("cq_hi", o, [6, SEQ], F32R); o += 6 * 2048
        CQL = at("cq_lo", o, [6, SEQ], F32R); o += 6 * 2048
        mV = at("mla_v", o, [6, VD]); o += 24 * VD
        mst = at("mla_stat", o, [2, 8]); o += 64
        assert o <= E
        mP = [at(f"mla_p{s}", L2 + s * 4 * T2, [T2]) for s in range(2)]
        mO = at("mla_o", L2 + 3 * 8 * T2, [NT, 512])
        o = EE
        mkr = at("mla_kr", o, [T2]); o += 4 * T2
        mks = [at("mla_k0", o, [T2]), at("mla_k1", E, [T2])]; o += 4 * T2
        mqs = [at("mla_q0", o, [SEQ]), at("mla_q1", E + 4 * T2, [SEQ])]; o += 2048
        mqr = at("mla_qr", o, [SEQ]); o += 2048
        mvT = at("mla_vT", o, [T2]); o += 4 * T2
        mT = [at(f"mla_pT{s}", o + s * 4 * T2, [6, P]) for s in range(2)]; o += 8 * T2
        assert o <= PH + 5 * ACT2 + 32512
        MH2 = at("merged2_hi", L2, [KC, SEQ], F32R)
        ML2 = at("merged2_lo", L2 + 16384, [KC, SEQ], F32R)
        ML_OH = at("mla_oT_hi", CQ + 2048, [4, SEQ], F32R)
        ML_OL = at("mla_oT_lo", CQ + 2048 + 8192, [4, SEQ], F32R)
        sgl = [at(f"gate2_{s}", CQ + 2048 + 16384 + s * 2048, [SEQ]) for s in range(2)]
        orow = [at(f"out_rows{s}", U2 + s * 4096, [D]) for s in range(2)]

        G = [ps(f"unit_acc{s}", 1024) for s in range(2)]
        A = [ps(f"aux{s}", 1024) for s in range(2)]

        raw_landed = [sem(f"raw_landed{s}") for s in range(2)]
        hi_split = sem("hi_split")
        lo_split = sem("lo_split")
        unit_done = sem("unit_done")
        evicted = [sem(f"evicted{s}") for s in range(2)]
        const_in = sem("const_in")
        pe_passed, act_passed = sem("pe_passed"), sem("act_passed")
        sp_passed, dve_passed = sem("sp_passed"), sem("dve_passed")
        x_in = sem("x_in")
        rows_in = sem("rows_in")
        decay_in = sem("decay_in")
        rel_in = sem("rel_in")
        rope_in = sem("rope_in")
        lam_in = sem("lam_in")
        xT_done = sem("xT_done")
        xT_out = sem("xT_out")
        cols_done = sem("cols_done")
        cols_out = sem("cols_out")
        cols_act = sem("cols_act")
        lam_dve = sem("lam_dve")
        lam_act = sem("lam_act")
        nrm_sq = sem("nrm_sq")
        nrm_add = sem("nrm_add")
        nrm_sum = sem("nrm_sum")
        nrm_root = sem("nrm_root")
        ap_tmp = sem("ap_tmp")
        ap_hi = sem("ap_hi")
        ap_lo = sem("ap_lo")
        r_sc = sem("ret_sc"); r_st = sem("ret_st"); r_vt = sem("ret_vt"); r_v = sem("ret_v_ready")
        r_pv = sem("ret_pv"); r_var = sem("ret_var_ready"); r_pow = sem("ret_pow"); r_y = sem("ret_y_ready")
        r_yt = sem("ret_yt"); r_tmp = sem("ret_tmp"); r_hi = sem("ret_hi")
        br_lo = sem("branch_ready")
        mg_add = sem("merged_added"); mg_hi = sem("merged_hi_done")
        d_bias = sem("diff_bias_ready"); d_qk = sem("diff_qk"); d_log = sem("diff_logits"); d_exp = sem("diff_exp")
        d_att = sem("diff_att"); d_tr = sem("diff_tr"); d_at = sem("diff_at"); d_pv = sem("diff_pv")
        d_o = sem("diff_o_out"); d_vt = sem("diff_vt"); d_v = sem("diff_v_ready"); d_ss = sem("diff_ss_ready")
        d_pow = sem("diff_pow"); d_on = sem("diff_on_ready"); d_ot = sem("diff_ot"); d_hi = sem("diff_hi")
        c_y = sem("conv_y_ready"); c_hi = sem("conv_hi")
        m_lo = sem("merged_ready")
        ff_r = sem("ff_relu"); ff_hi = sem("ff_hi"); ff_lo = sem("ff_lo")
        ada_landed = [sem(f"ada_landed{s}") for s in range(2)]
        ada_used = sem("ada_used")
        ada_mm = sem("ada_mm")
        ada_out = sem("ada_out")
        ctx_in = sem("ctx_in"); ctx_done = sem("ctx_done"); ctx_out = sem("ctx_out")
        x2_out = sem("x2_out"); x2_tmp = sem("x2_tmp")
        rpb_in = sem("rpb_in"); rpb_zero = sem("rpb_zero"); y_zero = sem("y_zero")
        n_qk = sem("na_qk"); n_log = sem("na_log"); n_exp = sem("na_exp"); n_tr = sem("na_tr"); n_at = sem("na_at")
        n_pv = sem("na_pv"); n_o = sem("na_o_out"); n_vt = sem("na_vt"); n_v = sem("na_v_ready")
        n_tab = sem("na_bias_ready"); n_bias = sem("na_bias_head_ready")
        n_ot = sem("na_ot"); n_hi = sem("na_hi"); n_lo = sem("na_lo")
        k_qk = sem("mla_qk"); k_log = sem("mla_log"); k_exp = sem("mla_exp"); k_tr = sem("mla_tr"); k_tr1 = sem("mla_tr_second")
        k_at = sem("mla_at"); k_ad = sem("mla_ad"); k_pv = sem("mla_pv"); k_o = sem("mla_o_out")
        k_vt = sem("mla_vt"); k_v = sem("mla_v_ready"); k_ot = sem("mla_ot"); k_hi = sem("mla_hi"); k_lo = sem("mla_lo")
        k_rot = sem("mla_rot"); k_q = sem("mla_q_ready"); k_kr = sem("mla_kr_ready"); k_kra = sem("mla_kr_act")
        o_tr = sem("out_tr"); o_cp = sem("out_cp"); o_st = [sem(f"out_st{s}") for s in range(2)]

        def two(ap, n):
            return ap.rearrange("p (s n) -> p s n", s=2)

        def acc(t, geo, rows=P, lo=0):
            n = geo[0][1]
            if len(geo) == 1:
                return t[lo:rows, 0:n]
            return t[:, :].rearrange("p (s n) -> p s n", s=2)[lo:rows, :, 0:n]

        def like(ap, geo):
            return ap if len(geo) == 1 else two(ap, geo[0][1])

        def meta_pT(t, n):
            a = P if t == 4 else 512 + P * t
            return A[1][0:META, a:a + n]

        def landed(eng, v):
            eng.wait_ge(raw_landed[v.slot], val(Count(16 * (v.base // 2) + 16, *((r, 8 * st) for r, st in v.terms))))

        NSQ = {}
        for k, chunks in enumerate((8, 8, 8, 8, 8, 8, 2, 6, 8, 8, 8)):
            NSQ[k + 1] = NSQ.get(k, 0) + chunks

        block = ctx.enter_context(nc.Block())

        @block.sync
        def _(sp):
            sp.dma_start(const[:, :], I["const"]).then_inc(const_in, 16)
            for t, (q0, n) in enumerate(TILES):
                src = I["meta_tokens"] if t == 0 else I["x"][0, P * (t - 1):P * t, :]
                sp.dma_start(xt[t][0:n, :], src).then_inc(x_in, 16)
            row = 0
            for src, n in ((I["norm1_w"], 8), (I["norm2_w"], 8), (I["final_norm_w"], 8), (I["conv_w"], 24),
                           (I["diff_subln_w"], 1), (I["c_2"], 8), (I["c_ctx_2"], 8)):
                sp.dma_start(rows_a[row:row + n, :], flat(src, P)).then_inc(rows_in, 16)
                row += n
            row = 0
            for src, n in ((I["norm_g_2"], 48), (I["b_gate_2"], 16), (I["g_q_lora_2"], 6), (I["g_kv_lora_2"], 2)):
                sp.dma_start(rows_b[row:row + n, :], flat(src, P)).then_inc(rows_in, 16)
                row += n
            sp.dma_start(rows_c[0:72, :], flat(I["b_ada_2"], P)).then_inc(rows_in, 16)
            sp.dma_start(lam_v[:, :, :], I["diff_lambda"].partition_broadcast(P)).then_inc(lam_in, 16)

            def load(u, src, kc, n):
                if u.terms or u.base >= 2:
                    sp.wait_ge(lo_split, val(u + (-1)))
                if u.terms:
                    alone(sp, sp_passed)
                sp.dma_start(raw[u.slot][:, 0:kc, 0:n], src.rearrange("(k p) n -> p k n", p=P)).then_inc(
                    raw_landed[u.slot], 16)

            def load_ada(q, chunk):
                sp.wait_ge(ada_used, val(q + 1))
                if q.terms:
                    alone(sp, sp_passed)
                sp.dma_start(araw[q.slot][:, :, :],
                             I["w_ada_2"][0, :, bass.ds(chunk.value() * P, P)].rearrange("(k p) n -> p k n", p=P)
                             ).then_inc(ada_landed[q.slot], 16)

            def cols(name, at_, n=P, j=None, r0=0, rn=D):
                w = I[name][0] if j is None else I[name][0, j]
                return w[r0:r0 + rn, bass.ds(at_, n)]

            def ret_cols(h, k):
                c, step = ((W_RQ, P), (W_RK, P), (W_RV, 256), (W_RV + P, 256), (W_RG, 256), (W_RG + P, 256))[k]
                return cols("w_in", h * step + c)

            for k in range(2):
                load(Count(k), ret_cols(0, k), KC, P)
            sp.dma_start(DT[:, :, :], I["decay"]).then_inc(decay_in, 16)
            sp.dma_start(rel[:, :], I["rel"]).then_inc(rel_in, 16)
            sp.dma_start(rope[NOPE:QK, :, :], I["rope"]).then_inc(rope_in, 16)
            with sp.Fori(0, RET_H - 1) as h:
                for k in range(2, 6):
                    load(Count(U_RET + k, (h, 6)), ret_cols(h, k), KC, P)
                for k in range(2):
                    load(Count(U_RET + 6 + k, (h, 6)), ret_cols(h + 1, k), KC, P)
            for k in range(2, 6):
                load(Count(U_RET + 6 * (RET_H - 1) + k), ret_cols(RET_H - 1, k), KC, P)

            def load_branch(r):
                with sp.Fori(0, KC // 2) as i:
                    for e in range(2):
                        u = Count(U_BR[r] + 2 * e, (i, 4))
                        load(u, cols("w_in", i * 256 + (W_GATE + r * D + e * P)), KC, P)
                        load(u + 1, cols("w_branch", i * 256 + e * P, j=r), KC, P)
                        q = Count(ADA_STEP[r] + e, (i, 2))
                        load_ada(q, q + ADA_BOTH)

            load_branch(0)
            with sp.Fori(0, DIFF_H // 2) as i:
                for e in range(2):
                    for k, c in enumerate((W_DQ, W_DK, W_DV)):
                        load(Count(U_DIFF + 3 * e + k, (i, 6)), cols("w_in", i * 256 + (c + e * P)), KC, P)
            load_branch(1)
            with sp.Fori(0, KC // 2) as i:
                for e in range(2):
                    for k, c in enumerate((W_CB, W_CC, W_CX)):
                        load(Count(U_CONV + 3 * e + k, (i, 6)), cols("w_in", i * 256 + (c + e * P)), KC, P)
                    q = Count(ADA_STEP_CONV + e, (i, 2))
                    load_ada(q, q + ADA_BOTH)
            load_branch(2)
            for n in range(KC):
                load(Count(U_OUT + n), cols("w_out", n * P), KC, P)
                load_ada(Count(ADA_STEPS + n), Count(n))
            for t in range(2):
                sp.dma_start(ctxr[t][:, :], I["ctx_2"][0, P * t:P * (t + 1), :]).then_inc(ctx_in, 16)
            with sp.Fori(0, FF1 // D) as part:
                with sp.Fori(0, 4) as i:
                    for e in range(2):
                        load(Count(U_FF + e, (part, 16), (i, 2)), cols("w_up", part * D + (i * 256 + e * P)), KC, P)
                        a = Count(KC + e, (part, 8), (i, 2))
                        load_ada(a + ADA_STEPS, a)
                with sp.Fori(0, 4) as i:
                    for e in range(2):
                        load(Count(U_FF + 8 + e, (part, 16), (i, 2)),
                             I["w_down"][0, bass.ds(part * D, D), bass.ds(i * 256 + e * P, P)], KC, P)

            def load_swiglu(base, w1, w3, w2):
                with sp.Fori(0, 2) as part:
                    with sp.Fori(0, 8) as n:
                        for e, w in enumerate((w1, w3)):
                            load(Count(base + e, (part, 24), (n, 2)), cols(w, part * D + n * P), KC, P)
                    with sp.Fori(0, 4) as i:
                        for e in range(2):
                            load(Count(base + 16 + e, (part, 24), (i, 2)),
                                 I[w2][0, bass.ds(part * D, D), bass.ds(i * 256 + e * P, P)], KC, P)
                with sp.Fori(0, 6) as n:
                    for e, w in enumerate((w1, w3)):
                        load(Count(base + 48 + e, (n, 2)), cols(w, n * P + 2 * D), KC, P)
                with sp.Fori(0, 4) as i:
                    for e in range(2):
                        load(Count(base + 60 + e, (i, 2)),
                             I[w2][0, 2 * D:FF2, bass.ds(i * 256 + e * P, P)], 6, P)

            src = I["rpb_2"][0]
            for r in range(GRID_H):
                sp.dma_start(
                    rpbG[r:P:GRID_H, :, :].rearrange("p (h a) n -> p h (a n)", h=NA_H),
                    src[:, GRID_H - 1 - r:2 * GRID_H - 1 - r, :].rearrange("h r n -> h (r n)").partition_broadcast(16)
                ).then_inc(rpb_in, 16)
            load_swiglu(U_FA, "ffn1_w1_2", "ffn1_w3_2", "ffn1_w2_2")
            with sp.Fori(0, 2) as i:
                for e in range(2):
                    for k, c in enumerate((W_QA, W_KA, W_VA)):
                        load(Count(U_NA + 3 * e + k, (i, 6)), cols("w_in_2", i * 256 + (c + e * P)), KC, P)
            for k in range(2):
                load(Count(U_LORA + k), cols("w_in_2", W_CKV + k * P), KC, P)
            load(Count(U_LORA + 2), cols("w_in_2", W_KR - NOPE, QK), KC, QK)
            for k in range(6):
                load(Count(U_LORA + 3 + k), cols("w_in_2", W_CQ + k * P), KC, P)
            with sp.Fori(0, 8) as h:
                load(Count(U_MLA, (h, 2)), I["w_uq_2"][0, :, bass.ds(h * QK, QK)], 6, QK)
                load(Count(U_MLA + 1, (h, 2)), I["w_ukv_2"][0, :, bass.ds(h * P, P)], 2, P)
            with sp.Fori(0, KC) as n:
                load(Count(U_GATE, (n, 4)), cols("w_in_2", n * P + W_G2), KC, P)
                load(Count(U_GATE + 1, (n, 4)), I["w_o_na_2"][0, :, bass.ds(n * P, P)], 4, P)
                load(Count(U_GATE + 2, (n, 4)), cols("w_in_2", n * P + (W_G2 + D)), KC, P)
                load(Count(U_GATE + 3, (n, 4)), I["w_o_mla_2"][0, :, bass.ds(n * P, P)], 4, P)
            with sp.Fori(0, 4) as i:
                for e in range(2):
                    load(Count(U_OUT2 + e, (i, 2)), cols("w_out_2", i * 256 + e * P), KC, P)
            load_swiglu(U_FB, "ffn2_w1_2", "ffn2_w3_2", "ffn2_w2_2")
            grid = out[0].rearrange("(r c) d -> c r d", r=GRID_H)
            for t in range(NT):
                sp.wait_ge(o_cp, t + 1)
                sp.dma_start(grid[16 * t:16 * t + 16, :, :], orow[t % 2][:, :]).then_inc(o_st[t % 2], 16)
            for s in range(2):
                sp.wait_ge(o_st[s], 32)

        @block.tensor
        def _(pe):
            def tr(dst, src, k=P, k0=0):
                return pe.transpose(dst, src, ident[k0:k0 + k, k0:k0 + k])

            def unit(u, hi, lo, geo, kc=KC, n=P, ready=None, part=None):
                k0, k1 = part or (0, kc)
                if k0 == 0:
                    pe.wait_ge(lo_split, val(u + 1))
                    pe.wait_ge(evicted[u.slot], val(u.turns() + 1))
                s = u.slot
                for k in range(k0, k1):
                    if ready is not None:
                        pe.wait_ge(ready[0], ready[1] + k + 1)
                    for i, (w, x) in enumerate(((wh, hi), (wh, lo), (wl, hi))):
                        for j, (a, m) in enumerate(geo):
                            last = pe.matmul(G[s][0:n, 512 * j:512 * j + m], w[s][:, k, 0:n], x[:, k, a:a + m],
                                             start=(k == 0 and i == 0), stop=(k == kc - 1 and i == 2))
                if k1 == kc:
                    last.then_inc(unit_done, 1)

            norms = [0]

            def sum_squares(src, geo):
                norms[0] += 1
                pe.wait_ge(nrm_add, NSQ[norms[0]])
                for j, (a, m) in enumerate(geo):
                    last = pe.matmul(A[0][:, 512 * j:512 * j + m], ones, src[:, a:a + m], start=True, stop=True)
                last.then_inc(nrm_sum, 1)

            pe.wait_ge(const_in, 16)
            pe.wait_ge(rows_in, 16 * 12)
            tr(A[0][:, 0:65], rows_a[0:65, :], 65)
            tr(A[0][:, 128:200], rows_b[0:72, :], 72)
            tr(A[0][:, 256:328], rows_c[0:72, :], 72).then_inc(cols_done, 1)
            pe.wait_ge(x_in, 16 * 5)
            pe.wait_ge(cols_out, 1)
            for c in range(KC):
                if c >= 2:
                    pe.wait_ge(xT_out, val(c - 1))
                for t, (q0, n) in enumerate(TILES):
                    dst = A[c % 2][:, 512:512 + n] if t == 0 else A[c % 2][:, P * (t - 1):P * t]
                    last = tr(dst, xt[t][0:n, P * c:P * (c + 1)], n)
                last.then_inc(xT_done, 1)
            sum_squares(ssq, G1)

            def retention(h):
                u = Count(U_RET, (h, 6))
                for k in range(3):
                    unit(u + k, HH, HL, G1, ready=(ap_lo, 0) if k == 0 else None)
                for s in range(2):
                    pe.wait_ge(evicted[s], val(u.turns() + 2))
                for c, (q0, n) in enumerate(TILES):
                    if c >= 2:
                        pe.wait_ge(r_st, val(Count(c - 1, (h, 5))))
                    w = ST_W[c]
                    for a in range(0, w, 512):
                        m = min(512, w - a)
                        last = pe.matmul(A[c % 2][0:n, a:a + m], rk[:, q0:q0 + n], rq[:, q0 + a:q0 + a + m],
                                         start=True, stop=True)
                    last.then_inc(r_sc, 1)
                unit(u + 3, HH, HL, G1)
                for s in range(2):
                    pe.wait_ge(evicted[s], val(u.turns() + 3))
                pe.wait_ge(r_st, val(Count(5, (h, 5))))
                for half in range(2):
                    for t, (q0, n) in reversed(list(enumerate(TILES))):
                        a = (t - 1) * RET_DV + half * P
                        dst = A[1][0:n, half * P:half * P + P] if t == 0 else A[0][:, a:a + P]
                        last = tr(dst, rvT[half][:, q0:q0 + n])
                last.then_inc(r_vt, 1)
                unit(u + 4, HH, HL, G1)
                pe.wait_ge(r_v, val(Count(1, (h, 1))))
                for t, (q0, n) in reversed(list(enumerate(TILES))):
                    dst = A[1][0:n, 0:RET_DV] if t == 0 else A[0][:, (t - 1) * RET_DV:t * RET_DV]
                    for c in range(t, -1, -1):
                        k0, kn = TILES[c]
                        a = ST_AT[c] + q0 - k0
                        last = pe.matmul(dst, rST[0:kn, a:a + n], rV[0:kn, c, :], start=(c == t), stop=(c == 0))
                last.then_inc(r_pv, 1)
                unit(u + 5, HH, HL, G1)
                pe.wait_ge(r_y, val(Count(1, (h, 1))))
                for half in range(2):
                    for t, (q0, n) in reversed(list(enumerate(TILES))):
                        a = 512 if t == 0 else P * (t - 1)
                        last = tr(A[half][:, a:a + n], rY[0:n, t, half * P:half * P + P], n)
                last.then_inc(r_yt, 1)

            with pe.Fori(0, RET_H) as h:
                retention(h)

            def ada_step(j):
                pe.wait_ge(ada_used, val(j + 3))
                pe.wait_ge(ada_out, val(j + 1))
                pe.matmul(A[1][:, 512:513], asum[:, :], ones[:, 0:1], start=True, stop=True).then_inc(ada_mm, 1)

            def merge(r):
                with pe.Fori(0, KC // 2) as i:
                    for e in range(2):
                        u = Count(U_BR[r] + 2 * e, (i, 4))
                        unit(u, HH, HL, G1)
                        unit(u + 1, BH, BL, G1, ready=(br_lo, KC * r))
                        ada_step(Count(ADA_STEP[r] + e, (i, 2)))
                pe.wait_ge(ada_out, ADA_STEP[r] + KC + 1)

            merge(0)

            def diff_head(i, e, more):
                u = turn(i, U_DIFF + 3 * e, 6)
                dq, dk = dqs[e], dks[e]

                def fill(k, k0, k1):
                    if more:
                        unit(u + 3 + k, HH, HL, G1, part=(k0, k1))

                def cnt(k):
                    return turn(i, k + 5 * e, 10)

                def qk(t):
                    q0, n = TILES[t]
                    if t < 4:
                        pe.wait_ge(d_log, val(cnt(4 - t)))
                    w = q0 + n
                    if t == 0:
                        alone(pe, pe_passed)
                    for m in range(2):
                        r = slice(64 * m, 64 * m + 64)
                        last = pe.matmul(A[0][0:n, 512 * m:512 * m + min(w, 512)], dq[r, q0:q0 + n],
                                         dk[r, 0:min(w, 512)], start=True, stop=True)
                    if w > 512:
                        for m in range(2):
                            r = slice(64 * m, 64 * m + 64)
                            last = pe.matmul(A[1][0:n, 512 * m:512 * m + w - 512], dq[r, q0:q0 + n],
                                             dk[r, 512:w], start=True, stop=True)
                    last.then_inc(d_qk, 1)

                def transpose_p(t):
                    q0, n = TILES[t]
                    pe.wait_ge(d_att, val(cnt(5 - t)))
                    if t < 4:
                        pe.wait_ge(d_at, val(cnt(4 - t)))
                    p = dL[t % 2][0]
                    if t == 0:
                        alone(pe, pe_passed)
                    for c in range(t, 0, -1):
                        tr(A[1][:, 512 + P * (c - 1):512 + P * (c - 1) + n],
                           p[0:n, TILES[c][0]:TILES[c][0] + P], n)
                    tr(meta_pT(t, n), p[0:n, 0:META], n).then_inc(d_tr, 1)

                def pv(t):
                    q0, n = TILES[t]
                    pe.wait_ge(d_at, val(cnt(5 - t)))
                    if t < 4:
                        pe.wait_ge(d_o, val(cnt(4 - t)))
                    if t == 0:
                        alone(pe, pe_passed)
                    for c in range(t, -1, -1):
                        kn = TILES[c][1]
                        last = pe.matmul(A[1][0:n, 256:384], dT[t % 2][0:kn, c, 0:n], dV[0:kn, c, :],
                                         start=(c == t), stop=(c == 0))
                    last.then_inc(d_pv, 1)

                for k in range(2):
                    pe.wait_ge(evicted[(u + k).slot], val((u + k).turns() + 2))
                pe.wait_ge(br_lo, val(turn(i, KC + e, 2)))
                qk(4)
                fill(0, 0, 3)
                qk(3)
                pe.wait_ge(evicted[u.slot], val((u + 2).turns() + 2))
                for t, (q0, n) in reversed(list(enumerate(TILES))):
                    dst = A[1][0:n, P:2 * P] if t == 0 else A[1][:, 512 + P * (t - 1):512 + P * t]
                    last = tr(dst, dvT[:, q0:q0 + n])
                last.then_inc(d_vt, 1)
                fill(0, 3, 8)
                pe.wait_ge(d_v, val(turn(i, 1 + e, 2)))
                transpose_p(4)
                qk(2)
                fill(1, 0, 3)
                pv(4)
                transpose_p(3)
                qk(1)
                fill(1, 3, 6)
                pv(3)
                transpose_p(2)
                qk(0)
                fill(1, 6, 8)
                pv(2)
                transpose_p(1)
                fill(2, 0, 1)
                pv(1)
                transpose_p(0)
                fill(2, 1, 2)
                pv(0)
                fill(2, 2, 6)
                pe.wait_ge(d_on, val(turn(i, 1 + e, 2)))
                for t, (q0, n) in reversed(list(enumerate(TILES))):
                    dst = A[1][:, 0:n] if t == 0 else A[0][:, P * (t - 1):P * t]
                    last = tr(dst, dOn[0:n, t, :], n)
                last.then_inc(d_ot, 1)
                fill(2, 6, 8)

            for k in range(3):
                unit(Count(U_DIFF + k), HH, HL, G1)
            with pe.Fori(0, DIFF_H // 2 - 1) as i:
                for e in range(2):
                    diff_head(i, e, True)
            for e in range(2):
                diff_head(DIFF_H // 2 - 1, e, e == 0)
            merge(1)

            with pe.Fori(0, KC // 2) as i:
                for e in range(2):
                    for k in range(3):
                        unit(Count(U_CONV + 3 * e + k, (i, 6)), HH, HL, G1)
                    ada_step(Count(ADA_STEP_CONV + e, (i, 2)))
            merge(2)

            def ada_unit(a):
                terms = [(r, 8 * st) for r, st in a.terms]
                pe.wait_ge(ada_landed[a.slot], val(Count(16 * ((a.base + ADA_STEPS) // 2) + 16, *terms)))
                dst = A[1][:, bass.ds(a.value() * 2 + 512, 2)]
                for k in range(KC):
                    last = pe.matmul(dst, araw[a.slot][:, k, :], silu_c[:, k, :], start=(k == 0), stop=(k == KC - 1))
                last.then_inc(ada_used, 1)

            for n in range(KC):
                unit(Count(U_OUT + n), MH, ML, G1, ready=(m_lo, 0))
                ada_unit(Count(n))
            sum_squares(ssq, G1)

            def ff_up(part):
                with pe.Fori(0, 4) as i:
                    for e in range(2):
                        unit(count(U_FF + e, (part, 16), (i, 2)), HH, HL, G1, ready=(ap_lo, KC))
                        ada_unit(count(KC + e, (part, 8), (i, 2)))

            def ff_down(part):
                with pe.Fori(0, 4) as i:
                    for e in range(2):
                        pe.wait_ge(ff_lo, val(count(8, (part, 8))))
                        unit(count(U_FF + 8 + e, (part, 16), (i, 2)), BH, BL, G1)

            with pe.Fori(0, FF1 // D - 1) as part:
                ff_up(part)
                ff_down(part)
            ff_up(FF1 // D - 1)
            pe.wait_ge(ctx_in, 32)
            for c in range(KC):
                if c >= 2:
                    pe.wait_ge(ctx_out, val(c - 1))
                for t in range(2):
                    last = tr(A[c % 2][:, P * t:P * t + P], ctxr[t][:, P * c:P * (c + 1)])
                last.then_inc(ctx_done, 1)
            ff_down(FF1 // D - 1)
            pe.wait_ge(ctx_out, KC)
            sum_squares(ssq, G1)

            sum_squares(ss2, G2)

            def swiglu(base, geo, ap0, f0):
                with pe.Fori(0, 2) as part:
                    with pe.Fori(0, 8) as n:
                        for e in range(2):
                            unit(Count(base + e, (part, 24), (n, 2)), H2H, H2L, geo,
                                 ready=(ap_lo, ap0) if e == 0 else None)
                    with pe.Fori(0, 4) as i:
                        for e in range(2):
                            pe.wait_ge(ff_lo, val(Count(f0 + 8, (part, 8))))
                            unit(Count(base + 16 + e, (part, 24), (i, 2)), UH2, UL2, geo)
                with pe.Fori(0, 6) as n:
                    for e in range(2):
                        unit(Count(base + 48 + e, (n, 2)), H2H, H2L, geo)
                with pe.Fori(0, 4) as i:
                    for e in range(2):
                        pe.wait_ge(ff_lo, f0 + 22)
                        unit(Count(base + 60 + e, (i, 2)), UH2, UL2, geo, kc=6)

            swiglu(U_FA, G2, 2 * KC, 32)
            sum_squares(ss2, G2)
            sum_squares(ss2, G2)

            def na_pair(i, p, last_pair):
                u = turn(i, U_NA + 3 * p, 6)
                nq, nk = nqs[p], nks[p]

                def fill(k, k0, k1):
                    unit(u + 3 + k, H2H, H2L, G2 if k or last_pair else GL, n=QK if k == 2 and last_pair else P,
                         part=(k0, k1))

                def token_v(half):
                    for j in (range(5) if half == 0 else range(5, NV + 2)):
                        a = CTX + V_STARTS[j] if j < NV else P * (j - NV)
                        b = j if half == 0 else j - 5
                        last = tr(A[1][:, P * b:P * b + P], nvT[:, a:a + P])
                    last.then_inc(n_vt, 1)

                def at_(s):
                    return turn(i, s + 8 * p, 16)

                def qk(s):
                    e, t = divmod(s, NT)
                    if s >= 2:
                        pe.wait_ge(n_exp, val(at_(s - 1)))
                    r = slice(64 * e, 64 * e + 64)
                    a = CTX + NA_START[t]
                    q = nq[r, P * t:P * t + P]
                    b = 512 * (s % 2)
                    pe.matmul(A[0][:, b:b + 256], q, nk[r, a:a + 256], start=True, stop=True)
                    pe.matmul(A[0][:, b + 256:b + 512], q, nk[r, 0:CTX], start=True, stop=True).then_inc(n_qk, 1)

                def transpose_p(s):
                    pe.wait_ge(n_exp, val(at_(s + 1)))
                    if s:
                        pe.wait_ge(n_at, val(at_(s)))
                    for j in range(4):
                        last = tr(A[1][:, P * j:P * j + P], nP[s % 2][:, P * j:P * j + P])
                    last.then_inc(n_tr, 1)

                def pv(s):
                    e, t = divmod(s, NT)
                    pe.wait_ge(n_at, val(at_(s + 1)))
                    if s:
                        pe.wait_ge(n_o, val(at_(s + 1)))
                    v0 = NA_START[t] // 64
                    for j, v in enumerate((v0, v0 + 2, NV, NV + 1)):
                        last = pe.matmul(A[1][:, 512:512 + NA_HD], nT[s % 2][:, j, :], nV[:, v, 64 * e:64 * e + 64],
                                         start=(j == 0), stop=(j == 3))
                    last.then_inc(n_pv, 1)

                for k in range(2):
                    pe.wait_ge(evicted[(u + k).slot], val((u + k).turns() + 2))
                qk(0)
                qk(1)
                pe.wait_ge(evicted[u.slot], val((u + 2).turns() + 2))
                pe.wait_ge(n_o, val(at_(0) + 1))
                token_v(0)
                fill(0, 0, 2)
                pe.wait_ge(n_v, val(turn(i, 1 + 2 * p, 4)))
                token_v(1)
                fill(0, 2, 4)
                pe.wait_ge(n_v, val(turn(i, 2 + 2 * p, 4)))
                pieces = ((0, 4, 6), (0, 6, 8), (1, 0, 2), (1, 2, 4), (1, 4, 6), (1, 6, 8), (2, 0, 2), (2, 2, 5))
                for s in range(8):
                    transpose_p(s)
                    if s:
                        pv(s - 1)
                    if s < 6:
                        qk(s + 2)
                    fill(*pieces[s])
                pv(7)
                fill(2, 5, 8)

            for c in range(KC):
                for k in range(2):
                    unit(Count(U_NA + k), H2H, H2L, G2 if k else GL, ready=None if k else (ap_lo, 3 * KC),
                         part=(c, c + 1))
            unit(Count(U_NA + 2), H2H, H2L, G2)
            with pe.Fori(0, NA_H // 4 - 1) as i:
                for p in range(2):
                    na_pair(i, p, False)
            for p in range(2):
                na_pair(NA_H // 4 - 1, p, p == 1)
            pe.wait_ge(n_o, 32 + 1)
            for c in range(4):
                if c >= 2:
                    pe.wait_ge(n_lo, val(c - 1))
                for t in range(NT):
                    last = tr(A[c % 2][:, P * t:P * t + P], nO[:, t, P * c:P * c + P])
                last.then_inc(n_ot, 1)

            unit(Count(U_LORA + 3), H2H, H2L, GL)
            pe.wait_ge(n_lo, 4)
            sum_squares(ss2, G2)
            for k in range(1, 6):
                unit(Count(U_LORA + 3 + k), H2H, H2L, GL)
            pe.wait_ge(k_kr, 1)
            pe.matmul(A[1][0:QK, 0:SEQ], cst("rot", 0, QK), mkr[0:QK, CTX:T2], start=True, stop=True).then_inc(k_rot, 1)
            sum_squares(ss2, GS)
            def mla_ready(u, e, head):
                pe.wait_ge(evicted[u.slot], val(u.turns() + 2))
                pe.matmul(A[1][0:QK, 0:SEQ], cst("rot", 0, QK), mqs[e][0:QK, :], start=True, stop=True).then_inc(k_rot, 1)
                pe.wait_ge(evicted[(u + 1).slot], val((u + 1).turns() + 2))
                if head:
                    pe.wait_ge(k_o, val(head))
                alone(pe, pe_passed)
                for j in range(6):
                    last = tr(A[1][:, 512 + VD * j:512 + VD * j + VD], mvT[64:P, P * j:P * j + P], 64, 64)
                last.then_inc(k_vt, 1)

            def mla_head(i, e, more):
                u = turn(i, U_MLA + 2 * e, 4)
                mq, mk = mqs[e], mks[e]

                def cnt(k):
                    return turn(i, k + NT * e, 2 * NT)

                def fill_q(k0, k1):
                    if more:
                        unit(u + 2, CQH, CQL, GS, kc=6, n=QK, part=(k0, k1))

                def fill_kv(k0, k1):
                    if more:
                        unit(u + 3, CKH, CKL, G2, kc=2, part=(k0, k1))

                def qk(t):
                    if t:
                        pe.wait_ge(k_exp, val(cnt(t)))
                    for a, m in ((0, 512), (512, T2 - 512)):
                        last = pe.matmul(A[0][:, a:a + m], mq[0:QK, P * t:P * t + P], mk[0:QK, a:a + m],
                                         start=True, stop=True)
                    last.then_inc(k_qk, 1)

                def transpose_p(t):
                    pe.wait_ge(k_exp, val(cnt(t + 1)))
                    if t:
                        pe.wait_ge(k_ad, val(cnt(t)))
                        pe.wait_ge(k_at, val(cnt(t)))
                    if t > 1:
                        pe.wait_ge(k_o, val(cnt(t - 1)))
                    for j in (4, 5):
                        last = tr(A[1][:, P * j:P * j + P], mP[t % 2][:, P * j:P * j + P])
                    last.then_inc(k_tr1, 1)
                    for j in range(4):
                        last = tr(A[1][:, P * j:P * j + P], mP[t % 2][:, P * j:P * j + P])
                    last.then_inc(k_tr, 1)

                def pv(t):
                    pe.wait_ge(k_at, val(cnt(t + 1)))
                    pe.wait_ge(k_ad, val(cnt(min(t + 2, NT))))
                    for j in range(6):
                        last = pe.matmul(A[1][:, 768:768 + VD], mT[t % 2][:, j, :], mV[:, j, :],
                                         start=(j == 0), stop=(j == 5))
                    last.then_inc(k_pv, 1)

                pe.wait_ge(k_q, val(turn(i, 1 + e, 2)))
                qk(0)
                fill_q(0, 2)
                pe.wait_ge(k_v, val(turn(i, 1 + e, 2)))
                qk(1)
                fill_q(2, 3)
                transpose_p(0)
                qk(2)
                fill_q(3, 5)
                transpose_p(1)
                pv(0)
                qk(3)
                fill_q(5, 6)
                transpose_p(2)
                pv(1)
                fill_kv(0, 1)
                transpose_p(3)
                fill_kv(1, 2)
                pv(2)
                pe.wait_ge(k_o, val(cnt(NT - 1)))
                pv(3)
                if more:
                    mla_ready(u + 2, 1 - e, cnt(NT))

            unit(Count(U_MLA), CQH, CQL, GS, kc=6, n=QK, ready=(ap_lo, 4 * KC + 2))
            unit(Count(U_MLA + 1), CKH, CKL, G2, kc=2)
            mla_ready(Count(U_MLA), 0, None)
            with pe.Fori(0, 3) as i:
                for e in range(2):
                    mla_head(i, e, True)
            for e in range(2):
                mla_head(3, e, e == 0)
            pe.wait_ge(k_o, 32)
            for c in range(4):
                if c >= 2:
                    pe.wait_ge(k_lo, val(c - 1))
                for t in range(NT):
                    last = tr(A[c % 2][:, P * t:P * t + P], mO[:, t, P * c:P * c + P])
                last.then_inc(k_ot, 1)

            with pe.Fori(0, KC) as n:
                u = Count(U_GATE, (n, 4))
                unit(u, H2H, H2L, GL)
                unit(u + 1, NA_OH, NA_OL, GS, kc=4)
                unit(u + 2, H2H, H2L, GL)
                pe.wait_ge(k_lo, 4)
                unit(u + 3, ML_OH, ML_OL, GS, kc=4)
            with pe.Fori(0, 4) as i:
                for e in range(2):
                    unit(Count(U_OUT2 + e, (i, 2)), MH2, ML2, GS, ready=(m_lo, KC))
            sum_squares(ss2, GL)
            sum_squares(ss2, GL)
            swiglu(U_FB, GL, 4 * KC + 8, 32 + 22)
            sum_squares(ss2, GL)

            for c in range(KC):
                pe.wait_ge(x2_out, 3 * KC + c + 1)
                for t in range(2):
                    last = tr(A[t][:, P * c:P * c + P], X2[:, c, CTX + P * t:CTX + P * t + P])
                    if c == KC - 1:
                        last.then_inc(o_tr, 1)
            for t in range(2, NT):
                pe.wait_ge(o_cp, t - 1)
                for c in range(KC):
                    last = tr(A[t % 2][:, P * c:P * c + P], X2[:, c, CTX + P * t:CTX + P * t + P])
                last.then_inc(o_tr, 1)

        @block.scalar
        def _(act):
            for s in range(2):
                act.sem_inc(evicted[s], 1)

            def split(v, kc=KC):
                act.drain()
                landed(act, v)
                if v.terms or v.base >= 2:
                    act.wait_ge(unit_done, val(v + (-1)))
                act.activation(wh[v.slot][:, 0:kc, :], raw[v.slot][:, 0:kc, :], ACT.Copy).then_inc(hi_split, 1)

            def done(u):
                act.drain()
                act.wait_ge(unit_done, val(u + 1))

            nsq, nroot, nap = [0], [0], [0]

            def square(chunk, buf, n):
                if nsq[0] >= 2:
                    act.wait_ge(nrm_add, val(nsq[0] - 1))
                act.activation(buf[nsq[0] % 2][:, 0:n], chunk, ACT.Square).then_inc(nrm_sq, 1)
                nsq[0] += 1

            def square_in_turn(chunk, buf, n, i, e):
                act.wait_ge(nrm_add, val(turn(i, nsq[0] - 1 + e, 2)))
                alone(act, act_passed)
                act.activation(buf[(nsq[0] + e) % 2][:, 0:n].unsqueeze(1), chunk, ACT.Square).then_inc(nrm_sq, 1)

            def root(dst, geo, features):
                nroot[0] += 1
                act.drain()
                act.wait_ge(nrm_sum, nroot[0])
                n0 = geo[0][0]
                n1 = geo[-1][0] + geo[-1][1]
                v = dst[:, n0:n1]
                act.activation(like(v, geo), acc(A[0], geo), ACT.Ln, bias=eps_col, scale=1.0 / features)
                act.drain()
                act.activation(v, v, ACT.Exp, scale=-0.5).then_inc(nrm_root, 1)

            def hi_part(dst, src):
                nap[0] += 1
                act.wait_ge(ap_tmp, nap[0])
                act.activation(dst, src, ACT.Copy).then_inc(ap_hi, 1)

            act.wait_ge(cols_out, 1)
            c2 = col_a[:, 49:65].rearrange("p (e k) -> p k e", e=2)
            act.activation(silu_c[:, :, :], c2, ACT.Silu).then_inc(cols_act, 1)
            act.wait_ge(lam_dve, 1)
            act.activation(small[:, 4:6], small[:, 2:4], ACT.Exp).then_inc(lam_act, 1)
            for v in range(2):
                split(Count(v))
            for c in range(KC):
                act.wait_ge(xT_out, c + 1)
                square(X[:, c, :], sqb, T1)
            root(rstd, G1, D)
            for c in range(KC):
                hi_part(HH[:, c, :], tmp[c % 2][:, :])

            with act.Fori(0, RET_H) as h:
                u = Count(U_RET, (h, 6))
                for k, dst in enumerate((rq, rk, rvT[0], rvT[1])):
                    done(u + k)
                    act.activation(two(dst[:, :], T1 // 2), acc(G[k % 2], G1), ACT.Copy).then_inc(evicted[k % 2], 1)
                    split(u + k + 2)
                act.wait_ge(r_vt, val(Count(1, (h, 1))))
                act.activation(rV[:, 1:5, :], A[0][:, :].rearrange("p (t n) -> p t n", t=4), ACT.Copy)
                act.activation(rV[0:META, 0, :], A[1][0:META, 0:RET_DV], ACT.Copy).then_inc(r_v, 1)
                for k in (4, 5):
                    done(u + k)
                    act.activation(two(rg[k - 4][:, :], T1 // 2), acc(G[k % 2], G1), ACT.Silu).then_inc(
                        evicted[k % 2], 1)
                    split(u + k + 2)
                for half in range(2):
                    act.wait_ge(r_tmp, val(Count(half + 1, (h, 2))))
                    act.activation(BH[:, bass.ds(h * 2 + half, 1), :], tmp[half][:, :].unsqueeze(1),
                                   ACT.Copy).then_inc(r_hi, 1)

            def merge(r):
                with act.Fori(0, KC) as n:
                    u = Count(U_BR[r], (n, 2))
                    done(u)
                    act.wait_ge(evicted[(u + -1).slot], val((u + -1).turns() + 2))
                    act.activation(two(sg[0][:, :], T1 // 2), acc(G[u.slot], G1), ACT.Sigmoid).then_inc(
                        evicted[u.slot], 1)
                    split(u + 2)
                    split(u + 3)
                    if r == 2:
                        act.wait_ge(mg_add, val(Count(1, (n, 1))))
                        act.activation(MH[:, bass.ds(n, 1), :], MG[:, bass.ds(n, 1), :], ACT.Copy).then_inc(mg_hi, 1)

            merge(0)

            def diff_project(u, k, e):
                v = u + k
                done(v)
                act.activation(two((dqs[e], dks[e], dvT)[k][:, :], T1 // 2), acc(G[v.slot], G1),
                               ACT.Copy).then_inc(evicted[v.slot], 1)
                split(v + 2)

            def diff_head(i, e, more):
                u = turn(i, U_DIFF + 3 * e, 6)

                def cnt(k):
                    return turn(i, k + 5 * e, 10)

                def next_head(k):
                    if more:
                        diff_project(u + 3, k, 1 - e)

                def exps(t):
                    q0, n = TILES[t]
                    act.drain()
                    act.wait_ge(d_log, val(cnt(5 - t)))
                    for m in range(2):
                        p = dL[t % 2][m][0:n, 0:q0 + n]
                        last = act.activation(p, p, ACT.Exp, bias=dnb[0:n, t % 2, m:m + 1], scale=0.125,
                                              accum_out=dsum[0:n, t % 2, m:m + 1])
                    last.then_inc(d_exp, 1)

                def copy_pT(t):
                    q0, n = TILES[t]
                    act.drain()
                    act.wait_ge(d_tr, val(cnt(5 - t)))
                    last = act.activation(dT[t % 2][0:META, 0, 0:n], meta_pT(t, n), ACT.Copy)
                    if t:
                        last = act.activation(dT[t % 2][:, 1:t + 1, :],
                                              A[1][:, 512:512 + P * t].rearrange("p (c n) -> p c n", n=P), ACT.Copy)
                    last.then_inc(d_at, 1)

                def out_o(t):
                    q0, n = TILES[t]
                    act.drain()
                    act.wait_ge(d_pv, val(cnt(5 - t)))
                    act.activation(dO[0:n, t, :], A[1][0:n, 256:384], ACT.Copy)
                    act.activation(dsq[0:n, :], A[1][0:n, 256:384], ACT.Square,
                                   accum_out=dss[0:n, t:t + 1]).then_inc(d_o, 1)

                head = i * 2 + e
                act.drain()
                act.activation(dR[:, :], rel[:, :], ACT.Copy,
                               scale=cst("slope8")[:, bass.ds(head, 1)]).then_inc(d_bias, 1)
                exps(4)
                act.drain()
                act.wait_ge(d_vt, val(turn(i, 1 + e, 2)))
                act.activation(dV[0:META, 0, :], A[1][0:META, P:2 * P], ACT.Copy)
                act.activation(dV[:, 1:5, :], A[1][:, 512:1024].rearrange("p (c n) -> p c n", n=P),
                               ACT.Copy).then_inc(d_v, 1)
                exps(3)
                next_head(0)
                copy_pT(4)
                exps(2)
                out_o(4)
                copy_pT(3)
                exps(1)
                out_o(3)
                copy_pT(2)
                exps(0)
                out_o(2)
                copy_pT(1)
                out_o(1)
                copy_pT(0)
                out_o(0)
                next_head(1)
                act.wait_ge(d_ot, val(turn(i, 1 + e, 2)))
                act.activation(BH[:, bass.ds(head, 1), META:T1], A[0][:, 0:SEQ].unsqueeze(1), ACT.Copy,
                               scale=small[:, 0:1])
                act.activation(BH[:, bass.ds(head, 1), 0:META], A[1][:, 0:META].unsqueeze(1), ACT.Copy,
                               scale=small[:, 0:1]).then_inc(d_hi, 1)
                next_head(2)

            act.wait_ge(rel_in, 16)
            for k in range(3):
                diff_project(Count(U_DIFF), k, 0)
            with act.Fori(0, DIFF_H // 2 - 1) as i:
                for e in range(2):
                    diff_head(i, e, True)
            for e in range(2):
                diff_head(DIFF_H // 2 - 1, e, e == 0)
            merge(1)

            with act.Fori(0, KC // 2) as i:
                for e in range(2):
                    u = Count(U_CONV + 3 * e, (i, 6))
                    for k, dst in enumerate((cb, cc)):
                        s = (u + k).slot
                        done(u + k)
                        act.activation(two(dst[:, :], T1 // 2), acc(G[s], G1), ACT.Copy).then_inc(evicted[s], 1)
                        split(u + k + 2)
                    split(u + 4)
                    act.wait_ge(c_y, val(Count(1 + e, (i, 2))))
                    act.activation(BH[:, bass.ds(i * 2 + e, 1), :], cy[:, :].unsqueeze(1), ACT.Copy).then_inc(c_hi, 1)
            merge(2)

            for n in range(KC):
                u = Count(U_OUT + n)
                split(u + 2)
                act.wait_ge(evicted[u.slot], val(u.turns() + 2))
                square(X[:, n, :], sqb, T1)
            root(rstd, G1, D)
            for c in range(KC):
                hi_part(HH[:, c, :], tmp[c % 2][:, :])

            def ff_up(part):
                with act.Fori(0, 4) as i:
                    for e in range(2):
                        u = count(U_FF + e, (part, 16), (i, 2))
                        done(u)
                        act.activation(two(sqb[0][:, :], T1 // 2), acc(G[u.slot], G1), ACT.Relu).then_inc(ff_r, 1)
                        split(u + 2)
                        act.wait_ge(evicted[u.slot], val(u.turns() + 2))
                        act.activation(BH[:, bass.ds(i * 2 + e, 1), :], sqb[1][:, :].unsqueeze(1),
                                       ACT.Copy).then_inc(ff_hi, 1)

            with act.Fori(0, FF1 // D - 1) as part:
                ff_up(part)
                with act.Fori(0, 4) as i:
                    for e in range(2):
                        split(Count(U_FF + 10 + e, (part, 16), (i, 2)))
            ff_up(FF1 // D - 1)
            act.drain()
            with act.Fori(0, 4) as i:
                for e in range(2):
                    u = Count(U_FA - 8 + e, (i, 2))
                    split(u + 2)
                    act.wait_ge(evicted[u.slot], val(u.turns() + 2))
                    square_in_turn(X[:, bass.ds(i * 2 + e, 1), :], sqb, T1, i, e)
            nsq[0] += KC
            root(rstd, G1, D)

            def squares2(src, n0, ready):
                act.drain()
                act.wait_ge(ap_lo, nap[0])
                for c in range(KC):
                    ready(c)
                    square(src[:, c, n0:T2], tm2, T2 - n0)

            def modulate(i, shift, n0):
                for c in range(KC):
                    t = tm2[c % 2]
                    act.wait_ge(ap_tmp, nap[0] + 1)
                    for e, (a, b) in enumerate(((CTX, T2), (0, CTX))):
                        if a >= n0:
                            v = t[:, a:b]
                            act.activation(v, v, ACT.Identity, bias=ada[:, shift * KC + c, e:e + 1],
                                           scale=gain[i][:, c, e:e + 1])
                    act.drain()
                    hi_part(H2H[:, c, n0:T2], t[:, n0:T2])

            def both_chunks(c):
                act.wait_ge(x2_out, c + 1)
                act.wait_ge(ctx_out, c + 1)

            squares2(X2, 0, both_chunks)
            root(rs2, G2, D)
            modulate(0, 0, 0)

            def swiglu(base, geo, n0, f0, final):
                g0 = geo[0][0]

                def up(u, n):
                    done(u)
                    act.activation(like(tm2[0][:, n0:T2], geo), acc(G[u.slot], geo), ACT.Silu).then_inc(
                        evicted[u.slot], 1)
                    split(u + 2)
                    split(u + 3)
                    act.wait_ge(evicted[(u + 1).slot], val((u + 1).turns() + 2))
                    act.activation(UH2[:, bass.ds(n, 1), n0:T2], tm2[1][:, n0:T2].unsqueeze(1),
                                   ACT.Copy).then_inc(ff_hi, 1)

                act.wait_ge(ap_lo, nap[0])
                with act.Fori(0, 2) as part:
                    with act.Fori(0, 8) as n:
                        up(Count(base, (part, 24), (n, 2)), n)
                    with act.Fori(0, 4) as i:
                        for e in range(2):
                            split(Count(base + 18 + e, (part, 24), (i, 2)))
                with act.Fori(0, 6) as n:
                    up(Count(base + 48, (n, 2)), n)
                act.drain()

                def final_chunk(i, e, more):
                    u = turn(i, base + 60 + e, 2)
                    if more:
                        split(u + 2)
                    act.wait_ge(evicted[u.slot], val(u.turns() + 2))
                    square_in_turn(Y2[:, bass.ds(i * 2 + e, 1), n0:T2], tm2, T2 - n0, i, e)

                with act.Fori(0, 3 if final else 4) as i:
                    for e in range(2):
                        final_chunk(i, e, True)
                if final:
                    for e in range(2):
                        final_chunk(3, e, False)
                nsq[0] += KC

            swiglu(U_FA, G2, 0, 32, False)
            root(rs2, G2, D)
            squares2(X2, 0, lambda c: act.wait_ge(x2_out, KC + c + 1))
            root(rs2, G2, D)
            modulate(1, 3, 0)

            def na_project(u, k, p):
                v = u + k
                dst, geo = ((nqs[p], GL), (nks[p], G2), (nvT, G2))[k]
                done(v)
                act.activation(like(dst[:, :], geo), acc(G[v.slot], geo), ACT.Copy).then_inc(evicted[v.slot], 1)
                split(v + 2)

            def low_rank_project(k):
                v = Count(U_LORA + k)
                done(v)
                if k < 2:
                    act.activation(two(ckvT[:, k, :], T2 // 2), acc(G[v.slot], G2), ACT.Copy).then_inc(
                        evicted[v.slot], 1)
                else:
                    act.activation(two(mkr[:, :], T2 // 2)[0:QK], acc(G[v.slot], G2, QK), ACT.Copy).then_inc(
                        evicted[v.slot], 1)
                    act.drain().then_inc(k_kr, 1)
                split(v + 2)

            def na_pair(i, p, last_pair):
                def project_next(k):
                    if last_pair:
                        low_rank_project(k)
                    else:
                        na_project(turn(i, U_NA + 3 * p + 3, 6), k, 1 - p)

                for s in range(8):
                    act.drain()
                    act.wait_ge(n_log, val(turn(i, s + 1 + 8 * p, 16)))
                    b = s % 2
                    act.activation(nP[b][:, 0:256], nP[b][:, 0:256], ACT.Exp, bias=nst[:, b, 3:4], scale=0.125,
                                   accum_out=nst[:, b, 4:5])
                    act.activation(nP[b][:, 256:512], A[0][:, 512 * b + 256:512 * b + 512], ACT.Exp,
                                   bias=nst[:, b, 3:4], scale=0.125, accum_out=nst[:, b, 5:6]).then_inc(n_exp, 1)
                    if s in (4, 7):
                        project_next(s // 5)
                project_next(2)

            for k in range(3):
                na_project(Count(U_NA), k, 0)
            with act.Fori(0, NA_H // 4 - 1) as i:
                for p in range(2):
                    na_pair(i, p, False)
            for p in range(2):
                na_pair(NA_H // 4 - 1, p, p == 1)
            for c in range(4):
                act.wait_ge(n_ot, c + 1)
                act.activation(NA_OH[:, c, :], A[c % 2][:, 0:SEQ], ACT.Copy).then_inc(n_hi, 1)

            def lora_square(src, n):
                act.drain()
                square(src, tm2, n)

            for k in range(2):
                lora_square(ckvT[:, k, :], T2)
            root(rs2, G2, KVR)
            for k in range(2):
                hi_part(CKH[:, k, :], tm2[k % 2][:, :])
            for k in range(6):
                u = Count(U_LORA + 3 + k)
                done(u)
                act.activation(cqT[:, k, :], acc(G[u.slot], GS), ACT.Copy).then_inc(evicted[u.slot], 1)
                split(u + 2)
                if k == 0:
                    act.wait_ge(ap_lo, nap[0])
                lora_square(cqT[:, k, :], SEQ)
            root(rs2, GS, QR)
            for k in range(6):
                hi_part(CQH[:, k, :], tm2[k % 2][:, 0:SEQ])

            def mla_q(u, e, kc):
                done(u)
                act.activation(mqs[e][0:QK, :], acc(G[u.slot], GS, QK), ACT.Copy).then_inc(evicted[u.slot], 1)
                split(u + 2, kc)

            def mla_kv(u, e, kc):
                done(u)
                s = u.slot
                act.activation(two(mks[e][:, :], T2 // 2)[0:NOPE], acc(G[s], G2, NOPE), ACT.Copy)
                act.activation(two(mvT[:, :], T2 // 2)[NOPE:P], acc(G[s], G2, P, NOPE), ACT.Copy).then_inc(evicted[s], 1)
                split(u + 2, kc)

            def mla_head(i, e, more):
                u = turn(i, U_MLA + 2 * e, 4)
                kq, kkv = (KC, 4) if isinstance(i, int) else (6, 2)

                def exps(t):
                    b = t % 2
                    act.drain()
                    act.wait_ge(k_log, val(turn(i, t + 1 + NT * e, 2 * NT)))
                    act.activation(mP[b][:, :], A[0][:, 0:T2], ACT.Exp, bias=mst[:, b, 1:2], scale=QK ** -0.5,
                                   accum_out=mst[:, b, 2:3]).then_inc(k_exp, 1)

                exps(0)
                for t in range(NT):
                    if t < NT - 1:
                        exps(t + 1)
                    act.wait_ge(k_tr, val(turn(i, t + 1 + NT * e, 2 * NT)))
                    act.activation(mT[t % 2][:, 0:4, :], A[1][:, 0:512].rearrange("p (c n) -> p c n", n=P),
                                   ACT.Copy).then_inc(k_at, 1)
                    if more and t == 2:
                        mla_q(u + 2, 1 - e, kq)
                if more:
                    mla_kv(u + 3, 1 - e, kkv)

            mla_q(Count(U_MLA), 0, 6)
            mla_kv(Count(U_MLA + 1), 0, 2)
            with act.Fori(0, 3) as i:
                for e in range(2):
                    mla_head(i, e, True)
            for e in range(2):
                mla_head(3, e, e == 0)
            for c in range(4):
                act.wait_ge(k_ot, c + 1)
                act.activation(ML_OH[:, c, :], A[c % 2][:, 0:SEQ], ACT.Copy).then_inc(k_hi, 1)

            with act.Fori(0, KC) as n:
                u = Count(U_GATE, (n, 4))
                for k in range(2):
                    v = u + 2 * k
                    split(v + 2)
                    done(v)
                    act.activation(sgl[k][:, :], acc(G[v.slot], GS), ACT.Sigmoid,
                                   bias=col_b[:, bass.ds(n + (48 + KC * k), 1)]).then_inc(evicted[v.slot], 1)
                    split(v + 3, KC if k else 4)
                act.wait_ge(mg_add, val(Count(KC + 1, (n, 1))))
                act.activation(MH2[:, bass.ds(n, 1), :], tm2[0][:, 0:SEQ].unsqueeze(1), ACT.Copy).then_inc(mg_hi, 1)
            with act.Fori(0, 4) as i:
                for e in range(2):
                    u = Count(U_OUT2 + e, (i, 2))
                    done(u)
                    act.activation(Y2[:, bass.ds(i * 2 + e, 1), CTX:T2], acc(G[u.slot], GS).unsqueeze(1),
                                   ACT.Copy).then_inc(evicted[u.slot], 1)
                    split(u + 2)
                    act.drain()
                    square_in_turn(Y2[:, bass.ds(i * 2 + e, 1), CTX:T2], tm2, SEQ, i, e)
            nsq[0] += KC
            root(rs2, GL, D)
            squares2(X2, CTX, lambda c: act.wait_ge(x2_out, 2 * KC + c + 1))
            root(rs2, GL, D)
            modulate(2, 6, CTX)
            swiglu(U_FB, GL, CTX, 54, True)
            root(rs2, GL, D)

        @block.gpsimd
        def _(pool):
            pool.wait_ge(const_in, 16)
            with pool.Fori(0, RET_H) as h:
                pool.wait_ge(r_var, val(Count(1, (h, 1))))
                pool.tensor_tensor(rpow[:, :], rvar[:, :], minus_half[:, 0:5], ALU.pow).then_inc(r_pow, 1)
            with pool.Fori(0, DIFF_H) as h:
                pool.wait_ge(d_ss, val(Count(1, (h, 1))))
                pool.tensor_tensor(dpow[:, :], dss2[:, :], minus_half[:, 0:5], ALU.pow).then_inc(d_pow, 1)
            pool.wait_ge(x2_out, KC)
            pool.memset(rpbT[:, :, :], 0.0).then_inc(rpb_zero, 1)
            pool.memset(Y2[:, :, :], 0.0).then_inc(y_zero, 1)
            pool.wait_ge(n_tab, 1)
            for e in range(2):
                pool.tensor_copy(nBs[e][:, :, :], nB[:, :, e, :]).then_inc(n_bias, 1)
            with pool.Fori(0, NA_H // 2 - 1) as p:
                for e in range(2):
                    pool.wait_ge(n_log, val(Count(4 * e + 4, (p, 8))))
                    pool.tensor_copy(nBs[e][:, :, :], nB[:, :, bass.ds(p * 2 + (2 + e), 1), :].rearrange(
                        "p k a n -> p k (a n)")).then_inc(n_bias, 1)
            pool.wait_ge(x2_out, 3 * KC)
            pool.memset(Y2[:, :, CTX:T2], 0.0).then_inc(y_zero, 1)

        @block.vector
        def _(dve):
            def split(v, kc=KC):
                dve.wait_ge(hi_split, val(v + 1))
                s = v.slot
                dve.tensor_tensor(wl[s][:, 0:kc, :], raw[s][:, 0:kc, :], wh[s][:, 0:kc, :].bitcast(F32),
                                  ALU.subtract).then_inc(lo_split, 1)

            def done(u):
                dve.drain()
                dve.wait_ge(unit_done, val(u + 1))

            nsq, nroot, nap = [0], [0], [0]

            def add_square(dst, buf, n, first):
                b = buf[nsq[0] % 2][:, 0:n]
                nsq[0] += 1
                dve.drain()
                dve.wait_ge(nrm_sq, nsq[0])
                if first:
                    dve.tensor_copy(dst, b).then_inc(nrm_add, 1)
                else:
                    dve.tensor_tensor(dst, dst, b, ALU.add).then_inc(nrm_add, 1)

            def add_in_turn(dst, buf, n, i, e):
                dve.drain()
                dve.wait_ge(nrm_sq, val(turn(i, nsq[0] + 1 + e, 2)))
                dve.tensor_tensor(dst, dst, buf[(nsq[0] + e) % 2][:, 0:n], ALU.add).then_inc(nrm_add, 1)

            def rooted():
                nroot[0] += 1
                dve.drain()
                dve.wait_ge(nrm_root, nroot[0])

            def scaled(chunks, bufs, hi, lo, scale):
                n0 = nap[0]

                def low(c):
                    dve.wait_ge(ap_hi, n0 + c + 1)
                    dve.tensor_tensor(lo(c), bufs(c), hi(c).bitcast(F32), ALU.subtract).then_inc(ap_lo, 1)

                for c in range(chunks):
                    if c >= 2:
                        dve.drain()
                    scale(c, bufs(c)).then_inc(ap_tmp, 1)
                    if c >= 1:
                        low(c - 1)
                low(chunks - 1)
                nap[0] += chunks
                dve.drain()

            dve.memset(bag[:, :, :], 1.0)
            dve.memset(ada[:, ADA_BOTH:, 1], 0.0)
            dve.sem_inc(ada_used, 2)
            dve.sem_inc(ada_out, 1)
            dve.wait_ge(cols_done, 1)
            dve.tensor_copy(col_a[:, :], A[0][:, 0:65])
            dve.tensor_copy(col_b[:, :], A[0][:, 128:200])
            dve.tensor_copy(col_c[:, :], A[0][:, 256:328]).then_inc(cols_out, 1)
            dve.wait_ge(lam_in, 16)
            dve.tensor_tensor(lam_p[:, :, :], lam_v[:, 0:4:2, :], lam_v[:, 1:4:2, :], ALU.mult)
            dve.drain()
            dve.tensor_reduce(small[:, 2:4], lam_p[:, :, :], AX, ALU.add).then_inc(lam_dve, 1)
            dve.tensor_scalar(small[:, 0:1], col_a[:, 48:49], 1.0 - LAM_INIT, None, ALU.mult)
            dve.wait_ge(lam_act, 1)
            dve.scalar_tensor_tensor(out=small[:, 1:2], in0=small[:, 4:5], scalar=LAM_INIT, in1=small[:, 5:6],
                                     op0=ALU.add, op1=ALU.subtract)
            for v in range(2):
                split(Count(v))
            for c in range(KC):
                dve.wait_ge(xT_done, c + 1)
                dve.tensor_copy(X[:, c, META:T1], A[c % 2][:, 0:SEQ])
                dve.tensor_copy(X[:, c, 0:META], A[c % 2][:, SEQ:T1]).then_inc(xT_out, 1)
                if c >= 1:
                    add_square(ssq[:, :], sqb, T1, c == 1)
            add_square(ssq[:, :], sqb, T1, False)
            rooted()

            def weighted(col):
                return lambda c, b: dve.scalar_tensor_tensor(out=b, in0=X[:, c, :], scalar=col_a[:, col + c:col + c + 1],
                                                             in1=rstd[:, :], op0=ALU.mult, op1=ALU.mult)

            scaled(KC, lambda c: tmp[c % 2][:, :], lambda c: HH[:, c, :], lambda c: HL[:, c, :], weighted(0))

            dve.wait_ge(decay_in, 16)
            with dve.Fori(0, RET_H) as h:
                u = Count(U_RET, (h, 6))
                split(u + 2)
                split(u + 3)
                for c, (q0, n) in enumerate(TILES):
                    dve.wait_ge(r_sc, val(Count(c + 1, (h, 5))))
                    w = ST_W[c]
                    dve.tensor_tensor(rST[0:n, ST_AT[c]:ST_AT[c] + w], A[c % 2][0:n, 0:w],
                                      DT[0:n, bass.ds(h, 1), 0:w].rearrange("p a n -> p (a n)"),
                                      ALU.mult).then_inc(r_st, 1)
                split(u + 4)
                split(u + 5)
                dve.drain()
                dve.wait_ge(r_pv, val(Count(1, (h, 1))))

                def head_psum(t, n):
                    return A[1][0:n, 0:RET_DV] if t == 0 else A[0][:, (t - 1) * RET_DV:t * RET_DV]

                for t, (q0, n) in enumerate(TILES):
                    dve.bn_stats(bst[0:n, t, :], head_psum(t, n))
                dve.drain()
                for t, (q0, n) in enumerate(TILES):
                    dve.bn_aggr(bag[0:n, t, :], bst[0:n, t, :])
                dve.drain()
                dve.tensor_scalar(rvar[:, :], bag[:, :, 1], EPS, None, ALU.add).then_inc(r_var, 1)
                split(u + 6)
                dve.wait_ge(r_pow, val(Count(1, (h, 1))))
                for t, (q0, n) in enumerate(TILES):
                    last = dve.tensor_scalar(rY[0:n, t, :], head_psum(t, n), bag[0:n, t, 0:1], rpow[0:n, t:t + 1],
                                             ALU.subtract, ALU.mult)
                last.then_inc(r_y, 1)
                split(u + 7)
                dve.drain()
                dve.wait_ge(r_yt, val(Count(1, (h, 1))))
                for half in range(2):
                    dve.tensor_tensor(tmp[half][:, META:T1], A[half][:, 0:SEQ], rg[half][:, META:T1], ALU.mult)
                    dve.tensor_tensor(tmp[half][:, 0:META], A[half][:, SEQ:T1], rg[half][:, 0:META],
                                      ALU.mult).then_inc(r_tmp, 1)
                dve.drain()
                for half in range(2):
                    dve.wait_ge(r_hi, val(Count(half + 1, (h, 2))))
                    dve.tensor_tensor(BL[:, bass.ds(h * 2 + half, 1), :], tmp[half][:, :].unsqueeze(1),
                                      BH[:, bass.ds(h * 2 + half, 1), :].bitcast(F32), ALU.subtract).then_inc(br_lo, 1)
                dve.drain()

            def ada_products(j):
                dve.drain()
                dve.wait_ge(ada_landed[j.slot], val(Count(16 * (j.base // 2) + 16, *((r, 8 * st) for r, st in j.terms))))
                alone(dve, dve_passed)
                for k in range(KC):
                    w, g = araw[j.slot][:, k, :], silu_c[:, k, 0:1]
                    if k == 0:
                        dve.tensor_scalar(asum[:, :], w, g, None, ALU.mult)
                    else:
                        dve.drain()
                        last = dve.scalar_tensor_tensor(out=asum[:, :], in0=w, scalar=g, in1=asum[:, :],
                                                        op0=ALU.mult, op1=ALU.add)
                last.then_inc(ada_used, 1)

            def ada_copy(j):
                dve.wait_ge(ada_mm, val(j + 1))
                dve.tensor_copy(ada[:, bass.ds(j.value(ADA_BOTH), 1), 0], A[1][:, 512:513]).then_inc(ada_out, 1)

            dve.wait_ge(cols_act, 1)

            def merge(r):
                with dve.Fori(0, KC // 2) as i:
                    for e in range(2):
                        merge_chunk(r, i * 2 + e, Count(U_BR[r] + 2 * e, (i, 4)), Count(1 + e, (i, 2)),
                                    Count(ADA_STEP[r] + e, (i, 2)))

            def merge_chunk(r, n, u, number, j):
                ada_products(j)
                split(u + 2)
                done(u + 1)
                s = (u + 1).slot
                g = two(sg[0][:, :], T1 // 2)
                mg = MG[:, bass.ds(n, 1), :]
                if r == 0:
                    dve.tensor_tensor(mg.rearrange("p a (s n) -> p (a s) n", s=2), acc(G[s], G1), g,
                                      ALU.mult).then_inc(evicted[s], 1)
                else:
                    dve.tensor_tensor(two(tmp[0][:, :], T1 // 2), acc(G[s], G1), g, ALU.mult).then_inc(evicted[s], 1)
                    dve.drain()
                    last = dve.tensor_tensor(mg, mg, tmp[0][:, :].unsqueeze(1), ALU.add)
                    if r == 2:
                        last.then_inc(mg_add, 1)
                split(u + 3)
                if r == 2:
                    dve.drain()
                    dve.wait_ge(mg_hi, val(number))
                    dve.tensor_tensor(ML[:, bass.ds(n, 1), :], mg, MH[:, bass.ds(n, 1), :].bitcast(F32),
                                      ALU.subtract).then_inc(m_lo, 1)
                ada_copy(j)

            merge(0)

            def diff_head(i, e, more):
                u = turn(i, U_DIFF + 3 * e, 6)

                def cnt(k):
                    return turn(i, k + 5 * e, 10)

                def logits(t):
                    q0, n = TILES[t]
                    w, b = q0 + n, t % 2
                    r0 = T1 - P - q0
                    w1 = min(w, 512)
                    dve.drain()
                    if t == 4:
                        dve.wait_ge(d_bias, val(turn(i, 1 + e, 2)))
                    dve.wait_ge(d_qk, val(cnt(5 - t)))
                    alone(dve, dve_passed)
                    for m in range(2):
                        dve.tensor_tensor_reduce(dL[b][m][0:n, 0:w1], A[0][0:n, 512 * m:512 * m + w1],
                                                 dR[0:n, r0:r0 + w1], 1.0, 3 * NEG * 1e7, ALU.add, ALU.max,
                                                 dmax[0:n, 0, m:m + 1])
                    if w > 512:
                        dve.drain()
                        for m in range(2):
                            dve.tensor_tensor_reduce(dL[b][m][0:n, 512:w], A[1][0:n, 512 * m:512 * m + w - 512],
                                                     dR[0:n, r0 + 512:r0 + w], 1.0, dmax[0:n, 0, m:m + 1],
                                                     ALU.add, ALU.max, dmax[0:n, 1, m:m + 1])
                    dve.drain()
                    dve.tensor_scalar(dnb[0:n, b, :], dmax[0:n, 1 if w > 512 else 0, :], -0.125, None,
                                      ALU.mult).then_inc(d_log, 1)

                def combine(t):
                    q0, n = TILES[t]
                    w, b = q0 + n, t % 2
                    dve.drain()
                    dve.wait_ge(d_exp, val(cnt(5 - t)))
                    dve.reciprocal(drc[0:n, b, :], dsum[0:n, b, :])
                    dve.drain()
                    dve.tensor_scalar(dlr[0:n, b, :], drc[0:n, b, 1:2], small[0:n, 1:2], None, ALU.mult)
                    dve.drain()
                    p0, p1 = dL[b][0][0:n, 0:w], dL[b][1][0:n, 0:w]
                    dve.tensor_scalar(p1, p1, dlr[0:n, b, 0:1], None, ALU.mult)
                    dve.drain()
                    dve.scalar_tensor_tensor(out=p0, in0=p0, scalar=drc[0:n, b, 0:1], in1=p1, op0=ALU.mult,
                                             op1=ALU.subtract).then_inc(d_att, 1)

                head = i * 2 + e
                for t in (4, 3, 2, 1, 0):
                    logits(t)
                    combine(t)
                    if more and t == 3:
                        split(u + 5)
                dve.drain()
                dve.wait_ge(d_o, val(cnt(5)))
                dve.tensor_scalar(dss2[:, :], dss[:, :], 1.0 / P, EPS, ALU.mult, ALU.add).then_inc(d_ss, 1)
                dve.wait_ge(d_pow, val(turn(i, 1 + e, 2)))
                dve.tensor_tensor(dOn[:, :, :], dO[:, :, :], dpow[:, :].unsqueeze(2).to_broadcast([P, 5, P]),
                                  ALU.mult).then_inc(d_on, 1)
                if more:
                    split(u + 6)
                dve.wait_ge(d_hi, val(turn(i, 1 + e, 2)))
                c = bass.ds(head, 1)
                dve.scalar_tensor_tensor(out=BL[:, c, META:T1], in0=A[0][:, 0:SEQ].unsqueeze(1), scalar=small[:, 0:1],
                                         in1=BH[:, c, META:T1].bitcast(F32), op0=ALU.mult, op1=ALU.subtract)
                dve.scalar_tensor_tensor(out=BL[:, c, 0:META], in0=A[1][:, 0:META].unsqueeze(1), scalar=small[:, 0:1],
                                         in1=BH[:, c, 0:META].bitcast(F32), op0=ALU.mult,
                                         op1=ALU.subtract).then_inc(br_lo, 1)
                if more:
                    split(u + 7)

            dve.drain()
            dve.memset(dO[:, :, :], 0.0)
            dve.memset(dss[:, :], 1.0)
            for k in range(3):
                split(Count(U_DIFF + 2 + k))
            with dve.Fori(0, DIFF_H // 2 - 1) as i:
                for e in range(2):
                    diff_head(i, e, True)
            for e in range(2):
                diff_head(DIFF_H // 2 - 1, e, e == 0)
            merge(1)

            with dve.Fori(0, KC // 2) as i:
                for e in range(2):
                    u = Count(U_CONV + 3 * e, (i, 6))
                    j = Count(ADA_STEP_CONV + e, (i, 2))
                    ada_products(j)
                    split(u + 2)
                    split(u + 3)
                    done(u + 2)
                    s = (u + 2).slot
                    dve.tensor_tensor(two(cu[:, :], T1 // 2), acc(G[s], G1), two(cc[:, :], T1 // 2),
                                      ALU.mult).then_inc(evicted[s], 1)
                    dve.drain()

                    def tap(k):
                        return col_a[:, bass.ds(i * 2 + (24 + KC * k + e), 1)]

                    dve.tensor_scalar(cy[:, :], cu[:, :], tap(2), None, ALU.mult)
                    for k in (1, 0):
                        dve.drain()
                        d = 2 - k
                        dve.scalar_tensor_tensor(out=cy[:, d:T1], in0=cu[:, 0:T1 - d], scalar=tap(k), in1=cy[:, d:T1],
                                                 op0=ALU.mult, op1=ALU.add)
                    dve.drain()
                    dve.tensor_tensor(cy[:, :], cy[:, :], cb[:, :], ALU.mult).then_inc(c_y, 1)
                    split(u + 4)
                    dve.drain()
                    dve.wait_ge(c_hi, val(Count(1 + e, (i, 2))))
                    c = bass.ds(i * 2 + e, 1)
                    dve.tensor_tensor(BL[:, c, :], cy[:, :].unsqueeze(1), BH[:, c, :].bitcast(F32),
                                      ALU.subtract).then_inc(br_lo, 1)
                    ada_copy(j)
            merge(2)

            for n in range(KC):
                u = Count(U_OUT + n)
                done(u)
                x = two(X[:, n, :], T1 // 2)
                dve.tensor_tensor(x, acc(G[u.slot], G1), x, ALU.add).then_inc(evicted[u.slot], 1)
                split(u + 2)
                if n >= 1:
                    add_square(ssq[:, :], sqb, T1, n == 1)
            add_square(ssq[:, :], sqb, T1, False)
            rooted()
            scaled(KC, lambda c: tmp[c % 2][:, :], lambda c: HH[:, c, :], lambda c: HL[:, c, :], weighted(8))

            def ff_up(part):
                with dve.Fori(0, 4) as i:
                    for e in range(2):
                        u = count(U_FF + e, (part, 16), (i, 2))
                        dve.drain()
                        dve.wait_ge(ff_r, val(count(1 + e, (part, 8), (i, 2))))
                        dve.scalar_tensor_tensor(out=two(sqb[1][:, :], T1 // 2), in0=acc(G[u.slot], G1), scalar=0.0,
                                                 in1=two(sqb[0][:, :], T1 // 2), op0=ALU.max,
                                                 op1=ALU.mult).then_inc(evicted[u.slot], 1)
                        split(u + 2)
                        dve.drain()
                        dve.wait_ge(ff_hi, val(count(1 + e, (part, 8), (i, 2))))
                        c = bass.ds(i * 2 + e, 1)
                        dve.tensor_tensor(BL[:, c, :], sqb[1][:, :].unsqueeze(1), BH[:, c, :].bitcast(F32),
                                          ALU.subtract).then_inc(ff_lo, 1)

            def ff_down(part, last):
                with dve.Fori(0, 4) as i:
                    for e in range(2):
                        u = count(U_FF + 8 + e, (part, 16), (i, 2))
                        done(u)
                        x = X[:, bass.ds(i * 2 + e, 1), :].rearrange("p a (s n) -> p (a s) n", s=2)
                        dve.tensor_tensor(x, acc(G[u.slot], G1), x, ALU.add).then_inc(evicted[u.slot], 1)
                        split(u + 2)
                        if last:
                            add_in_turn(ssq[:, :], sqb, T1, i, e)

            with dve.Fori(0, FF1 // D - 1) as part:
                ff_up(part)
                ff_down(part, False)
            ff_up(FF1 // D - 1)
            dve.wait_ge(ada_used, 2 + ADA_STEPS + ADA_BOTH)
            for c in range(KC):
                dve.wait_ge(ctx_done, c + 1)
                dve.tensor_copy(X2[:, c, 0:CTX], A[c % 2][:, 0:CTX]).then_inc(ctx_out, 1)
            dve.tensor_copy(ada[:, 0:ADA_BOTH, :], A[1][:, 512:512 + 2 * ADA_BOTH].rearrange("p (n e) -> p n e", e=2))
            dve.drain()
            for e in range(2):
                dve.tensor_tensor(ada[:, :, e], ada[:, :, e], col_c[:, :], ALU.add)
            dve.drain()

            def mod(j, e):
                return ada[:, KC * j:KC * j + KC, e]

            for i, (g, sc) in enumerate(((0, 1), (2, 4), (4, 7))):
                for e in range(2):
                    dve.scalar_tensor_tensor(out=gain[i][:, :, e], in0=mod(sc, e), scalar=1.0,
                                             in1=col_b[:, KC * g:KC * g + KC], op0=ALU.add, op1=ALU.mult)
            for i, (g, gt, weight) in enumerate(((1, 2, 0.5), (3, 5, 1.0), (5, 8, 0.5))):
                for e in range(2):
                    dve.scalar_tensor_tensor(out=resg[i][:, :, e], in0=mod(gt, e), scalar=weight,
                                             in1=col_b[:, KC * g:KC * g + KC], op0=ALU.mult, op1=ALU.mult)
            dve.memset(ssq[:, :], 0.0)
            ff_down(FF1 // D - 1, True)
            nsq[0] += KC
            rooted()

            def by_column(ap):
                return ap.rearrange("p (r c) -> p c r", r=GRID_H)

            for c in range(KC):
                dve.scalar_tensor_tensor(out=X2[:, c, CTX:T2].rearrange("p (c r) -> p c r", r=GRID_H),
                                         in0=by_column(X[:, c, META:T1]), scalar=col_a[:, 16 + c:17 + c],
                                         in1=by_column(rstd[:, META:T1]), op0=ALU.mult,
                                         op1=ALU.mult).then_inc(x2_out, 1)

            def sums2(n0):
                for c in range(KC):
                    add_square(ss2[:, n0:T2], tm2, T2 - n0, c == 0)
                rooted()

            def normed(n0):
                scaled(KC, lambda c: tm2[c % 2][:, n0:T2], lambda c: H2H[:, c, n0:T2], lambda c: H2L[:, c, n0:T2],
                       lambda c, b: dve.tensor_tensor(b, X2[:, c, n0:T2], rs2[:, n0:T2], ALU.mult))

            def residual(i, n0):
                for c in range(KC):
                    for e, (a, b) in enumerate(((CTX, T2), (0, CTX))):
                        if a >= n0:
                            dve.scalar_tensor_tensor(out=Y2[:, c, a:b], in0=Y2[:, c, a:b], scalar=resg[i][:, c, e:e + 1],
                                                     in1=rs2[:, a:b], op0=ALU.mult, op1=ALU.mult)
                    dve.drain()
                    x = X2[:, c, n0:T2]
                    dve.tensor_tensor(x, x, Y2[:, c, n0:T2], ALU.add).then_inc(x2_out, 1)

            sums2(0)
            normed(0)

            def swiglu(base, geo, n0, f0, final, shift):
                def up(u, n, fcount):
                    split(u + 2)
                    done(u + 1)
                    s = (u + 1).slot
                    dve.wait_ge(evicted[u.slot], val(u.turns() + 2))
                    dve.tensor_tensor(like(tm2[1][:, n0:T2], geo), acc(G[s], geo), like(tm2[0][:, n0:T2], geo),
                                      ALU.mult).then_inc(evicted[s], 1)
                    split(u + 3)
                    dve.drain()
                    dve.wait_ge(ff_hi, val(fcount + 1))
                    c = bass.ds(n, 1)
                    dve.tensor_tensor(UL2[:, c, n0:T2], tm2[1][:, n0:T2].unsqueeze(1), UH2[:, c, n0:T2].bitcast(F32),
                                      ALU.subtract).then_inc(ff_lo, 1)

                def down(u, n, last):
                    done(u)
                    m = len(geo)
                    y = Y2[:, bass.ds(n, 1), n0:T2]
                    y = y.rearrange("p a (s n) -> p (a s) n", s=m)
                    p = acc(G[u.slot], geo) if m == 2 else acc(G[u.slot], geo).unsqueeze(1)
                    dve.tensor_tensor(y, p, y, ALU.add).then_inc(evicted[u.slot], 1)
                    if not last:
                        split(u + 2)

                with dve.Fori(0, 2) as part:
                    with dve.Fori(0, 8) as n:
                        up(Count(base, (part, 24), (n, 2)), n, Count(f0, (part, 8), (n, 1)))
                        if shift:
                            b = part * 8 + n
                            t = rpbT[:, :, bass.ds(b + 1, 31)]
                            dve.scalar_tensor_tensor(out=t, in0=rpbG[:, :, :], scalar=cst("onehot8")[:, bass.ds(b, 1)],
                                                     in1=t, op0=ALU.mult, op1=ALU.add)
                    with dve.Fori(0, 4) as i:
                        for e in range(2):
                            down(Count(base + 16 + e, (part, 24), (i, 2)), i * 2 + e, False)
                with dve.Fori(0, 6) as n:
                    up(Count(base + 48, (n, 2)), n, Count(f0 + 16, (n, 1)))
                dve.memset(ss2[:, n0:T2], 0.0)
                with dve.Fori(0, 3 if final else 4) as i:
                    for e in range(2):
                        down(Count(base + 60 + e, (i, 2)), i * 2 + e, False)
                        add_in_turn(ss2[:, n0:T2], tm2, T2 - n0, i, e)
                if final:
                    for e in range(2):
                        down(Count(base + 66 + e), 6 + e, True)
                        add_in_turn(ss2[:, n0:T2], tm2, T2 - n0, 3, e)
                nsq[0] += KC

            dve.wait_ge(rpb_zero, 1)
            dve.wait_ge(rpb_in, 16 * GRID_H)
            dve.wait_ge(y_zero, 1)
            swiglu(U_FA, G2, 0, 32, False, True)
            rooted()
            residual(0, 0)
            sums2(0)
            normed(0)

            for kind, off in enumerate((16, 8, 0)):
                dve.tensor_tensor(
                    nB[:, kind, :, :].rearrange("p h (a r) -> p h a r", r=GRID_H),
                    rpbT[:, :, off:off + 32].rearrange("p (h r) a -> p h a r", r=GRID_H),
                    cst("window")[:, 32 * kind:32 * kind + 32].unsqueeze(1).unsqueeze(3).to_broadcast(
                        [P, NA_H, 32, GRID_H]), ALU.add)
            dve.drain()
            dve.memset(nst[:, :, :], 0.0).then_inc(n_tab, 1)
            dve.drain()
            for k in range(3):
                split(Count(U_NA + k + 2))

            def na_pair(i, p):
                u = turn(i, U_NA + 3 * p, 6)
                for half in range(2):
                    dve.drain()
                    dve.wait_ge(n_vt, val(turn(i, half + 1 + 2 * p, 4)))
                    if half == 0:
                        dve.tensor_copy(nV[:, 0:5, :], A[1][:, 0:640].rearrange("p (c n) -> p c n", n=P)).then_inc(
                            n_v, 1)
                    else:
                        dve.tensor_copy(nV[:, 5:9, :], A[1][:, 0:512].rearrange("p (c n) -> p c n", n=P)).then_inc(
                            n_v, 1)

                def cnt(k):
                    return turn(i, k + 8 * p, 16)

                def logits(s):
                    e, t = divmod(s, NT)
                    b = s % 2
                    kind = (0, 1, 1, 2)[t]
                    dve.drain()
                    if t == 0:
                        dve.wait_ge(n_bias, val(turn(i, 2 * p + e + 1, 4)))
                    dve.wait_ge(n_qk, val(cnt(s + 1)))
                    alone(dve, dve_passed)
                    dve.tensor_tensor_reduce(nP[b][:, 0:256], A[0][:, 512 * b:512 * b + 256],
                                             nBs[e][:, kind, :],
                                             1.0, 3 * NEG * 1e7, ALU.add, ALU.max, nst[:, b, 0:1])
                    dve.tensor_reduce(nst[:, b, 1:2], A[0][:, 512 * b + 256:512 * b + 512], AX, ALU.max)
                    dve.drain()
                    dve.tensor_tensor(nst[:, b, 2:3], nst[:, b, 0:1], nst[:, b, 1:2], ALU.max)
                    dve.drain()
                    dve.tensor_scalar(nst[:, b, 3:4], nst[:, b, 2:3], -0.125, None, ALU.mult).then_inc(n_log, 1)

                def copy_pT(s):
                    b = s % 2
                    dve.wait_ge(n_tr, val(cnt(s + 1)))
                    dve.tensor_copy(nT[b][:, :, :], A[1][:, 0:512].rearrange("p (c n) -> p c n", n=P)).then_inc(
                        n_at, 1)
                    dve.tensor_tensor(nst[:, b, 6:7], nst[:, b, 4:5], nst[:, b, 5:6], ALU.add)
                    dve.drain()
                    dve.reciprocal(nst[:, b, 7:8], nst[:, b, 6:7])
                    dve.drain()

                def out_o(s):
                    e, t = divmod(s, NT)
                    dve.wait_ge(n_pv, val(cnt(s + 1)))
                    dve.tensor_scalar(nO[:, t, bass.ds(i * 256 + (2 * p + e) * NA_HD, NA_HD)],
                                      A[1][:, 512:512 + NA_HD], nst[:, s % 2, 7:8], None, ALU.mult).then_inc(n_o, 1)

                logits(0)
                logits(1)
                for s in range(8):
                    copy_pT(s)
                    if s:
                        out_o(s - 1)
                    if s < 6:
                        logits(s + 2)
                    if s in (3, 6):
                        split(u + 4 + s // 3)
                out_o(7)
                split(u + 7)
                dve.drain()

            dve.drain().then_inc(n_o, 1)
            with dve.Fori(0, NA_H // 4 - 1) as i:
                for p in range(2):
                    na_pair(i, p)
            for p in range(2):
                na_pair(NA_H // 4 - 1, p)
            for c in range(4):
                dve.wait_ge(n_hi, c + 1)
                dve.tensor_tensor(NA_OL[:, c, :], A[c % 2][:, 0:SEQ], NA_OH[:, c, :].bitcast(F32),
                                  ALU.subtract).then_inc(n_lo, 1)

            for k in range(2):
                add_square(ss2[:, :], tm2, T2, k == 0)
            rooted()
            scaled(2, lambda c: tm2[c % 2][:, :], lambda c: CKH[:, c, :], lambda c: CKL[:, c, :],
                   lambda c, b: dve.scalar_tensor_tensor(out=b, in0=ckvT[:, c, :], scalar=col_b[:, 70 + c:71 + c],
                                                         in1=rs2[:, :], op0=ALU.mult, op1=ALU.mult))
            for k in range(6):
                split(Count(U_LORA + 5 + k))
                add_square(ss2[:, 0:SEQ], tm2, SEQ, k == 0)
            dve.wait_ge(rope_in, 16)
            R = slice(NOPE, QK)

            def rotate(x, n):
                dve.drain()
                dve.wait_ge(k_rot, val(n))
                dve.tensor_tensor(mqr[R, :], A[1][R, 0:SEQ], rope[R, 1, :], ALU.mult)
                dve.tensor_tensor(x, x, rope[R, 0, :], ALU.mult)
                dve.drain()
                return dve.tensor_tensor(x, x, mqr[R, :], ALU.add)

            rotate(mkr[R, CTX:T2], 1)
            dve.drain()
            dve.tensor_copy(mks[0][R, :], mkr[R, :])
            rooted()
            scaled(6, lambda c: tm2[c % 2][:, 0:SEQ], lambda c: CQH[:, c, :], lambda c: CQL[:, c, :],
                   lambda c, b: dve.scalar_tensor_tensor(out=b, in0=cqT[:, c, :], scalar=col_b[:, 64 + c:65 + c],
                                                         in1=rs2[:, 0:SEQ], op0=ALU.mult, op1=ALU.mult))

            dve.tensor_copy(mks[1][R, :], mkr[R, :])

            def mla_ready(i, e, parity):
                rotate(mqs[parity][R, :], turn(i, 2 + e, 2)).then_inc(k_q, 1)
                dve.wait_ge(k_vt, val(turn(i, 1 + e, 2)))
                dve.tensor_copy(mV[:, :, :], A[1][:, 512:896].rearrange("p (c n) -> p c n", n=VD)).then_inc(k_v, 1)

            def mla_head(i, e, more):
                u = turn(i, U_MLA + 2 * e, 4)
                kq, kkv = (KC, 4) if isinstance(i, int) else (6, 2)

                def cnt(t):
                    return turn(i, t + 1 + NT * e, 2 * NT)

                def row_max(t):
                    b = t % 2
                    dve.drain()
                    dve.wait_ge(k_qk, val(cnt(t)))
                    dve.tensor_reduce(mst[:, b, 0:1], A[0][:, 0:T2], AX, ALU.max)
                    dve.drain()
                    dve.tensor_scalar(mst[:, b, 1:2], mst[:, b, 0:1], -(QK ** -0.5), None, ALU.mult).then_inc(k_log, 1)

                def copy_pT(t):
                    dve.wait_ge(k_tr1, val(cnt(t)))
                    dve.tensor_copy(mT[t % 2][:, 4:6, :], A[1][:, 512:768].rearrange("p (c n) -> p c n", n=P)).then_inc(
                        k_ad, 1)
                    dve.reciprocal(mst[:, t % 2, 3:4], mst[:, t % 2, 2:3])
                    dve.drain()

                def out_o(t):
                    dve.wait_ge(k_pv, val(cnt(t)))
                    at_ = i * 128 + VD * e
                    dve.tensor_scalar(mO[:, t, bass.ds(at_, VD)], A[1][:, 768:768 + VD], mst[:, t % 2, 3:4], None,
                                      ALU.mult).then_inc(k_o, 1)

                row_max(0)
                for t in range(NT):
                    if t < NT - 1:
                        row_max(t + 1)
                    copy_pT(t)
                    if t:
                        out_o(t - 1)
                    if more and t == 2:
                        split(u + 4, kq)
                out_o(NT - 1)
                dve.drain()
                if more:
                    mla_ready(i, 1 + e, 1 - e)
                    split(u + 5, kkv)

            for k in range(2):
                split(Count(U_MLA + 2 + k), 2 if k else 6)
            mla_ready(0, 0, 0)
            with dve.Fori(0, 3) as i:
                for e in range(2):
                    mla_head(i, e, True)
            for e in range(2):
                mla_head(3, e, e == 0)
            for c in range(4):
                dve.wait_ge(k_hi, c + 1)
                dve.tensor_tensor(ML_OL[:, c, :], A[c % 2][:, 0:SEQ], ML_OH[:, c, :].bitcast(F32),
                                  ALU.subtract).then_inc(k_lo, 1)

            with dve.Fori(0, KC) as n:
                u = Count(U_GATE, (n, 4))
                for k in range(2):
                    v = u + (2 * k)
                    split(v + 2)
                    done(v + 1)
                    s = (v + 1).slot
                    dve.wait_ge(evicted[v.slot], val(v.turns() + 2))
                    dve.tensor_tensor(tm2[k][:, 0:SEQ], acc(G[s], GS), sgl[k][:, :], ALU.mult).then_inc(evicted[s], 1)
                    if k == 0:
                        split(v + 3, 4)
                dve.drain()
                dve.tensor_tensor(tm2[0][:, 0:SEQ], tm2[0][:, 0:SEQ], tm2[1][:, 0:SEQ], ALU.add).then_inc(mg_add, 1)
                split(u + 5)
                dve.drain()
                dve.wait_ge(mg_hi, val(Count(KC + 1, (n, 1))))
                c = bass.ds(n, 1)
                dve.tensor_tensor(ML2[:, c, :], tm2[0][:, 0:SEQ].unsqueeze(1), MH2[:, c, :].bitcast(F32),
                                  ALU.subtract).then_inc(m_lo, 1)
            dve.memset(ss2[:, CTX:T2], 0.0)
            with dve.Fori(0, 4) as i:
                for e in range(2):
                    split(Count(U_OUT2 + 2 + e, (i, 2)))
                    add_in_turn(ss2[:, CTX:T2], tm2, SEQ, i, e)
            nsq[0] += KC
            rooted()
            residual(1, CTX)
            sums2(CTX)
            normed(CTX)
            dve.wait_ge(y_zero, 2)
            swiglu(U_FB, GL, CTX, 54, True, False)
            rooted()
            residual(2, CTX)

            for t in range(NT):
                dve.wait_ge(o_tr, t + 1)
                if t >= 2:
                    dve.wait_ge(o_st[t % 2], val(16 * (t // 2)))
                dve.tensor_copy(orow[t % 2][:, :], A[t % 2][:, :]).then_inc(o_cp, 1)


_INS = ["x", "meta_tokens", "norm1_w", "w_in", "conv_w", "diff_lambda", "diff_subln_w", "w_branch", "w_out",
        "norm2_w", "w_up", "w_down", "final_norm_w", "c_2", "ctx_2", "c_ctx_2", "w_ada_2", "b_ada_2", "norm_g_2",
        "ffn1_w1_2", "ffn1_w3_2", "ffn1_w2_2", "w_in_2", "b_gate_2", "g_q_lora_2", "g_kv_lora_2", "w_uq_2",
        "w_ukv_2", "rpb_2", "w_o_na_2", "w_o_mla_2", "w_out_2", "ffn2_w1_2", "ffn2_w3_2", "ffn2_w2_2"]


def kernel(**inputs):
    import concourse.bacc as _bacc
    from concourse.bass_utils import run_bass_kernel_spmd as _run

    nc = _bacc.Bacc("TRN2", target_bir_lowering=False, num_devices=1)
    arrays, aps = {}, {}
    for name in _INS:
        a = np.ascontiguousarray(inputs[name])
        arrays[f"in_{name}_dram"] = a
        aps[name] = nc.dram_tensor(f"in_{name}_dram", a.shape, mybir.dt.from_np(a.dtype), kind="ExternalInput").ap()
    for name, a in shape_constants().items():
        a = np.ascontiguousarray(a)
        arrays[f"const_{name}_dram"] = a
        aps[name] = nc.dram_tensor(f"const_{name}_dram", a.shape, F32, kind="ExternalInput").ap()
    out = nc.dram_tensor("out_0_dram", (1, SEQ, D), F32, kind="ExternalOutput").ap()
    build(nc, aps, out)
    r = _run(nc, [arrays], core_ids=[0])
    return r.results[0]["out_0_dram"]
```
